# Optimizing a Trainium2 kernel written in Bass

```python
import math
import jax, jax.numpy as jnp
from jax import lax
import numpy as np

D_MODEL = 1024
BATCH = 1
SEQ = 512
DEPTH = 2

CHUNK = 64
N_MIXERS = 4
RMS_EPS = 1e-6

A_HEADS = 16
A_HEAD_DIM = D_MODEL // A_HEADS
A_WIDTH = A_HEADS * A_HEAD_DIM
A_LEFT_CHUNKS = 8
A_BAND = (A_LEFT_CHUNKS + 1) * CHUNK
A_MAX_REL = 256
A_REL_SIZE = (CHUNK - 1) + A_MAX_REL + 1

SG_FF = 6 * D_MODEL
SG_HALF = SG_FF // 2
SG_GROUPS = 8
SG_WINDOW = 128

GLA_HEADS = 4
GLA_KEY_WIDTH = D_MODEL // 2
GLA_VALUE_WIDTH = D_MODEL
GLA_DK = GLA_KEY_WIDTH // GLA_HEADS
GLA_DV = GLA_VALUE_WIDTH // GLA_HEADS
GLA_GATE_RANK = 16
GLA_TAU = 16.0
GLA_IN_WIDTH = 2 * GLA_KEY_WIDTH + 2 * GLA_VALUE_WIDTH + GLA_GATE_RANK

SB_HEADS = 16
SB_HEAD_DIM = D_MODEL // SB_HEADS
SB_WIDTH = SB_HEADS * SB_HEAD_DIM
SB_BLOCK = 128

FFN_HIDDEN = 4 * D_MODEL


def rms_norm(x, gain):
    xf = x.astype(jnp.float32)
    y = xf * lax.rsqrt(jnp.mean(xf * xf, axis=-1, keepdims=True) + RMS_EPS)
    return (y * gain.astype(jnp.float32)).astype(x.dtype)

def chunked_relpos_attention(h, w_in, q_gain, k_gain, rel_bias, w_out):
    B, S, _ = h.shape
    nc = S // CHUNK
    q, k, v = jnp.split(h @ w_in, 3, axis=-1)
    q = rms_norm(q.reshape(B, S, A_HEADS, A_HEAD_DIM), q_gain) * (A_HEAD_DIM ** -0.5)
    k = rms_norm(k.reshape(B, S, A_HEADS, A_HEAD_DIM), k_gain)
    v = v.reshape(B, S, A_HEADS, A_HEAD_DIM)
    pad = A_LEFT_CHUNKS * CHUNK
    kp = jnp.pad(k, ((0, 0), (pad, 0), (0, 0), (0, 0)))
    vp = jnp.pad(v, ((0, 0), (pad, 0), (0, 0), (0, 0)))
    rel = jnp.arange(CHUNK)[:, None] + pad - jnp.arange(A_BAND)[None, :]
    bias_idx = jnp.clip(rel, -(CHUNK - 1), A_MAX_REL) + (CHUNK - 1)
    bias = rel_bias.astype(jnp.float32)[:, bias_idx]

    def one_chunk(ci):
        start = ci * CHUNK
        qc = lax.dynamic_slice_in_dim(q, start, CHUNK, axis=1)
        kb = lax.dynamic_slice_in_dim(kp, start, A_BAND, axis=1)
        vb = lax.dynamic_slice_in_dim(vp, start, A_BAND, axis=1)
        s = jnp.einsum('bihd,bjhd->bhij', qc, kb).astype(jnp.float32) + bias
        valid = (start + jnp.arange(A_BAND)) >= pad
        s = jnp.where(valid[None, None, None, :], s, -jnp.inf)
        p = jax.nn.softmax(s, axis=-1).astype(vb.dtype)
        return jnp.einsum('bhij,bjhd->bihd', p, vb)

    o = lax.map(one_chunk, jnp.arange(nc))
    o = o.transpose(1, 0, 2, 3, 4).reshape(B, S, A_WIDTH)
    return o @ w_out

def chunked_spatial_gating(h, w_in, v_gain, w_s, b_s, w_out):
    B, S, _ = h.shape
    nw = S // SG_WINDOW
    z = jax.nn.gelu(h @ w_in, approximate=False)
    u, v = jnp.split(z, 2, axis=-1)
    v = rms_norm(v, v_gain).reshape(B, nw, SG_WINDOW, SG_GROUPS, SG_HALF // SG_GROUPS)
    chunk_id = jnp.arange(SG_WINDOW) // CHUNK
    mask = chunk_id[:, None] >= chunk_id[None, :]
    w = jnp.where(mask[None], w_s, 0.0).astype(v.dtype)
    vm = jnp.einsum('gij,bnjgc->bnigc', w, v) + b_s.T.astype(v.dtype)[None, None, :, :, None]
    return (u * vm.reshape(B, S, SG_HALF)) @ w_out

def gated_linear_attention(h, w_in, w_gate_up, b_gate, o_gain, w_out):
    B, S, _ = h.shape
    nc = S // CHUNK
    splits = [GLA_KEY_WIDTH, 2 * GLA_KEY_WIDTH, 2 * GLA_KEY_WIDTH + GLA_VALUE_WIDTH,
              2 * GLA_KEY_WIDTH + 2 * GLA_VALUE_WIDTH]
    q, k, v, r, a = jnp.split(h @ w_in, splits, axis=-1)
    log_alpha = jax.nn.log_sigmoid((a @ w_gate_up + b_gate).astype(jnp.float32)) / GLA_TAU

    def to_chunks(t, d):
        return t.reshape(B, nc, CHUNK, GLA_HEADS, d).transpose(1, 0, 3, 2, 4).astype(jnp.float32)

    qc = to_chunks(q, GLA_DK) * (GLA_DK ** -0.5)
    kc = to_chunks(k, GLA_DK)
    vc = to_chunks(v, GLA_DV)
    bc = jnp.cumsum(to_chunks(log_alpha, GLA_DK), axis=3)
    causal = jnp.tril(jnp.ones((CHUNK, CHUNK), dtype=bool))

    def step(state, inp):
        qt, kt, vt, bt = inp
        o_inter = jnp.einsum('bhtk,bhkv->bhtv', qt * jnp.exp(bt), state)
        decay = bt[:, :, :, None, :] - bt[:, :, None, :, :]
        decay = jnp.exp(jnp.where(causal[None, None, :, :, None], decay, -jnp.inf))
        att = jnp.einsum('bhtk,bhsk,bhtsk->bhts', qt, kt, decay)
        o_intra = jnp.einsum('bhts,bhsv->bhtv', att, vt)
        b_last = bt[:, :, -1:, :]
        k_dec = kt * jnp.exp(b_last - bt)
        state = state * jnp.exp(b_last[:, :, 0, :])[..., None] + jnp.einsum('bhsk,bhsv->bhkv', k_dec, vt)
        return state, o_inter + o_intra

    state0 = jnp.zeros((B, GLA_HEADS, GLA_DK, GLA_DV), jnp.float32)
    _, o = lax.scan(step, state0, (qc, kc, vc, bc))
    o = o.transpose(1, 0, 3, 2, 4).reshape(B, S, GLA_HEADS, GLA_DV).astype(h.dtype)
    o = rms_norm(o, o_gain).reshape(B, S, GLA_VALUE_WIDTH)
    return (jax.nn.silu(r) * o) @ w_out

def stick_breaking_attention(h, w_in, w_out):
    B, S, _ = h.shape
    q, k, v = jnp.split(h @ w_in, 3, axis=-1)
    q = q.reshape(B, S, SB_HEADS, SB_HEAD_DIM).transpose(0, 2, 1, 3)
    k = k.reshape(B, S, SB_HEADS, SB_HEAD_DIM).transpose(0, 2, 1, 3)
    v = v.reshape(B, S, SB_HEADS, SB_HEAD_DIM).transpose(0, 2, 1, 3)
    scale = SB_HEAD_DIM ** -0.5
    outs = []
    for blk in range(S // SB_BLOCK):
        q0 = blk * SB_BLOCK
        kend = q0 + SB_BLOCK
        z = jnp.einsum('bhtd,bhsd->bhts', q[:, :, q0:kend], k[:, :, :kend]).astype(jnp.float32) * scale
        t_pos = q0 + jnp.arange(SB_BLOCK)
        strict = jnp.arange(kend)[None, :] < t_pos[:, None]
        log_not = jnp.where(strict, jax.nn.log_sigmoid(-z), 0.0)
        tail = lax.cumsum(log_not, axis=3, reverse=True)
        excl = jnp.concatenate([tail[..., 1:], jnp.zeros_like(tail[..., :1])], axis=-1)
        weights = jnp.where(strict, jnp.exp(jax.nn.log_sigmoid(z) + excl), 0.0)
        outs.append(jnp.einsum('bhts,bhsd->bhtd', weights.astype(v.dtype), v[:, :, :kend]))
    o = jnp.concatenate(outs, axis=2).transpose(0, 2, 1, 3).reshape(B, S, SB_WIDTH)
    return o @ w_out

def squared_relu_mlp(h, w1, w2):
    return jnp.square(jax.nn.relu(h @ w1)) @ w2

def _n_mixer_layers(m):
    return len(range(m, DEPTH, N_MIXERS))

def first_inputs(seed: int = 0) -> dict:
    key = jax.random.key(seed)
    keys = iter(jax.random.split(key, 32))
    D = D_MODEL

    def nrm(shape, scale):
        return jax.random.normal(next(keys), shape, jnp.float32) * scale

    nA, nB, nC, nD = (_n_mixer_layers(m) for m in range(N_MIXERS))
    return {
        "x": nrm((BATCH, SEQ, D), 1.0),
        "c": nrm((BATCH, D), 1.0),
        "ada_w": nrm((DEPTH, D, 6 * D), 0.5 * D ** -0.5),
        "ada_b": nrm((DEPTH, 6 * D), 0.02),
        "norm_mix": 1.0 + nrm((DEPTH, D), 0.05),
        "norm_ffn": 1.0 + nrm((DEPTH, D), 0.05),
        "ffn_w1": nrm((DEPTH, D, FFN_HIDDEN), D ** -0.5),
        "ffn_w2": nrm((DEPTH, FFN_HIDDEN, D), FFN_HIDDEN ** -0.5),
        "a_w_in": nrm((nA, D, 3 * A_WIDTH), D ** -0.5),
        "a_q_gain": 1.0 + nrm((nA, A_HEAD_DIM), 0.05),
        "a_k_gain": 1.0 + nrm((nA, A_HEAD_DIM), 0.05),
        "a_rel_bias": nrm((nA, A_HEADS, A_REL_SIZE), 0.5),
        "a_w_out": nrm((nA, A_WIDTH, D), A_WIDTH ** -0.5),
        "b_w_in": nrm((nB, D, SG_FF), D ** -0.5),
        "b_v_gain": 1.0 + nrm((nB, SG_HALF), 0.05),
        "b_w_s": nrm((nB, SG_GROUPS, SG_WINDOW, SG_WINDOW), SG_WINDOW ** -0.5),
        "b_b_s": 1.0 + nrm((nB, SG_GROUPS, SG_WINDOW), 0.05),
        "b_w_out": nrm((nB, SG_HALF, D), SG_HALF ** -0.5),
        "c_w_in": nrm((nC, D, GLA_IN_WIDTH), D ** -0.5),
        "c_w_gate_up": nrm((nC, GLA_GATE_RANK, GLA_KEY_WIDTH), GLA_GATE_RANK ** -0.5),
        "c_b_gate": nrm((nC, GLA_KEY_WIDTH), 0.02),
        "c_o_gain": 1.0 + nrm((nC, GLA_DV), 0.05),
        "c_w_out": nrm((nC, GLA_VALUE_WIDTH, D), GLA_VALUE_WIDTH ** -0.5),
        "d_w_in": nrm((nD, D, 3 * SB_WIDTH), D ** -0.5),
        "d_w_out": nrm((nD, SB_WIDTH, D), SB_WIDTH ** -0.5),
    }

def first_block(x, c, ada_w, ada_b, norm_mix, norm_ffn, ffn_w1, ffn_w2,
              a_w_in, a_q_gain, a_k_gain, a_rel_bias, a_w_out,
              b_w_in, b_v_gain, b_w_s, b_b_s, b_w_out,
              c_w_in, c_w_gate_up, c_b_gate, c_o_gain, c_w_out,
              d_w_in, d_w_out):
    cond = jax.nn.silu(c)
    for i in range(DEPTH):
        m, j = i % N_MIXERS, i // N_MIXERS
        mod = cond @ ada_w[i] + ada_b[i]
        sh1, sc1, g1, sh2, sc2, g2 = [t[:, None, :] for t in jnp.split(mod, 6, axis=-1)]
        h = rms_norm(x, norm_mix[i]) * (1.0 + sc1) + sh1
        if m == 0:
            y = chunked_relpos_attention(h, a_w_in[j], a_q_gain[j], a_k_gain[j], a_rel_bias[j], a_w_out[j])
        elif m == 1:
            y = chunked_spatial_gating(h, b_w_in[j], b_v_gain[j], b_w_s[j], b_b_s[j], b_w_out[j])
        elif m == 2:
            y = gated_linear_attention(h, c_w_in[j], c_w_gate_up[j], c_b_gate[j], c_o_gain[j], c_w_out[j])
        else:
            y = stick_breaking_attention(h, d_w_in[j], d_w_out[j])
        x = x + g1 * y
        h = rms_norm(x, norm_ffn[i]) * (1.0 + sc2) + sh2
        x = x + g2 * squared_relu_mlp(h, ffn_w1[i], ffn_w2[i])
    return x


DEPTH_2 = 1

ATTN_WIDTH = 512
N_HEADS = 8
HEAD_DIM = 64
N_KV_GROUPS = 2
HEADS_PER_GROUP = N_HEADS // N_KV_GROUPS
KV_WIDTH = N_KV_GROUPS * HEAD_DIM
CMP_LEN = 32
CMP_STRIDE = 16
CMP_HIDDEN = 256
SEL_BLOCK = 64
SEL_TOPN = 16
WINDOW = 512
Q_BLOCK = 64
N_BRANCH = 3
ROPE_THETA = 10000.0
SSM_WIDTH = D_MODEL - ATTN_WIDTH
SSM_GROUP = 16
SSM_GROUPS = SSM_WIDTH // SSM_GROUP
SSM_STATE = 64
SSM_CHUNK = 128
DT_MIN = 1e-3
DT_MAX = 1e-1
EPS = 1e-6
IN_WIDTH = ATTN_WIDTH + 6 * KV_WIDTH + ATTN_WIDTH + N_BRANCH * N_HEADS + 2 * SSM_WIDTH


def rms_norm_2(x, g):
    xf = x.astype(jnp.float32)
    y = xf * lax.rsqrt(jnp.mean(xf * xf, axis=-1, keepdims=True) + EPS)
    return (y * g.astype(jnp.float32)).astype(x.dtype)

def rope_tables(T, dtype):
    inv = 1.0 / (ROPE_THETA ** (jnp.arange(0, HEAD_DIM, 2, dtype=jnp.float32) / HEAD_DIM))
    ang = jnp.arange(T, dtype=jnp.float32)[:, None] * inv[None, :]
    return jnp.cos(ang).astype(dtype), jnp.sin(ang).astype(dtype)

def apply_rope(x, cos, sin):
    x1, x2 = jnp.split(x, 2, axis=-1)
    c = cos[None, :, None, :]
    s = sin[None, :, None, :]
    return jnp.concatenate([x1 * c - x2 * s, x2 * c + x1 * s], axis=-1)

def masked_softmax(s, mask):
    s = jnp.where(mask, s.astype(jnp.float32), -jnp.inf)
    m = jnp.max(s, axis=-1, keepdims=True)
    m = jnp.where(jnp.isfinite(m), m, 0.0)
    e = jnp.where(mask, jnp.exp(s - m), 0.0)
    return e / jnp.maximum(jnp.sum(e, axis=-1, keepdims=True), 1e-30)

def compress(kv_raw, pos, w1, w2):
    B, T = kv_raw.shape[0], kv_raw.shape[1]
    nc = (T - CMP_LEN) // CMP_STRIDE + 1
    idx = jnp.arange(nc)[:, None] * CMP_STRIDE + jnp.arange(CMP_LEN)[None, :]
    blocks = kv_raw[:, idx] + pos[None, None, :, None, :]
    blocks = blocks.transpose(0, 1, 3, 2, 4).reshape(B, nc, N_KV_GROUPS, CMP_LEN * HEAD_DIM)
    return jax.nn.gelu(blocks @ w1) @ w2

def block_importance(p_cmp, nsb):
    r = SEL_BLOCK // CMP_STRIDE
    ov = CMP_LEN // CMP_STRIDE
    nc = p_cmp.shape[-1]
    left = ov - 1
    right = r * nsb + r - nc
    pp = jnp.pad(p_cmp, [(0, 0)] * (p_cmp.ndim - 1) + [(left, right)])
    terms = []
    for m in range(r):
        for n in range(ov):
            start = m - n + left
            terms.append(pp[..., start:start + r * (nsb - 1) + 1:r])
    return sum(terms[1:], terms[0])

def nsa_attention(q, kc, vc, k_slc, v_slc, k_win, v_win, gates):
    B, T = q.shape[0], q.shape[1]
    cos, sin = rope_tables(T, q.dtype)
    q_r = apply_rope(q, cos, sin)
    k_slc = apply_rope(k_slc, cos, sin)
    k_win = apply_rope(k_win, cos, sin)
    q_g = q.reshape(B, T, N_KV_GROUPS, HEADS_PER_GROUP, HEAD_DIM)
    q_rg = q_r.reshape(B, T, N_KV_GROUPS, HEADS_PER_GROUP, HEAD_DIM)
    gates = gates.reshape(B, T, N_KV_GROUPS, HEADS_PER_GROUP, N_BRANCH)
    nsb = T // SEL_BLOCK
    n_sel = min(SEL_TOPN, nsb)
    nc = kc.shape[1]
    k_blocks = k_slc.reshape(B, nsb, SEL_BLOCK, N_KV_GROUPS, HEAD_DIM).transpose(0, 3, 1, 2, 4)
    v_blocks = v_slc.reshape(B, nsb, SEL_BLOCK, N_KV_GROUPS, HEAD_DIM).transpose(0, 3, 1, 2, 4)
    k_win_p = jnp.pad(k_win, ((0, 0), (WINDOW, 0), (0, 0), (0, 0)))
    v_win_p = jnp.pad(v_win, ((0, 0), (WINDOW, 0), (0, 0), (0, 0)))
    cmp_end = jnp.arange(nc) * CMP_STRIDE + CMP_LEN - 1
    blk = jnp.arange(nsb)
    scale = HEAD_DIM ** -0.5
    gather = jax.vmap(jax.vmap(lambda kb, ix: kb[ix]))
    n_keys = n_sel * SEL_BLOCK

    def block_fn(qb):
        t0 = qb * Q_BLOCK
        t = t0 + jnp.arange(Q_BLOCK)
        qc = lax.dynamic_slice_in_dim(q_g, t0, Q_BLOCK, 1)
        qr = lax.dynamic_slice_in_dim(q_rg, t0, Q_BLOCK, 1)
        g = lax.dynamic_slice_in_dim(gates, t0, Q_BLOCK, 1)
        s = jnp.einsum('bqghd,bngd->bghqn', qc, kc) * scale
        p = masked_softmax(s, cmp_end[None, :] <= t[:, None])
        o_cmp = jnp.einsum('bghqn,bngd->bqghd', p.astype(vc.dtype), vc)
        imp = block_importance(jnp.sum(p, axis=2), nsb)
        cur = t // SEL_BLOCK
        forced = (blk[None, :] == 0) | (blk[None, :] == cur[:, None]) | (blk[None, :] == cur[:, None] - 1)
        valid = blk[None, :] * SEL_BLOCK <= t[:, None]
        imp = jnp.where(forced, jnp.inf, jnp.where(valid, imp, -jnp.inf))
        _, idx = lax.top_k(imp, n_sel)
        ks = gather(k_blocks, idx).reshape(B, N_KV_GROUPS, Q_BLOCK, n_keys, HEAD_DIM)
        vs = gather(v_blocks, idx).reshape(B, N_KV_GROUPS, Q_BLOCK, n_keys, HEAD_DIM)
        kpos = (idx[..., None] * SEL_BLOCK + jnp.arange(SEL_BLOCK)).reshape(B, N_KV_GROUPS, Q_BLOCK, n_keys)
        s = jnp.einsum('bqghd,bgqkd->bghqk', qr, ks) * scale
        p = masked_softmax(s, (kpos <= t[:, None])[:, :, None])
        o_slc = jnp.einsum('bghqk,bgqkd->bqghd', p.astype(vs.dtype), vs)
        kw = lax.dynamic_slice_in_dim(k_win_p, t0, WINDOW + Q_BLOCK, 1)
        vw = lax.dynamic_slice_in_dim(v_win_p, t0, WINDOW + Q_BLOCK, 1)
        wpos = t0 - WINDOW + jnp.arange(WINDOW + Q_BLOCK)
        dist = t[:, None] - wpos[None, :]
        wmask = (dist >= 0) & (dist < WINDOW) & (wpos[None, :] >= 0)
        s = jnp.einsum('bqghd,bkgd->bghqk', qr, kw) * scale
        p = masked_softmax(s, wmask)
        o_win = jnp.einsum('bghqk,bkgd->bqghd', p.astype(vw.dtype), vw)
        return g[..., 0:1] * o_cmp + g[..., 1:2] * o_slc + g[..., 2:3] * o_win

    out = lax.map(block_fn, jnp.arange(T // Q_BLOCK))
    return out.transpose(1, 0, 2, 3, 4, 5).reshape(B, T, ATTN_WIDTH)

def s5_mixer(u, a_re, a_im, log_dt, b_re, b_im, c_re, c_im, d_skip):
    B, T = u.shape[0], u.shape[1]
    f32 = jnp.float32
    uf = u.astype(f32)
    lam = lax.complex(a_re.astype(f32), a_im.astype(f32))
    dt = jnp.exp(log_dt.astype(f32))[:, None]
    lam_bar = jnp.exp(lam * dt)
    b_bar = ((lam_bar - 1.0) / lam)[..., None] * lax.complex(b_re.astype(f32), b_im.astype(f32))
    c_mat = lax.complex(c_re.astype(f32), c_im.astype(f32))
    nch = T // SSM_CHUNK
    uc = uf.reshape(B, nch, SSM_CHUNK, SSM_GROUPS, SSM_GROUP).transpose(1, 0, 2, 3, 4)

    def binop(e1, e2):
        a1, b1 = e1
        a2, b2 = e2
        return a1 * a2, a2 * b1 + b2

    def step(carry, u_chunk):
        bu = jnp.einsum('btgc,gpc->btgp', u_chunk.astype(jnp.complex64), b_bar)
        a = jnp.broadcast_to(lam_bar, bu.shape)
        a_cum, b_cum = lax.associative_scan(binop, (a, bu), axis=1)
        s = a_cum * carry[:, None] + b_cum
        y = jnp.real(jnp.einsum('gcp,btgp->btgc', c_mat, s))
        return s[:, -1], y

    carry0 = jnp.zeros((B, SSM_GROUPS, SSM_STATE), jnp.complex64)
    _, y = lax.scan(step, carry0, uc)
    y = y.transpose(1, 0, 2, 3, 4).reshape(B, T, SSM_WIDTH)
    return y + d_skip.astype(f32) * uf

def hybrid_layer(x, c, w_ada, b_ada, norm_g, w_in, q_norm_g, k_cmp_norm_g, k_slc_norm_g, k_win_norm_g,
                 cmp_pos_k, cmp_pos_v, cmp_w1_k, cmp_w2_k, cmp_w1_v, cmp_w2_v,
                 ssm_a_re, ssm_a_im, ssm_log_dt, ssm_b_re, ssm_b_im, ssm_c_re, ssm_c_im, ssm_d,
                 glu_w, glu_b, w_out):
    B, T = x.shape[0], x.shape[1]
    mod = jax.nn.silu(c) @ w_ada + b_ada
    shift, scale, gate = jnp.split(mod, 3, axis=-1)
    h = rms_norm_2(x, norm_g) * (1 + scale[:, None, :]) + shift[:, None, :]
    proj = h @ w_in
    widths = [ATTN_WIDTH] + [KV_WIDTH] * 6 + [ATTN_WIDTH, N_BRANCH * N_HEADS, SSM_WIDTH, SSM_WIDTH]
    offs = [int(v) for v in np.cumsum(widths)[:-1]]
    q, kcr, vcr, ksl, vsl, kwn, vwn, z_a, g_br, u, z_s = jnp.split(proj, offs, axis=-1)

    def kv_heads(t):
        return t.reshape(B, T, N_KV_GROUPS, HEAD_DIM)

    q = rms_norm_2(q.reshape(B, T, N_HEADS, HEAD_DIM), q_norm_g)
    kc = rms_norm_2(compress(kv_heads(kcr), cmp_pos_k, cmp_w1_k, cmp_w2_k), k_cmp_norm_g)
    vc = compress(kv_heads(vcr), cmp_pos_v, cmp_w1_v, cmp_w2_v)
    k_slc = rms_norm_2(kv_heads(ksl), k_slc_norm_g)
    k_win = rms_norm_2(kv_heads(kwn), k_win_norm_g)
    gates = jax.nn.sigmoid(g_br).reshape(B, T, N_HEADS, N_BRANCH)
    attn = nsa_attention(q, kc, vc, k_slc, kv_heads(vsl), k_win, kv_heads(vwn), gates)
    attn = attn * jax.nn.silu(z_a)

    y = s5_mixer(u, ssm_a_re, ssm_a_im, ssm_log_dt, ssm_b_re, ssm_b_im, ssm_c_re, ssm_c_im, ssm_d)
    y = jax.nn.gelu(y)
    y = y * jax.nn.sigmoid(y @ glu_w.astype(jnp.float32) + glu_b.astype(jnp.float32))
    ssm = y.astype(x.dtype) * jax.nn.silu(z_s)

    mix = jnp.concatenate([attn, ssm], axis=-1) @ w_out
    return x + gate[:, None, :] * mix

def second_inputs(seed: int = 0) -> dict:
    key = jax.random.key(seed)
    ks = jax.random.split(key, 32)
    f32 = jnp.float32

    def nrm(k, shape, s):
        return jax.random.normal(k, shape, f32) * s

    D = D_MODEL
    L = DEPTH_2
    ng, p, cg = SSM_GROUPS, SSM_STATE, SSM_GROUP
    return {
        "x": nrm(ks[0], (BATCH, SEQ, D), 1.0),
        "c": nrm(ks[1], (BATCH, D), 1.0),
        "w_ada": nrm(ks[2], (L, D, 3 * D), 0.5 * D ** -0.5),
        "b_ada": nrm(ks[3], (L, 3 * D), 0.01),
        "norm_g": 1.0 + nrm(ks[4], (L, D), 0.02),
        "w_in": nrm(ks[5], (L, D, IN_WIDTH), D ** -0.5),
        "q_norm_g": 1.0 + nrm(ks[6], (L, HEAD_DIM), 0.02),
        "k_cmp_norm_g": 1.0 + nrm(ks[7], (L, HEAD_DIM), 0.02),
        "k_slc_norm_g": 1.0 + nrm(ks[8], (L, HEAD_DIM), 0.02),
        "k_win_norm_g": 1.0 + nrm(ks[9], (L, HEAD_DIM), 0.02),
        "cmp_pos_k": nrm(ks[10], (L, CMP_LEN, HEAD_DIM), 0.1),
        "cmp_pos_v": nrm(ks[11], (L, CMP_LEN, HEAD_DIM), 0.1),
        "cmp_w1_k": nrm(ks[12], (L, CMP_LEN * HEAD_DIM, CMP_HIDDEN), (CMP_LEN * HEAD_DIM) ** -0.5),
        "cmp_w2_k": nrm(ks[13], (L, CMP_HIDDEN, HEAD_DIM), CMP_HIDDEN ** -0.5),
        "cmp_w1_v": nrm(ks[14], (L, CMP_LEN * HEAD_DIM, CMP_HIDDEN), (CMP_LEN * HEAD_DIM) ** -0.5),
        "cmp_w2_v": nrm(ks[15], (L, CMP_HIDDEN, HEAD_DIM), CMP_HIDDEN ** -0.5),
        "ssm_a_re": -0.5 + nrm(ks[16], (L, ng, p), 0.01),
        "ssm_a_im": math.pi * jnp.arange(p, dtype=f32)[None, None, :] + nrm(ks[17], (L, ng, p), 0.01),
        "ssm_log_dt": jax.random.uniform(ks[18], (L, ng), f32, math.log(DT_MIN), math.log(DT_MAX)),
        "ssm_b_re": nrm(ks[19], (L, ng, p, cg), (2 * cg) ** -0.5),
        "ssm_b_im": nrm(ks[20], (L, ng, p, cg), (2 * cg) ** -0.5),
        "ssm_c_re": nrm(ks[21], (L, ng, cg, p), p ** -0.5),
        "ssm_c_im": nrm(ks[22], (L, ng, cg, p), p ** -0.5),
        "ssm_d": nrm(ks[23], (L, SSM_WIDTH), 1.0),
        "glu_w": nrm(ks[24], (L, SSM_WIDTH, SSM_WIDTH), SSM_WIDTH ** -0.5),
        "glu_b": nrm(ks[25], (L, SSM_WIDTH), 0.01),
        "w_out": nrm(ks[26], (L, D, D), D ** -0.5),
    }

def second_block(x, c, w_ada, b_ada, norm_g, w_in, q_norm_g, k_cmp_norm_g, k_slc_norm_g, k_win_norm_g,
              cmp_pos_k, cmp_pos_v, cmp_w1_k, cmp_w2_k, cmp_w1_v, cmp_w2_v,
              ssm_a_re, ssm_a_im, ssm_log_dt, ssm_b_re, ssm_b_im, ssm_c_re, ssm_c_im, ssm_d,
              glu_w, glu_b, w_out):
    for l in range(DEPTH_2):
        x = hybrid_layer(x, c, w_ada[l], b_ada[l], norm_g[l], w_in[l], q_norm_g[l], k_cmp_norm_g[l],
                         k_slc_norm_g[l], k_win_norm_g[l], cmp_pos_k[l], cmp_pos_v[l], cmp_w1_k[l],
                         cmp_w2_k[l], cmp_w1_v[l], cmp_w2_v[l], ssm_a_re[l], ssm_a_im[l], ssm_log_dt[l],
                         ssm_b_re[l], ssm_b_im[l], ssm_c_re[l], ssm_c_im[l], ssm_d[l], glu_w[l], glu_b[l],
                         w_out[l])
    return x


def setup_inputs(seed=0):
    out = dict(first_inputs(seed))
    for name, value in second_inputs(seed + 1).items():
        if name != "x":
            out[name + "_2"] = value
    return out


def reference(
    x, c, ada_w, ada_b, norm_mix, norm_ffn, ffn_w1, ffn_w2, a_w_in, a_q_gain, a_k_gain,
    a_rel_bias, a_w_out, b_w_in, b_v_gain, b_w_s, b_b_s, b_w_out, c_w_in, c_w_gate_up, c_b_gate,
    c_o_gain, c_w_out, d_w_in, d_w_out, c_2, w_ada_2, b_ada_2, norm_g_2, w_in_2, q_norm_g_2,
    k_cmp_norm_g_2, k_slc_norm_g_2, k_win_norm_g_2, cmp_pos_k_2, cmp_pos_v_2, cmp_w1_k_2,
    cmp_w2_k_2, cmp_w1_v_2, cmp_w2_v_2, ssm_a_re_2, ssm_a_im_2, ssm_log_dt_2, ssm_b_re_2,
    ssm_b_im_2, ssm_c_re_2, ssm_c_im_2, ssm_d_2, glu_w_2, glu_b_2, w_out_2,
):
    x = first_block(
        x, c, ada_w, ada_b, norm_mix, norm_ffn, ffn_w1, ffn_w2, a_w_in, a_q_gain, a_k_gain,
        a_rel_bias, a_w_out, b_w_in, b_v_gain, b_w_s, b_b_s, b_w_out, c_w_in, c_w_gate_up,
        c_b_gate, c_o_gain, c_w_out, d_w_in, d_w_out,
    )
    return second_block(
        x, c_2, w_ada_2, b_ada_2, norm_g_2, w_in_2, q_norm_g_2, k_cmp_norm_g_2, k_slc_norm_g_2,
        k_win_norm_g_2, cmp_pos_k_2, cmp_pos_v_2, cmp_w1_k_2, cmp_w2_k_2, cmp_w1_v_2,
        cmp_w2_v_2, ssm_a_re_2, ssm_a_im_2, ssm_log_dt_2, ssm_b_re_2, ssm_b_im_2, ssm_c_re_2,
        ssm_c_im_2, ssm_d_2, glu_w_2, glu_b_2, w_out_2,
    )


_drawn_inputs = setup_inputs


def setup_inputs(seed=0):
    import zlib

    import numpy as np

    out = dict(_drawn_inputs(seed))
    spreads = {}
    factors = {'norm_mix': 3.529,
     'a_q_gain': 8.0,
     'a_k_gain': 8.0,
     'a_rel_bias': 3.118,
     'b_v_gain': 6.637,
     'b_b_s': 5.618,
     'b_ada_2': 8.0,
     'norm_g_2': 8.0,
     'q_norm_g_2': 8.0,
     'k_cmp_norm_g_2': 21.679,
     'k_slc_norm_g_2': 8.0,
     'k_win_norm_g_2': 8.0,
     'cmp_pos_k_2': 8.0,
     'cmp_pos_v_2': 8.0,
     'cmp_w1_k_2': 6.278,
     'cmp_w2_k_2': 6.613,
     'ssm_a_re_2': 64.0,
     'ssm_a_im_2': 64.0,
     'ssm_log_dt_2': 64.0,
     'ssm_b_re_2': 64.0,
     'ssm_b_im_2': 64.0,
     'ssm_c_re_2': 64.0,
     'ssm_c_im_2': 64.0,
     'glu_w_2': 3.521,
     'glu_b_2': 200.0}
    for name, (base, spread) in spreads.items():
        noise = np.random.default_rng([zlib.crc32(name.encode()), seed]).standard_normal(out[name].shape)
        drawn = base * np.exp(spread * noise) if base else spread * noise
        out[name] = __import__('jax').numpy.asarray(drawn.astype(out[name].dtype))
    for name, factor in factors.items():
        out[name] = (out[name] * factor).astype(out[name].dtype)
    return out
```

```python
import concourse.bass as bass
from concourse import mybir
from concourse.alu_op_type import AluOpType as ALU
from contextlib import ExitStack
import math

F32 = mybir.dt.float32
F32R = mybir.dt.float32r
ACT = mybir.ActivationFunctionType
AX = mybir.AxisListType

P = 128
T = 512
D = 1024
KT = D // P
TT = T // P
SLAB = 2048
BIG = 1e30
EPS = 1e-6

N_QKV = 12
N_AOUT = 4
N_FFN = 32
N_BV = 12
N_BUO = 24
QUARTERS = 4
CHUNKS = 3
S_QKV = 0
S_AOUT = S_QKV + N_QKV
S_FFN0 = S_AOUT + N_AOUT
S_BV = S_FFN0 + N_FFN
S_BUO = S_BV + N_BV
S_FFN1 = S_BUO + N_BUO
S_HQ = S_FFN1 + N_FFN
S_HKV = S_HQ + 2
S_HCR = S_HKV + 2
S_HZA = S_HCR + 1
S_HZS = S_HZA + 2
S_HU = S_HZS + 2
S_HCK = S_HU + 2
S_HCV = S_HCK + 2
S_HGLU = S_HCV + 2
S_HOUT = S_HGLU + 1
N_SLABS = S_HOUT + 4
ADA_TILES = 48
ADA2_TILES = 24
N_ADA = 2 * ADA_TILES + ADA2_TILES

A_HEADS, HD = 16, 64
SG_HALF, SG_GROUPS = 3072, 8
H_HEADS, H_GROUPS, N_BR = 8, 2, 3
CMP_N, CMP_PAD = 31, 32
G_ALL, CH, ST, L = 32, 16, 64, 8
NCH = T // L
GB = 8
NBLK = G_ALL // GB
TAPS = L + 1
ZPAD = (L - 1) * CH


def program(nc, I, out):
    ctx = ExitStack()
    with ctx:
        sems = {}

        def sem(name):
            if name not in sems:
                sems[name] = ctx.enter_context(nc.semaphore(name))
            return sems[name]

        def sb(name, shape, dt=F32):
            return ctx.enter_context(nc.sbuf_tensor(name, shape, dt))

        ARENA = nc.sbuf_base + 31 & ~31
        placed = [0]

        def at(name, offset, shape, dt=F32):
            size = 4 * math.prod(shape[1:])
            assert ARENA + offset + size <= nc.sbuf_usable_end, (name, offset, size)
            return nc.alloc_sbuf_tensor_at(name, shape, dt, offset=ARENA + offset)

        def seq(name, shape, dt=F32):
            o = placed[0]
            placed[0] += 4 * math.prod(shape[1:]) + 31 & ~31
            return at(name, o, shape, dt)

        K = 1024
        placed[0] = 109 * K
        xT = seq("xT", [P, KT, T])
        h_hi = seq("h_hi", [P, KT, T], F32R)
        h_lo = seq("h_lo", [P, KT, T], F32R)
        w_raw = seq("w_raw", [P, 2, SLAB])
        w_hi = seq("w_hi", [P, SLAB], F32R), seq("w_hi1", [P, SLAB], F32R)
        w_lo = seq("w_lo", [P, SLAB], F32R), seq("w_lo1", [P, SLAB], F32R)
        mod = seq("mod", [P, N_ADA])
        mod_b = seq("mod_b", [P, N_ADA])
        mod_s = seq("mod_s", [P, 16])
        norm_g = seq("norm_g", [P, 5, KT])
        mod_a = seq("mod_a", [P, KT])
        ident = seq("ident", [P, P])
        ones = seq("ones", [P, P])
        eps = seq("eps", [P, 1])
        rstd = seq("rstd", [P, 32])
        stat = seq("stat", [P, 32])
        aqk_g = seq("aqk_g", [P, 2])
        bv_g = seq("bv_g", [P, SG_HALF // P])
        neg_max = seq("neg_max", [P, 4])
        row_sum = seq("row_sum", [P, 4])
        row_inv = seq("row_inv", [P, 4])
        vss = seq("vss", [P, TT, 6])
        ada_raw = at("ada_raw", 93 * K, [P, 2, D])
        cond = at("cond", 101 * K, [P, 2, D])
        sq_x = at("sq_x", 0, [P, KT, T])
        diag = at("diag", 16 * K, [P, TT, P])
        pre = at("pre", 18 * K, [P, KT, T])
        hid_hi = at("hid_hi", 0, [P, KT, T], F32R)
        hid_lo = at("hid_lo", 16 * K, [P, KT, T], F32R)
        relu = at("relu", 34 * K, [P, 2, T])
        relu2 = at("relu2", 38 * K, [P, 2, T])
        a_qT = at("a_qT", 0, [P, A_HEADS // 2, T])
        a_kT = at("a_kT", 16 * K, [P, A_HEADS // 2, T])
        a_v = at("a_v", 32 * K, [P, TT, D])
        a_qn = at("a_qn", 48 * K, [P, 2, TT, 512])
        a_sq = at("a_sq", 64 * K, [P, TT, 512])
        a_o = at("a_o", 72 * K, [P, TT, D])
        a_bias = at("a_bias", 48 * K, [P, 3, T])
        a_s = at("a_s", 54 * K, [P, 2, T])
        a_p = at("a_p", 58 * K, [P, 3, T])
        a_pt = at("a_pt", 64 * K, [P, 3, T])
        b_v = at("b_v", 0, [P, TT, SG_HALF])
        g_hi = at("g_hi", 48 * K, [P, KT, T], F32R)
        g_lo = at("g_lo", 64 * K, [P, KT, T], F32R)
        b_ws = at("b_ws", 80 * K, [P, SG_GROUPS, P])
        b_bs = at("b_bs", 84 * K, [P, SG_GROUPS, P])
        b_u = at("b_u", 88 * K, [P, T])
        b_vm = at("b_vm", 90 * K, [P, T])
        za = at("za", 0, [P, 4, T])
        zs = at("zs", 8 * K, [P, 4, T])
        uT = at("uT", 16 * K, [P, 4, T])
        hq = at("hq", 24 * K, [P, 4, T])
        hqr = at("hqr", 32 * K, [P, 4, T])
        hk = at("hk", 40 * K, [P, 2, T])
        hv = at("hv", 44 * K, [P, TT, 256])
        h_p = at("h_p", 48 * K, [P, 3, T])
        h_pt = at("h_pt", 54 * K, [P, 3, T])
        h_s = at("h_s", 60 * K, [P, 2, T])
        h_o = at("h_o", 64 * K, [P, TT, 512])
        h_qn = at("h_qn", 48 * K, [P, TT, 512])
        h_sq = at("h_sq", 56 * K, [P, TT, 512])
        h_qr = at("h_qr", 56 * K, [P, TT, 512])
        h_kn = at("h_kn", 64 * K, [P, TT, 256])
        h_kr = at("h_kr", 68 * K, [P, TT, 256])
        h_t1 = at("h_t1", 72 * K, [P, TT, 8, 32])
        h_t2 = at("h_t2", 76 * K, [P, TT, 8, 32])
        crT = at("crT", 72 * K, [P, 2, T])
        bl_hi = at("bl_hi", 76 * K, [P, 16, 2 * CMP_PAD], F32R)
        bl_lo = at("bl_lo", 80 * K, [P, 16, 2 * CMP_PAD], F32R)
        bl = at("bl", 84 * K, [P, 16, 2 * CMP_PAD])
        h_mask = at("h_mask", 88 * K, [P, T])
        placed[0] = 93 * K
        h_cmask = seq("h_cmask", [P, TT, CMP_PAD])
        h_gts = seq("h_gts", [P, TT, N_BR * H_HEADS])
        h_flag = seq("h_flag", [P, TT])
        kcT = seq("kcT", [P, CMP_PAD])
        vc = seq("vc", [CMP_PAD, H_GROUPS, HD])
        wbr = seq("wbr", [P, 4])
        cos = seq("cos", [P, TT, 32])
        sin = seq("sin", [P, TT, 32])
        qg_b = seq("qg_b", [P, HD])
        kg_b = seq("kg_b", [P, 4, HD])
        wg = seq("wg", [P, KT, 24])
        wg_hi = seq("wg_hi", [P, KT, 24], F32R)
        wg_lo = seq("wg_lo", [P, KT, 24], F32R)
        posT = seq("posT", [P, 2, 32])
        w2c = seq("w2c", [P, 2, 2, HD])
        hdn = seq("hdn", [P, 2, 2, 2 * CMP_PAD])
        kcn = seq("kcn", [CMP_PAD, H_GROUPS, HD])
        kcsq = seq("kcsq", [CMP_PAD, H_GROUPS, HD])
        kcg_b = seq("kcg_b", [CMP_PAD, HD])
        kst = seq("kst", [CMP_PAD, 4])
        PAR = ["ar", "ai", "dt", "xr", "th", "kk", "r1", "sn", "cs", "h2", "nr", "d2", "fr", "fs",
               "t1", "t2", "t3", "r8", "er", "ei"]
        par = {x: seq("s5_" + x, [P, G_ALL]) for x in PAR}
        Lr = seq("Lr", [P, TAPS, G_ALL])
        Ls = seq("Ls", [P, TAPS, G_ALL])
        LrR = at("LrR", 89 * K, [P, L, G_ALL])
        LsR = at("LsR", 92 * K, [P, L, G_ALL])
        glu_b = seq("glu_b", [P, 4])
        sgn = seq("sgn", [P, 2])
        assert placed[0] <= 109 * K, placed
        U = at("U", 24 * K, [NCH, G_ALL, L * CH])
        UT = at("UT", 40 * K, [P, G_ALL, NCH])
        Y = at("Y", 48 * K, [P, G_ALL, NCH])
        placed[0] = 24 * K
        t_a = seq("t_a", [P, GB, TAPS * CH])
        t_b = seq("t_b", [P, GB, TAPS * CH])
        Gb = seq("Gb", [P, GB, L * CH])
        wst = seq("wst", [P, GB, NCH])
        bbo = seq("bbo", [P, GB, CH])
        bbx = seq("bbx", [P, GB, CH])
        assert placed[0] <= 40 * K
        placed[0] = 56 * K
        Hc = seq("Hc", [P, GB, TAPS * CH])
        Hs = seq("Hs", [P, GB, TAPS * CH])
        Gt = seq("Gt", [P, GB, 2 * P])
        Tz = seq("Tz", [P, GB, L * CH])
        Er = seq("Er", [P, GB, NCH])
        Ei = seq("Ei", [P, GB, NCH])
        KTp = seq("KTp", [CH, GB, ZPAD + L * CH])
        assert placed[0] <= 89 * K, placed
        placed[0] = 0
        Bo = seq("Bo", [P, G_ALL, CH])
        Bx = seq("Bx", [P, G_ALL, CH])
        Co = seq("Co", [P, G_ALL, CH])
        Cx = seq("Cx", [P, G_ALL, CH])
        dsk = at("dsk", 90 * K, [CH, G_ALL, CH])
        ynat = at("ynat", 56 * K, [NCH, L, T])
        yT = at("yT", 72 * K, [P, 4, T])
        y_hi = at("y_hi", 80 * K, [P, 4, T], F32R)
        y_lo = at("y_lo", 32 * K, [P, 4, T], F32R)
        sg_t = at("sg_t", 24 * K, [P, 2, T])
        mx_t = at("mx_t", 28 * K, [P, 2, T])

        ps = [ctx.enter_context(nc.psum_tensor(f"ps{b}", [P, 512], F32)) for b in range(8)]
        block = ctx.enter_context(nc.Block())

        class Count:

            def __init__(self):
                self.at, self.turn, self.reg = {}, {}, None

            def __call__(self, name, more=0):
                n = self.at.get(name, 0) + more
                return n if self.reg is None or not self.turn.get(name) else self.reg * self.turn[name] + n

            def add(self, name, n=1):
                self.at[name] = self.at.get(name, 0) + n
                return self(name)

            def base(self, name):
                return self.at.get(name, 0)

            def loop(self, eng, turns, turn):
                self.turn, before = turn, dict(self.at)
                with eng.Fori(0, turns) as reg:
                    self.reg = reg
                    yield reg
                for name, n in self.at.items():
                    assert n - before.get(name, 0) == turn.get(name, 0), (name, n - before.get(name, 0), turn.get(name, 0))
                    self.at[name] = before.get(name, 0) + turns * turn.get(name, 0)
                self.reg, self.turn = None, {}

        def ps_of(c):
            return ps[c.base("bank") % 8]

        def wait(eng, name, value):
            if not isinstance(value, int) or value > 0:
                eng.wait_ge(sem(name), value)

        A_WALK = [("p", 0), ("p", 1), ("x", 0), ("p", 2), ("x", 1), ("p", 3), ("x", 2), ("v", 0), ("x", 3), ("v", 1)]
        UNITS_A = [(h, it) for h in range(A_HEADS) for it in range(TT)]
        UNITS_H = [(i, g, it, br) for i in range(4) for g in range(H_GROUPS) for it in range(TT) for br in range(N_BR)]
        NUA, NUH = len(UNITS_A), len(UNITS_H)

        @block.sync
        def _(sp):
            for name, tile in (("xT", xT), ("ident", ident), ("norm_g", norm_g), ("mod_b", mod_b), ("aqk_g", aqk_g), ("bv_g", bv_g)):
                sp.dma_start(tile[:], I[name]).then_inc(sem("consts_in"), 16)
            for s in range(2):
                sp.dma_start(w_raw[:, s, :], I["slabs"][s]).then_inc(sem(f"raw_in{s}"), 16)
            with sp.Fori(1, N_SLABS // 2) as i:
                for s in range(2):
                    sp.wait_ge(sem("lo_done"), i * 2 + (s - 1))
                    sp.dma_start(w_raw[:, s, :], I["slabs"][i * 2 + s]).then_inc(sem(f"raw_in{s}"), 16)
            for m in range(KT):
                sp.wait_ge(sem("x_final"), m + 1)
                sp.dma_start(out[:, m, :], xT[:, m, :]).then_inc(sem("stored"), 16)
            sp.wait_ge(sem("stored"), 16 * KT)

        @block.gpsimd
        def _(gp):
            for s in range(2):
                gp.dma_start(cond[:, s, :], I["c"][s:s + 1, :].to_broadcast([P, D])).then_inc(sem("c_in"), 16)
            gp.memset(ones[:], 1.0).then_inc(sem("ones_set"), 1)
            gp.memset(eps[:], EPS).then_inc(sem("ones_set"), 1)

            def ada(k0, k1):
                for k in range(k0, k1):
                    if k >= 2:
                        gp.wait_ge(sem("ada_used"), k - 1)
                    gp.dma_start(ada_raw[:, k % 2, :], I["ada"][k]).then_inc(sem(f"ada_in{k % 2}"), 16)

            ada(0, 16)
            gp.wait_ge(sem("acc_free"), 40)
            for h in range(A_HEADS):
                if h >= 3:
                    gp.wait_ge(sem("s_done"), TT * (h - 2))
                gp.dma_start(a_bias[:, h % 3, :], I["a_bias"][h]).then_inc(sem(f"bias_in{h % 3}"), 16)
                ada(16 + 2 * h, 18 + 2 * h)
            with gp.Fori(0, ADA_TILES // 2) as i:
                for s in range(2):
                    gp.wait_ge(sem("ada_used"), i * 2 + (ADA_TILES + s - 1))
                    gp.dma_start(ada_raw[:, s, :], I["ada"][i * 2 + (ADA_TILES + s)]).then_inc(sem(f"ada_in{s}"), 16)
            gp.wait_ge(sem("slab_used"), S_BV)
            gp.dma_start(b_ws[:], I["b_ws"]).then_inc(sem("bws_in"), 16)
            gp.dma_start(b_bs[:], I["b_bs"][0:1].to_broadcast([P, SG_GROUPS, P])).then_inc(sem("bws_in"), 16)
            with gp.Fori(0, ADA2_TILES // 2) as i:
                for s in range(2):
                    gp.wait_ge(sem("ada_used"), i * 2 + (2 * ADA_TILES + s - 1))
                    gp.dma_start(ada_raw[:, s, :], I["ada"][i * 2 + (2 * ADA_TILES + s)]).then_inc(sem(f"ada_in{s}"), 16)
            gp.wait_ge(sem("ada_used"), N_ADA)

            small = [("h_cmask", h_cmask), ("h_flag", h_flag), ("cos", cos), ("sin", sin), ("qg_b", qg_b), ("kg_b", kg_b),
                     ("wg", wg), ("posT", posT), ("w2c", w2c), ("kcg_b", kcg_b), ("h_mask", h_mask), ("glu_b", glu_b),
                     ("sgn", sgn), ("s5_ar", par["ar"]), ("s5_ai", par["ai"]), ("s5_dt", par["dt"]), ("dsk", dsk)]
            for name, tile in small:
                gp.dma_start(tile[:], I[name]).then_inc(sem("h_in"), 16)
            gp.wait_ge(sem("hx_done"), 4)
            for name, tile in (("Bo", Bo), ("Bx", Bx), ("Co", Co), ("Cx", Cx)):
                gp.dma_start(tile[:], I[name]).then_inc(sem("s5_in"), 16)
            for b in range(NBLK):
                gp.wait_ge(sem("ktp_done"), b + 1)
                if b:
                    gp.wait_ge(sem("y_mm"), b)
                for j in range(L):
                    gp.dma_start(Tz[CH * j:CH * (j + 1), :, :], KTp[:, :, ZPAD - CH * j:ZPAD - CH * j + L * CH])\
                      .then_inc(sem("tz_in"), 16)

        @block.tensor
        def _(pe):
            c = Count()
            mm = nc.tensor.matmul

            def bank(full=False):
                wait(pe, "acc_free", c("bank", -7))
                b = ps_of(c)
                c.add("bank")
                return b

            def three(o, w, x, start, stop, weights_move=False):
                for n, (a, b) in enumerate(((0, 0), (0, 1), (1, 0))):
                    l, r = (x[a], w[b]) if weights_move else (w[a], x[b])
                    last = mm(o, l, r, start=start and n == 0, stop=stop and n == 2)
                return last

            def slab_t(x, nk=KT, tiles=2, ready=None, first=True, final=True, after=None, banks=None, n=T):
                s = c.base("slab") % 2
                wait(pe, "lo_done", c("slab", 1))
                for m in range(tiles):
                    b = banks[m] if banks else bank()
                    for k in range(nk):
                        if ready and m == 0:
                            pe.wait_ge(sem(ready[0]), c(ready[1], k + 1))
                        cols = slice((k * tiles + m) * P, (k * tiles + m + 1) * P)
                        last = three(b[:, 0:n], (w_hi[s][:, cols], w_lo[s][:, cols]), (x[0](k), x[1](k)),
                                     first and k == 0, final and k == nk - 1)
                    last.then_inc(sem("slab_used" if m == tiles - 1 else "acc_full"), 1)
                    if after:
                        after(m)
                if ready:
                    c.add(ready[1], nk)
                c.add("slab")

            def tile_of(hi, lo):
                return (lambda k: hi[:, k, :]), (lambda k: lo[:, k, :])

            H = tile_of(h_hi, h_lo)

            def panel_natural():
                bs = [bank() for _ in range(TT)]
                for half in range(2):
                    s = c.base("slab") % 2
                    wait(pe, "lo_done", c("slab", 1))
                    for t in range(TT):
                        ts = slice(t * P, (t + 1) * P)
                        for kk in range(4):
                            k, cols = 4 * half + kk, slice(kk * 512, (kk + 1) * 512)
                            last = three(bs[t][:], (w_hi[s][:, cols], w_lo[s][:, cols]), (h_hi[:, k, ts], h_lo[:, k, ts]),
                                         k == 0, k == KT - 1, weights_move=True)
                        if t == TT - 1:
                            last.then_inc(sem("slab_used"), 1)
                        elif half:
                            last.then_inc(sem("acc_full"), 1)
                    c.add("slab")

            def norm():
                pe.wait_ge(sem("nsq"), KT * c.add("norm"))
                b = bank()
                for t in range(TT):
                    for k in range(KT):
                        last = mm(b[:, t:t + 1], sq_x[:, k, t * P:(t + 1) * P], ones[:, 0:1], start=k == 0, stop=k == KT - 1)
                last.then_inc(sem("nsum"), 1)
                pe.wait_ge(sem("ndiag"), TT * c("norm"))
                b = bank()
                for t in range(TT):
                    last = mm(b[:, t * P:(t + 1) * P], ones[:], diag[:, t, :], start=True, stop=True)
                last.then_inc(sem("nbc"), 1)
                pe.wait_ge(sem("nlo"), KT * c("norm"))

            def transposes(src, signal, parts=P):
                b, col = bank(), 0
                for a in src:
                    w = a.shape[0]
                    last = nc.tensor.transpose(b[0:a.shape[-1], col:col + w], a, ident[0:w, 0:w])
                    col += w
                last.then_inc(sem(signal), 1)

            def attention(units, score, value, pre):
                U = len(units)
                for s in range(U + 3):
                    if s < U:
                        if s >= 3:
                            pe.wait_ge(sem(pre + "s_done"), s - 2)
                        q, k, n = score(units[s])
                        mm(ps[s % 3][:, 0:n], q, k, start=True, stop=True).then_inc(sem(pre + "s_full"), 1)
                    u = s - 2
                    if 0 <= u < U:
                        pe.wait_ge(sem(pre + "p_ready"), u + 1)
                        if u >= 3:
                            pe.wait_ge(sem(pre + "pt_ready"), u - 2)
                        n = score(units[u])[2]
                        b, pt = ps[3 + u % 3], (a_p if pre == "" else h_p)
                        for j in range(0, n, P):
                            w = min(P, n)
                            last = nc.tensor.transpose(b[0:w, j:j + P], pt[:, u % 3, j:j + w], ident[:])
                        last.then_inc(sem(pre + "t_full"), 1)
                    u = s - 3
                    if 0 <= u < U:
                        pe.wait_ge(sem(pre + "pt_ready"), u + 1)
                        if u >= 2:
                            pe.wait_ge(sem(pre + "o_done"), u - 1)
                        b, n = ps[6 + u % 2], score(units[u])[2]
                        pt, nb = (a_pt if pre == "" else h_pt), max(1, n // P)
                        for j in range(nb):
                            w = min(P, n)
                            last = mm(b[:, 0:HD], pt[0:w, u % 3, j * P:(j + 1) * P], value(units[u], j), start=j == 0, stop=j == nb - 1)
                        last.then_inc(sem(pre + "o_full"), 1)

            def ffn():
                turn = dict(slab=8, bank=16, hid=KT)
                for _ in c.loop(pe, QUARTERS, turn):
                    for _ in range(4):
                        slab_t(H)
                    for s in range(4):
                        slab_t(tile_of(hid_hi, hid_lo), ready=("hid_lo_done", "hid") if s == 0 else None)

            pe.wait_ge(sem("consts_in"), 96)
            pe.wait_ge(sem("ones_set"), 2)
            norm()
            for kind, p in A_WALK:
                if kind != "x":
                    panel_natural()
                else:
                    pe.wait_ge(sem("qn_done"), p + 1)
                    for b in range(4):
                        transposes([a_qn[:, p % 2, t, b * P:(b + 1) * P] for t in range(TT)], "xp_full")
            pe.wait_ge(sem("acc_free"), c("bank"))

            def score_a(u):
                h, it = u
                r = slice(HD * (h % 2), HD * (h % 2) + HD)
                return a_qT[r, h // 2, it * P:(it + 1) * P], a_kT[r, h // 2, 0:P * (it + 1)], P * (it + 1)

            attention(UNITS_A, score_a, lambda u, j: a_v[:, j, u[0] * HD:(u[0] + 1) * HD], "")
            pe.wait_ge(sem("o_done"), NUA)
            for i in range(KT):
                transposes([a_o[:, t, i * P:(i + 1) * P] for t in range(TT)], "xo_full")
            pe.wait_ge(sem("xo_lo"), KT)
            for _ in range(N_AOUT):
                slab_t(H)
            norm()
            ffn()

            norm()
            for _ in range(6):
                panel_natural()
            pe.wait_ge(sem("bws_masked"), 1)
            for ch in range(CHUNKS):
                for s in range(4):
                    def mix(m):
                        gm = KT * ch + 2 * s + m
                        if gm == 0:
                            pe.wait_ge(sem("bv_scaled"), TT)
                        b = bank()
                        for t in range(TT):
                            last = mm(b[:, t * P:(t + 1) * P], b_v[:, t, gm * P:(gm + 1) * P], b_ws[:, gm // 3, :], start=True, stop=True)
                        last.then_inc(sem("mix_full"), 1)
                    slab_t(H, after=mix)
                for s in range(4):
                    slab_t(tile_of(g_hi, g_lo), ready=("g_lo_done", "g") if s == 0 else None)
            norm()
            ffn()

            norm()
            panel_natural()
            panel_natural()
            pe.wait_ge(sem("wg_split"), 1)
            b = bank()
            for t in range(TT):
                for k in range(KT):
                    last = three(b[:, t * 24:(t + 1) * 24], (wg_hi[:, k, :], wg_lo[:, k, :]),
                                 (h_hi[:, k, t * P:(t + 1) * P], h_lo[:, k, t * P:(t + 1) * P]), k == 0, k == KT - 1, weights_move=True)
            last.then_inc(sem("gates_full"), 1)
            for _ in range(7):
                slab_t(H)
            pe.wait_ge(sem("hq_done"), 1)
            for i in range(4):
                transposes([h_qn[:, t, i * P:(i + 1) * P] for t in range(TT)], "hx_full")
            for i in range(4):
                transposes([h_qr[:, t, i * P:(i + 1) * P] for t in range(TT)], "hx_full")
            pe.wait_ge(sem("hk_done"), 1)
            for i in range(2):
                transposes([h_kr[:, t, i * P:(i + 1) * P] for t in range(TT)], "hx_full")
            for kind in range(2):
                pe.wait_ge(sem("bl_done"), kind + 1)
                bs = [bank(), bank()]
                for s in range(2):
                    x = (lambda k, s=s: bl_hi[:, 8 * s + k, :]), (lambda k, s=s: bl_lo[:, 8 * s + k, :])
                    slab_t(x, banks=bs, first=s == 0, final=s == 1, n=2 * CMP_PAD)
            pe.wait_ge(sem("hdn_done"), 2)
            b = bank()
            for kind in range(2):
                for g in range(H_GROUPS):
                    for m in range(2):
                        col = (kind * 2 + g) * HD
                        last = mm(b[0:CMP_PAD, col:col + HD], hdn[:, kind, m, g * CMP_PAD:(g + 1) * CMP_PAD], w2c[:, kind, m, :],
                                  start=m == 0, stop=m == 1)
            last.then_inc(sem("kc_full"), 1)
            pe.wait_ge(sem("kcn_done"), 1)
            transposes([kcn[:].rearrange("n g d -> n (g d)")], "kct_full")
            pe.wait_ge(sem("acc_free"), c("bank"))

            def score_h(u):
                i, g, it, br = u
                r, ts = slice(HD * g, HD * g + HD), slice(it * P, (it + 1) * P)
                if br == 0:
                    return hq[r, i, ts], kcT[r, :], CMP_PAD
                return hqr[r, i, ts], hk[r, br - 1, 0:P * (it + 1)], P * (it + 1)

            def value_h(u, j):
                i, g, it, br = u
                return vc[:, g, :] if br == 0 else hv[:, j, (br - 1) * P + g * HD:(br - 1) * P + (g + 1) * HD]

            attention(UNITS_H, score_h, value_h, "h")
            pe.wait_ge(sem("ho_done"), NUH)
            for i in range(4):
                transposes([h_o[:, t, i * P:(i + 1) * P] for t in range(TT)], "hxo_full")

            pe.wait_ge(sem("hx_done"), 4)
            for ct in range(4):
                for jj in range(2):
                    transposes([uT[:, ct, :].rearrange("p (n j) -> p j n", j=L)[:, 4 * jj + j, :] for j in range(4)], "u_full")
            pe.wait_ge(sem("u_done"), 8)
            for q in range(4):
                transposes([U[:, 8 * q + g, :] for g in range(8)], "ut_full")
            pe.wait_ge(sem("ut_done"), 4)
            for blk in range(NBLK):
                pe.wait_ge(sem("gb_done"), blk + 1)
                for q in range(2):
                    transposes([Gb[:, 4 * q + g, :] for g in range(4)], "gb_full")
                pe.wait_ge(sem("hc_done"), blk + 1)
                for q in range(2):
                    b = bank()
                    for g in range(4):
                        last = mm(b[0:CH, g * P:(g + 1) * P], bbo[:, 4 * q + g, :], Hc[:, 4 * q + g, 0:L * CH], start=True, stop=True)
                    last.then_inc(sem("kt_full"), 1)
                pe.wait_ge(sem("gt_done"), 2 * (blk + 1))
                for q in range(2):
                    b = bank()
                    for g in range(GB):
                        last = mm(b[:, g * NCH:(g + 1) * NCH], Gt[:, g, q * P:(q + 1) * P], UT[:, blk * GB + g, :], start=True, stop=True)
                    last.then_inc(sem("x_full"), 1)
                pe.wait_ge(sem("tz_in"), 16 * L * (blk + 1))
                pe.wait_ge(sem("st_done"), blk + 1)
                b = bank()
                for g in range(GB):
                    o, o1 = b[:, g * NCH:(g + 1) * NCH], b[:, g * NCH + 1:(g + 1) * NCH]
                    mm(o, Tz[:, g, :], UT[:, blk * GB + g, :], start=True, stop=False)
                    mm(o1, Hc[:, g, CH:], t_a[:, g, 0:NCH - 1], start=False, stop=False)
                    last = mm(o1, Hs[:, g, CH:], t_b[:, g, 0:NCH - 1], start=False, stop=True)
                last.then_inc(sem("y_mm"), 1)
            pe.wait_ge(sem("y_done"), NBLK)
            for q in range(8):
                transposes([Y[:, 4 * q + g, :] for g in range(4)], "yn_full")
            pe.wait_ge(sem("yn_gelu"), 1)
            for ct in range(4):
                transposes([ynat[:, i, ct * P:(ct + 1) * P] for i in range(L)], "yt_full")
            pe.wait_ge(sem("y_lo_done"), 4)
            slab_t(tile_of(y_hi, y_lo), nk=4, tiles=4)
            pe.wait_ge(sem("mix_lo"), 4)
            pe.wait_ge(sem("hx_done"), 4)
            for _ in range(4):
                slab_t(H)

        @block.scalar
        def _(act):
            c = Count()
            A = nc.scalar.activation

            def split():
                n = c.base("split")
                if c.reg is None and n >= N_SLABS:
                    return
                s = n % 2
                act.wait_ge(sem(f"raw_in{s}"), (c("split", -s) if c.reg is None else c("split", -s)) * 8 + 16)
                wait(act, "slab_used", c("split", -1))
                A(w_hi[s][:], w_raw[:, s, :], ACT.Copy).then_inc(sem("hi_done"), 1)
                c.add("split")

            def full(m, tiles=2):
                if m == tiles - 1:
                    act.wait_ge(sem("slab_used"), c("slab", 1))
                else:
                    act.wait_ge(sem("acc_full"), c.add("full"))
                b = ps_of(c)
                c.add("bank")
                return b

            def skip_t(tiles=2):
                split()
                c.add("full", tiles - 1)
                c.add("bank", tiles)
                c.add("slab")

            def natural(use):
                split()
                c.add("slab")
                split()
                for t in range(TT):
                    use(t, full(t, TT)) if use else (c.add("bank"), c.add("full", t < TT - 1))
                c.add("slab")

            def norm(shift):
                n = c.add("norm")
                wait(act, "acc_free", c("bank"))
                for k in range(KT):
                    A(sq_x[:, k, :], xT[:, k, :], ACT.Square).then_inc(sem("nsq"), 1)
                act.wait_ge(sem("nsum"), n)
                A(stat[:, 0:TT], ps_of(c)[:, 0:TT], ACT.Sqrt, bias=eps[:], scale=1.0 / D).then_inc(sem("nstd"), 1)
                c.add("bank", 2)
                for k in range(KT):
                    if k < KT - 1:
                        act.wait_ge(sem("npre"), (KT - 1) * (n - 1) + k + 1)
                    else:
                        act.wait_ge(sem("acc_free"), c("bank"))
                    A(h_hi[:, k, :], pre[:, k, :], ACT.Identity, bias=mod[:, shift + k:shift + k + 1]).then_inc(sem("nhi"), 1)

            def attention(units, width, pre):
                U = len(units)
                S, Pm, PT = (a_s, a_p, a_pt) if pre == "" else (h_s, h_p, h_pt)
                for s in range(U + 2):
                    if s < U:
                        n = width(units[s])
                        act.wait_ge(sem(pre + "s_done"), s + 1)
                        if s >= 3:
                            act.wait_ge(sem(pre + "t_full"), s - 2)
                        if s >= 4:
                            act.wait_ge(sem(pre + "inv_done"), s - 3)
                        A(Pm[:, s % 3, 0:n], S[:, s % 2, 0:n], ACT.Exp, bias=neg_max[:, s % 4:s % 4 + 1], scale=-1.0,
                          accum_out=row_sum[:, s % 4:s % 4 + 1]).then_inc(sem(pre + "p_ready"), 1)
                    u = s - 2
                    if 0 <= u < U:
                        n = width(units[u])
                        w = min(P, n)
                        act.wait_ge(sem(pre + "t_full"), u + 1)
                        if u >= 3:
                            act.wait_ge(sem(pre + "o_full"), u - 2)
                        A(PT[0:w, u % 3, 0:max(P, n)], ps[3 + u % 3][0:w, 0:max(P, n)], ACT.Copy).then_inc(sem(pre + "pt_ready"), 1)

            def ffn():
                turn = dict(slab=8, split=8, bank=16, full=8, hid=KT, used=8)
                for _ in c.loop(act, QUARTERS, turn):
                    for s in range(4):
                        split()
                        for m in range(2):
                            g = 2 * s + m
                            b = full(m)
                            A(relu[:, g % 2, :], b[:], ACT.Relu).then_inc(sem("relu_done"), 1)
                            if g:
                                high(g - 1, 1)
                        c.add("slab")
                    high(KT - 1, 0)
                    for s in range(4):
                        skip_t()
                    c.add("hid", KT)
                    c.add("used", 8)

            def high(g, behind):
                act.wait_ge(sem("acc_free"), c("bank", -behind))
                A(hid_hi[:, g, :], relu2[:, g % 2, :], ACT.Copy).then_inc(sem("hid_hi_done"), 1)

            act.wait_ge(sem("c_in"), 32)
            for s in range(2):
                A(cond[:, s, :], cond[:, s, :], ACT.Silu).then_inc(sem("cond_done"), 1)
            act.wait_ge(sem("consts_in"), 96)
            act.wait_ge(sem("ones_set"), 2)
            split()
            norm(0)
            for kind, p in A_WALK:
                if kind == "p":
                    def square(t, b):
                        wait(act, "a_red", p)
                        A(a_sq[:, t, :], b[:], ACT.Square).then_inc(sem("a_sq_done"), 1)
                    natural(square)
                    act.wait_ge(sem("a_red"), p + 1)
                    A(rstd[:], stat[:], ACT.Sqrt, bias=eps[:], scale=1.0 / HD).then_inc(sem("a_std"), 1)
                elif kind == "v":
                    natural(None)
                else:
                    c.add("bank", 4)
            attention(UNITS_A, lambda u: P * (u[1] + 1), "")
            for i in range(KT):
                act.wait_ge(sem("xo_full"), i + 1)
                A(h_hi[:, i, :], ps_of(c)[:], ACT.Copy).then_inc(sem("xo_hi"), 1)
                c.add("bank")
            for _ in range(N_AOUT):
                skip_t()
            norm(24)
            ffn()

            norm(48)
            for p in range(6):
                natural(lambda t, b: A(b_v[:, t, p * 512:(p + 1) * 512], b[:], ACT.Gelu).then_inc(sem("bv_done"), 1))
            act.wait_ge(sem("v_red"), 1)
            A(stat[:, 0:TT], stat[:, 0:TT], ACT.Sqrt, bias=eps[:], scale=1.0 / SG_HALF).then_inc(sem("v_std"), 1)
            for ch in range(CHUNKS):
                for s in range(4):
                    split()
                    for m in range(2):
                        b = full(m)
                        wait(act, "acc_free", c("bank", -1))
                        A(b_u[:], b[:], ACT.Gelu).then_inc(sem("bu_done"), 1)
                        c.add("bank")
                        act.wait_ge(sem("acc_free"), c("bank"))
                        A(g_hi[:, 2 * s + m, :], b_vm[:], ACT.Copy).then_inc(sem("g_hi_done"), 1)
                    c.add("slab")
                for _ in range(4):
                    skip_t()
            norm(72)
            ffn()

            norm(96)

            def square_q(t, b):
                A(h_sq[:, t, :], b[:], ACT.Square).then_inc(sem("h_sq_done"), 1)
            natural(square_q)
            act.wait_ge(sem("h_red"), 1)
            A(rstd[:], stat[:], ACT.Sqrt, bias=eps[:], scale=1.0 / HD).then_inc(sem("h_std"), 1)
            act.wait_ge(sem("hq_done"), 1)

            def square_k(t, b):
                A(h_t1[:, t, :, :], b[:, 0:256].rearrange("p (a b) -> p a b", b=32), ACT.Square).then_inc(sem("h_sq_done"), 1)
            natural(square_k)
            act.wait_ge(sem("h_red"), 2)
            A(rstd[:, 0:16], stat[:, 0:16], ACT.Sqrt, bias=eps[:], scale=1.0 / HD).then_inc(sem("h_std"), 1)
            c.add("bank")
            act.wait_ge(sem("gates_copied"), 1)
            A(h_gts[:], h_gts[:], ACT.Sigmoid).then_inc(sem("gts_done"), 1)
            for _ in range(7):
                skip_t()
            act.wait_ge(sem("z_copied"), 1)
            A(za[:], za[:], ACT.Silu).then_inc(sem("z_done"), 1)
            A(zs[:], zs[:], ACT.Silu).then_inc(sem("z_done"), 1)
            c.add("bank", 10)
            for kind in range(2):
                split()
                c.add("slab")
                split()
                c.add("slab")
                c.add("full", 2)
                c.add("bank", 2)
                act.wait_ge(sem("hdn_copied"), kind + 1)
                A(hdn[:, kind, :, :], hdn[:, kind, :, :], ACT.Gelu_apprx_tanh).then_inc(sem("hdn_done"), 1)
            act.wait_ge(sem("kc_red"), 1)
            A(kst[:, 0:2], kst[:, 0:2], ACT.Sqrt, bias=eps[0:CMP_PAD, :], scale=1.0 / HD).then_inc(sem("kc_std"), 1)
            c.add("bank", 2)
            attention(UNITS_H, lambda u: CMP_PAD if u[3] == 0 else P * (u[2] + 1), "h")
            for i in range(4):
                act.wait_ge(sem("hxo_gated"), i + 1)
                A(h_hi[:, i, :], h_pt[:, i % 2, :], ACT.Copy).then_inc(sem("hxo_hi"), 1)
                c.add("bank")
            A(par["dt"][:], par["dt"][:], ACT.Exp).then_inc(sem("dt_done"), 1)
            act.wait_ge(sem("ang_done"), 1)
            A(par["r1"][:], par["xr"][:], ACT.Exp).then_inc(sem("trig_done"), 1)
            A(par["r8"][:], par["xr"][:], ACT.Exp, scale=float(L)).then_inc(sem("trig_done"), 1)
            A(par["sn"][:], par["th"][:], ACT.Sin).then_inc(sem("trig_done"), 1)
            A(par["h2"][:], par["th"][:], ACT.Sin, scale=0.5).then_inc(sem("trig_done"), 1)
            act.wait_ge(sem("yn_done"), 8)
            A(ynat[:], ynat[:], ACT.Gelu_apprx_tanh).then_inc(sem("yn_gelu"), 1)
            c.add("bank", 8 + 4 + NBLK * 7 + 8)
            for ct in range(4):
                act.wait_ge(sem("yt_done"), ct + 1)
                A(y_hi[:, ct, :], yT[:, ct, :], ACT.Copy).then_inc(sem("y_hi_done"), 1)
                c.add("bank")
            split()
            for m in range(4):
                b = full(m, 4)
                if m >= 2:
                    act.wait_ge(sem("acc_free"), c("bank", -2))
                A(sg_t[:, m % 2, :], b[:], ACT.Sigmoid, bias=glu_b[:, m:m + 1]).then_inc(sem("sg_done"), 1)
                act.wait_ge(sem("mx_done"), m + 1)
                A(h_hi[:, 4 + m, :], mx_t[:, m % 2, :], ACT.Copy).then_inc(sem("mix_hi"), 1)
            c.add("slab")
            for _ in range(4):
                skip_t()

        @block.vector
        def _(dve):
            c = Count()
            V = nc.vector
            tt, ts_, stt, cp = V.tensor_tensor, V.tensor_scalar, V.scalar_tensor_tensor, V.tensor_copy

            def step(ins, *more):
                for i in (ins, *more):
                    i.then_inc(sem("dve_step"), 1)
                    c.add("step")
                dve.wait_ge(sem("dve_step"), c("step"))

            def split():
                n = c.base("split")
                if c.reg is None and n >= N_SLABS:
                    return
                s = n % 2
                dve.wait_ge(sem("hi_done"), c("split", 1))
                tt(w_lo[s][:], w_raw[:, s, :], w_hi[s][:].bitcast(F32), ALU.subtract).then_inc(sem("lo_done"), 1)
                c.add("split")

            def full(m, tiles=2):
                if m == tiles - 1:
                    dve.wait_ge(sem("slab_used"), c("slab", 1))
                else:
                    dve.wait_ge(sem("acc_full"), c.add("full"))
                b = ps_of(c)
                c.add("bank")
                return b

            def free(ins, n=1):
                ins.then_inc(sem("acc_free"), n)

            def freed():
                dve.wait_ge(sem("acc_free"), c("bank"))

            def ada(n, which):
                k0, first = c.base("ada"), c("ada")
                for o in range(n):
                    s = (k0 + o) % 2
                    dve.wait_ge(sem(f"ada_in{s}"), c("ada", -s) * 8 + 16)
                    V.tensor_tensor_reduce(out=ada_raw[:, s, :], in0=ada_raw[:, s, :], in1=cond[:, which, :], scale=1.0,
                                           scalar=0.0, op0=ALU.mult, op1=ALU.add, accum_out=mod_s[:, o:o + 1]).then_inc(sem("ada_used"), 1)
                    c.add("ada")
                dve.wait_ge(sem("ada_used"), c("ada"))
                tt(mod[:, bass.ds(first, n)], mod_s[:, 0:n], mod_b[:, bass.ds(first, n)], ALU.add).then_inc(sem("mod_done"), 1)
                c.add("mod")
                dve.wait_ge(sem("mod_done"), c("mod"))

            def residual(g):
                for s in range(4):
                    split()
                    for m in range(2):
                        o = 2 * s + m
                        b = full(m)
                        free(stt(xT[:, o, :], b[:], mod[:, g + o:g + o + 1], xT[:, o, :], ALU.mult, ALU.add))
                    c.add("slab")

            def natural(use):
                split()
                c.add("slab")
                split()
                for t in range(TT):
                    use(t, full(t, TT))
                c.add("slab")

            def norm(i, shift, gather=None):
                n = c.add("norm")
                step(stt(mod_a[:], mod[:, shift + 8:shift + 16], 1.0, norm_g[:, i, :], ALU.add, ALU.mult))
                dve.wait_ge(sem("nstd"), n)
                c.add("bank")
                free(V.reciprocal(rstd[:, 0:TT], stat[:, 0:TT]))
                freed()
                for t in range(TT):
                    ts_(diag[:, t, :], ident[:], rstd[:, t:t + 1], None, ALU.mult).then_inc(sem("ndiag"), 1)
                dve.wait_ge(sem("nbc"), n)
                b = ps_of(c)
                c.add("bank")
                for k in range(KT):
                    ins = stt(pre[:, k, :], xT[:, k, :], mod_a[:, k:k + 1], b[:], ALU.mult, ALU.mult)
                    if k < KT - 1:
                        ins.then_inc(sem("npre"), 1)
                    else:
                        free(ins)
                for k in range(KT):
                    dve.wait_ge(sem("nhi"), KT * (n - 1) + k + 1)
                    stt(h_lo[:, k, :], pre[:, k, :], mod[:, shift + k:shift + k + 1], h_hi[:, k, :].bitcast(F32), ALU.add, ALU.subtract)\
                        .then_inc(sem("nlo"), 1)

            def attention(units, width, mask, combine, pre):
                U = len(units)
                S = a_s if pre == "" else h_s
                for s in range(U + 3):
                    if s < U:
                        n = width(units[s])
                        dve.wait_ge(sem(pre + "s_full"), s + 1)
                        if s >= 2:
                            dve.wait_ge(sem(pre + "p_ready"), s - 1)
                        V.tensor_tensor_reduce(out=S[:, s % 2, 0:n], in0=ps[s % 3][:, 0:n], in1=mask(units[s]), scale=-1.0,
                                               scalar=3e38, op0=ALU.add, op1=ALU.min, accum_out=neg_max[:, s % 4:s % 4 + 1])\
                         .then_inc(sem(pre + "s_done"), 1)
                    u = s - 3
                    if 0 <= u < U:
                        dve.wait_ge(sem(pre + "p_ready"), u + 1)
                        V.reciprocal(row_inv[:, u % 4:u % 4 + 1], row_sum[:, u % 4:u % 4 + 1]).then_inc(sem(pre + "inv_done"), 1)
                        dve.wait_ge(sem(pre + "inv_done"), u + 1)
                        combine(u, units[u])

            def ffn(g, tiles, which):
                turn = dict(slab=8, split=8, bank=16, full=8, hid=KT, ada=tiles, mod=1)
                for _ in c.loop(dve, QUARTERS, turn):
                    for s in range(4):
                        split()
                        for m in range(2):
                            o = 2 * s + m
                            b = full(m)
                            dve.wait_ge(sem("relu_done"), c("hid", o + 1))
                            if o >= 2:
                                dve.wait_ge(sem("hid_lo_done"), c("hid", o - 1))
                            free(stt(relu2[:, o % 2, :], b[:], 0.0, relu[:, o % 2, :], ALU.max, ALU.mult))
                            if o:
                                low(o - 1)
                        c.add("slab")
                    low(KT - 1)
                    c.add("hid", KT)
                    ada(tiles, which)
                    residual(g)

            def low(o):
                dve.wait_ge(sem("hid_hi_done"), c("hid", o + 1))
                tt(hid_lo[:, o, :], relu2[:, o % 2, :], hid_hi[:, o, :].bitcast(F32), ALU.subtract).then_inc(sem("hid_lo_done"), 1)

            dve.wait_ge(sem("consts_in"), 96)
            dve.wait_ge(sem("ones_set"), 2)
            dve.wait_ge(sem("cond_done"), 2)
            split()
            ada(16, 0)
            norm(0, 0)
            for kind, p in A_WALK:
                if kind == "p":
                    banks = {}
                    natural(lambda t, b: banks.setdefault(t, b))
                    dve.wait_ge(sem("a_sq_done"), TT * (p + 1))
                    V.tensor_reduce(stat[:], a_sq[:].rearrange("p t (h d) -> p (t h) d", d=HD), AX.X, ALU.add).then_inc(sem("a_red"), 1)
                    dve.wait_ge(sem("a_std"), p + 1)
                    step(V.reciprocal(stat[:], rstd[:]))
                    for t in range(TT):
                        free(tt(a_qn[:, p % 2, t, :].rearrange("p (h d) -> p h d", d=HD), banks[t][:].rearrange("p (h d) -> p h d", d=HD),
                                stat[:, 8 * t:8 * t + 8].unsqueeze(2).to_broadcast([P, 8, HD]), ALU.mult))
                    freed()
                    V.engine_nop().then_inc(sem("qn_done"), 1)
                elif kind == "v":
                    natural(lambda t, b: free(cp(a_v[:, t, p * 512:(p + 1) * 512], b[:])))
                else:
                    for i in range(4):
                        dve.wait_ge(sem("xp_full"), 4 * p + i + 1)
                        o = (a_qT if p < 2 else a_kT)[:, 4 * (p % 2) + i, :]
                        free(ts_(o, ps_of(c)[:], aqk_g[:, p // 2:p // 2 + 1], HD ** -0.5 if p < 2 else 1.0, ALU.mult, ALU.mult))
                        c.add("bank")

            def mask_a(u):
                h, it = u
                if it == 0:
                    dve.wait_ge(sem(f"bias_in{h % 3}"), 16 * (h // 3 + 1))
                return a_bias[:, h % 3, P * (TT - 1 - it):T]

            def combine_a(u, unit):
                h, it = unit
                dve.wait_ge(sem("o_full"), u + 1)
                ts_(a_o[:, it, h * HD:(h + 1) * HD], ps[6 + u % 2][:, 0:HD], row_inv[:, u % 4:u % 4 + 1], None, ALU.mult).then_inc(sem("o_done"), 1)
                if it == TT - 1:
                    ada(2, 0)

            attention(UNITS_A, lambda u: P * (u[1] + 1), mask_a, combine_a, "")
            for i in range(KT):
                dve.wait_ge(sem("xo_hi"), i + 1)
                tt(h_lo[:, i, :], ps_of(c)[:], h_hi[:, i, :].bitcast(F32), ALU.subtract).then_inc(sem("xo_lo"), 1)
                dve.wait_ge(sem("xo_lo"), i + 1)
                free(V.engine_nop())
                c.add("bank")
            residual(16)
            norm(1, 24)
            ffn(40, 12, 0)

            norm(2, 48)
            dve.wait_ge(sem("bws_in"), 32)
            V.memset(b_ws[HD:P, :, 0:HD], 0.0).then_inc(sem("bws_masked"), 1)
            for p in range(6):
                def sq(t, b):
                    dve.wait_ge(sem("bv_done"), TT * p + t + 1)
                    v = b_v[:, t, p * 512:(p + 1) * 512]
                    free(V.tensor_tensor_reduce(out=b[:], in0=v, in1=v, scale=1.0, scalar=0.0, op0=ALU.mult, op1=ALU.add,
                                                accum_out=vss[:, t, p:p + 1]))
                natural(sq)
            freed()
            V.tensor_reduce(stat[:, 0:TT], vss[:], AX.X, ALU.add).then_inc(sem("v_red"), 1)
            dve.wait_ge(sem("v_std"), 1)
            step(V.reciprocal(rstd[:, 0:TT], stat[:, 0:TT]))
            for t in range(TT):
                ts_(b_v[:, t, :], b_v[:, t, :], rstd[:, t:t + 1], None, ALU.mult).then_inc(sem("bv_scaled"), 1)
            for ch in range(CHUNKS):
                for s in range(4):
                    split()
                    for m in range(2):
                        gm = KT * ch + 2 * s + m
                        full(m)
                        dve.wait_ge(sem("mix_full"), gm + 1)
                        b = ps_of(c)
                        c.add("bank")
                        if gm:
                            dve.wait_ge(sem("g_lo_done"), gm)
                        stt(b_vm[:].rearrange("p (n i) -> p n i", i=P), b[:].rearrange("p (n i) -> p n i", i=P), bv_g[:, gm:gm + 1],
                            b_bs[:, gm // 3, :].unsqueeze(1).to_broadcast([P, TT, P]), ALU.mult, ALU.add).then_inc(sem("bvm_done"), 1)
                        dve.wait_ge(sem("bvm_done"), gm + 1)
                        dve.wait_ge(sem("bu_done"), gm + 1)
                        free(tt(b_vm[:], b_vm[:], b_u[:], ALU.mult), 2)
                        dve.wait_ge(sem("g_hi_done"), gm + 1)
                        tt(g_lo[:, 2 * s + m, :], b_vm[:], g_hi[:, 2 * s + m, :].bitcast(F32), ALU.subtract).then_inc(sem("g_lo_done"), 1)
                    c.add("slab")
                residual(64)
            norm(3, 72)
            ffn(88, 6, 1)

            norm(4, 96)
            N_SMALL = 17
            banks = {}
            natural(lambda t, b: banks.setdefault(t, b))
            dve.wait_ge(sem("h_sq_done"), TT)
            V.tensor_reduce(stat[:], h_sq[:].rearrange("p t (h d) -> p (t h) d", d=HD), AX.X, ALU.add).then_inc(sem("h_red"), 1)
            dve.wait_ge(sem("h_std"), 1)
            step(V.reciprocal(stat[:], rstd[:]))
            for t in range(TT):
                free(tt(h_qn[:, t, :].rearrange("p (h d) -> p h d", d=HD), banks[t][:].rearrange("p (h d) -> p h d", d=HD),
                        stat[:, 8 * t:8 * t + 8].unsqueeze(2).to_broadcast([P, 8, HD]), ALU.mult))
            freed()
            dve.wait_ge(sem("h_in"), 16 * N_SMALL)
            step(*[tt(h_qn[:, t, :].rearrange("p (h d) -> p h d", d=HD), h_qn[:, t, :].rearrange("p (h d) -> p h d", d=HD),
                      qg_b[:].unsqueeze(1).to_broadcast([P, 8, HD]), ALU.mult) for t in range(TT)])

            def rope(src, dst, heads, signal):
                x = src[:].rearrange("p t (h d) -> p t h d", d=HD)
                o = dst[:].rearrange("p t (h d) -> p t h d", d=HD)
                x1, x2, o1, o2 = x[:, :, :, 0:32], x[:, :, :, 32:HD], o[:, :, :, 0:32], o[:, :, :, 32:HD]
                co = cos[:].unsqueeze(2).to_broadcast([P, TT, heads, 32])
                si = sin[:].unsqueeze(2).to_broadcast([P, TT, heads, 32])
                a, b = h_t1[:, :, 0:heads, :], h_t2[:, :, 0:heads, :]
                step(tt(a, x1, co, ALU.mult), tt(b, x2, si, ALU.mult))
                step(tt(o1, a, b, ALU.subtract))
                step(tt(a, x2, co, ALU.mult), tt(b, x1, si, ALU.mult))
                tt(o2, a, b, ALU.add).then_inc(sem(signal), 1)
                dve.wait_ge(sem(signal), 1)

            rope(h_qn, h_qr, 8, "hq_done")
            step(cp(wg_hi[:], wg[:]))
            tt(wg_lo[:], wg[:], wg_hi[:].bitcast(F32), ALU.subtract).then_inc(sem("wg_split"), 1)
            banks = {}
            natural(lambda t, b: banks.setdefault(t, b))
            dve.wait_ge(sem("h_sq_done"), 2 * TT)
            V.tensor_reduce(stat[:, 0:16], h_t1[:].rearrange("p t a b -> p (t a b)").rearrange("p (n d) -> p n d", d=HD), AX.X, ALU.add)\
             .then_inc(sem("h_red"), 1)
            dve.wait_ge(sem("h_std"), 2)
            step(V.reciprocal(stat[:, 0:16], rstd[:, 0:16]))
            for t in range(TT):
                step(tt(h_kn[:, t, :].rearrange("p (h d) -> p h d", d=HD), banks[t][:, 0:256].rearrange("p (h d) -> p h d", d=HD),
                        stat[:, 4 * t:4 * t + 4].unsqueeze(2).to_broadcast([P, 4, HD]), ALU.mult))
                free(cp(hv[:, t, :], banks[t][:, 256:512]))
            step(*[tt(h_kn[:, t, :].rearrange("p (h d) -> p h d", d=HD), h_kn[:, t, :].rearrange("p (h d) -> p h d", d=HD),
                      kg_b[:], ALU.mult) for t in range(TT)])
            rope(h_kn, h_kr, 4, "hk_done")
            dve.wait_ge(sem("gates_full"), 1)
            b = ps_of(c)
            c.add("bank")
            step(cp(h_gts[:], b[:, 0:TT * 24].rearrange("p (t n) -> p t n", n=24)))
            V.engine_nop().then_inc(sem("gates_copied"), 1)
            free(V.engine_nop())
            for tile, tiles in ((crT, 2), (za, 4), (zs, 4), (uT, 4)):
                for s in range(tiles // 2):
                    split()
                    for m in range(2):
                        b = full(m)
                        free(cp(tile[:, 2 * s + m, :], b[:]))
                    c.add("slab")
                if tile is zs:
                    freed()
                    V.engine_nop().then_inc(sem("z_copied"), 1)
            freed()
            for i in range(8):
                dve.wait_ge(sem("hx_full"), i + 1)
                free(ts_((hq if i < 4 else hqr)[:, i % 4, :], ps_of(c)[:], HD ** -0.5, None, ALU.mult))
                c.add("bank")
            for i in range(2):
                dve.wait_ge(sem("hx_full"), 9 + i)
                free(cp(hk[:, i, :], ps_of(c)[:]))
                c.add("bank")
            step(V.memset(bl[:], 0.0))
            for kind in range(2):
                ins = []
                src = crT[:, kind, :].rearrange("p (n l) -> p l n", l=16)
                for lp in range(2):
                    for g in range(H_GROUPS):
                        r = slice(HD * g, HD * g + HD)
                        for half in range(2):
                            ins.append(tt(bl[HD * lp:HD * lp + HD, 8 * half:8 * half + 8, CMP_PAD * g:CMP_PAD * g + CMP_N],
                                          src[r, :, half:half + CMP_N].rearrange("p (a b) n -> p a b n", b=2)[:, :, lp, :],
                                          posT[r, kind, 16 * half:16 * half + 16].rearrange("p (a b) -> p a b", b=2)[:, :, lp].unsqueeze(2)
                                          .to_broadcast([HD, 8, CMP_N]), ALU.add))
                step(*ins)
                if kind:
                    dve.wait_ge(sem("slab_used"), S_HCK + 2)
                step(cp(bl_hi[:], bl[:]))
                tt(bl_lo[:], bl[:], bl_hi[:].bitcast(F32), ALU.subtract).then_inc(sem("bl_done"), 1)
                dve.wait_ge(sem("bl_done"), kind + 1)
                split()
                c.add("slab")
                split()
                c.add("full", 1)
                for m in range(2):
                    b = full(m)
                    free(cp(hdn[:, kind, m, :], b[:, 0:2 * CMP_PAD]))
                freed()
                V.engine_nop().then_inc(sem("hdn_copied"), 1)
                c.add("slab")
            dve.wait_ge(sem("kc_full"), 1)
            b = ps_of(c)
            c.add("bank")
            step(cp(kcn[:], b[0:CMP_PAD, 0:2 * HD].rearrange("n (g d) -> n g d", d=HD)),
                 cp(vc[:], b[0:CMP_PAD, 2 * HD:4 * HD].rearrange("n (g d) -> n g d", d=HD)))
            free(tt(kcsq[:], kcn[:], kcn[:], ALU.mult))
            freed()
            V.tensor_reduce(kst[:, 0:2], kcsq[:], AX.X, ALU.add).then_inc(sem("kc_red"), 1)
            dve.wait_ge(sem("kc_std"), 1)
            step(V.reciprocal(kst[:, 2:4], kst[:, 0:2]))
            step(tt(kcn[:], kcn[:], kst[:, 2:4].unsqueeze(2).to_broadcast([CMP_PAD, 2, HD]), ALU.mult))
            tt(kcn[:], kcn[:], kcg_b[:].unsqueeze(1).to_broadcast([CMP_PAD, 2, HD]), ALU.mult).then_inc(sem("kcn_done"), 1)
            dve.wait_ge(sem("kct_full"), 1)
            free(cp(kcT[:], ps_of(c)[:, 0:CMP_PAD]))
            c.add("bank")
            dve.wait_ge(sem("gts_done"), 1)

            def mask_h(u):
                i, g, it, br = u
                return h_cmask[:, it, :] if br == 0 else h_mask[:, P * (TT - 1 - it):T]

            def combine_h(u, unit):
                i, g, it, br = unit
                hp = 2 * i + g
                w = wbr[:, u % 4:u % 4 + 1]
                step(stt(w, row_inv[:, u % 4:u % 4 + 1], h_flag[:, it:it + 1] if br == 0 else 1.0,
                         h_gts[:, it, N_BR * hp + br:N_BR * hp + br + 1], ALU.mult, ALU.mult))
                dve.wait_ge(sem("ho_full"), u + 1)
                o, p_ = h_o[:, it, hp * HD:(hp + 1) * HD], ps[6 + u % 2][:, 0:HD]
                if br == 0:
                    ins = ts_(o, p_, w, None, ALU.mult)
                else:
                    dve.wait_ge(sem("ho_done"), u)
                    ins = stt(o, p_, w, o, ALU.mult, ALU.add)
                ins.then_inc(sem("ho_done"), 1)

            attention(UNITS_H, lambda u: CMP_PAD if u[3] == 0 else P * (u[2] + 1), mask_h, combine_h, "h")
            dve.wait_ge(sem("z_done"), 2)
            dve.wait_ge(sem("ho_done"), NUH)
            for i in range(4):
                dve.wait_ge(sem("hxo_full"), i + 1)
                tt(h_pt[:, i % 2, :], ps_of(c)[:], za[:, i, :], ALU.mult).then_inc(sem("hxo_gated"), 1)
                dve.wait_ge(sem("hxo_hi"), i + 1)
                tt(h_lo[:, i, :], h_pt[:, i % 2, :], h_hi[:, i, :].bitcast(F32), ALU.subtract).then_inc(sem("hx_done"), 1)
                dve.wait_ge(sem("hx_done"), i + 1)
                free(V.engine_nop())
                c.add("bank")

            p_ = {k: v[:] for k, v in par.items()}

            def m_(o, a, b, op=ALU.mult):
                return tt(p_[o], p_[a], p_[b], op)

            dve.wait_ge(sem("dt_done"), 1)
            step(m_("xr", "ar", "dt"), m_("th", "ai", "dt"))
            MAGIC, C1 = 12582912.0, 6.28125
            C2 = 2 * math.pi - C1
            PI_DOWN = 3.1415925
            step(ts_(p_["kk"], p_["th"], 1 / (2 * math.pi), MAGIC, ALU.mult, ALU.add))
            step(ts_(p_["kk"], p_["kk"], MAGIC, None, ALU.subtract))
            step(stt(p_["t1"], p_["kk"], -C1, p_["th"], ALU.mult, ALU.add))
            step(stt(p_["th"], p_["kk"], -C2, p_["t1"], ALU.mult, ALU.add))
            ts_(p_["th"], p_["th"], PI_DOWN, -PI_DOWN, ALU.min, ALU.max).then_inc(sem("ang_done"), 1)
            dve.wait_ge(sem("trig_done"), 4)
            step(m_("t1", "h2", "h2"))
            step(ts_(p_["cs"], p_["t1"], -2.0, 1.0, ALU.mult, ALU.add))
            step(V.memset(Lr[:, 0, :], 1.0), V.memset(Ls[:, 0, :], 0.0),
                 tt(Lr[:, 1, :], p_["r1"], p_["cs"], ALU.mult), tt(Ls[:, 1, :], p_["r1"], p_["sn"], ALU.mult))
            for lo, n in ((2, 1), (3, 2), (5, 4)):
                wide = lambda a: a.unsqueeze(1).to_broadcast([P, n, G_ALL])
                br_, bi_ = wide(Lr[:, lo - 1, :]), wide(Ls[:, lo - 1, :])
                a_r, a_i = Lr[:, 1:1 + n, :], Ls[:, 1:1 + n, :]
                v = [z[:].rearrange("p a b -> p (a b)")[:, 0:n * G_ALL].rearrange("p (a b) -> p a b", b=G_ALL)
                     for z in (t_a, t_b, Er, Ei)]
                step(tt(v[0], a_r, br_, ALU.mult), tt(v[1], a_i, bi_, ALU.mult), tt(v[2], a_r, bi_, ALU.mult), tt(v[3], a_i, br_, ALU.mult))
                step(tt(Lr[:, lo:lo + n, :], v[0], v[1], ALU.subtract), tt(Ls[:, lo:lo + n, :], v[2], v[3], ALU.add))
            step(ts_(p_["nr"], Lr[:, 1, :], 1.0, None, ALU.subtract), m_("t1", "ar", "ar"), m_("t2", "ai", "ai"))
            step(m_("t3", "t1", "t2", ALU.add))
            step(V.reciprocal(p_["d2"], p_["t3"]))
            step(m_("t1", "nr", "ar"), tt(p_["t2"], Ls[:, 1, :], p_["ai"], ALU.mult))
            step(m_("t3", "t1", "t2", ALU.add))
            step(m_("fr", "t3", "d2"))
            step(tt(p_["t1"], Ls[:, 1, :], p_["ar"], ALU.mult), m_("t2", "nr", "ai"))
            step(m_("t3", "t1", "t2", ALU.subtract))
            step(m_("fs", "t3", "d2"))
            step(ts_(p_["fs"], p_["fs"], sgn[:, 0:1], None, ALU.mult), ts_(Ls[:], Ls[:], sgn[:, 0:1], None, ALU.mult))
            step(*[cp(o[:, j, :], i_[:, L - 1 - j, :]) for o, i_ in ((LrR, Lr), (LsR, Ls)) for j in range(L)])
            step(cp(p_["er"], p_["cs"]), cp(p_["ei"], p_["sn"]))
            for _ in range(3):
                step(m_("t1", "er", "er"), m_("t2", "ei", "ei"), m_("t3", "er", "ei"))
                step(m_("er", "t1", "t2", ALU.subtract), ts_(p_["ei"], p_["t3"], 2.0, None, ALU.mult))

            for q in range(8):
                dve.wait_ge(sem("u_full"), q + 1)
                ct, jj = q // 2, q % 2
                src = ps_of(c)[0:NCH, :].rearrange("n (j g c) -> n j g c", j=4, g=8)
                for j in range(4):
                    ins = cp(U[:, 8 * ct:8 * ct + 8, (4 * jj + j) * CH:(4 * jj + j + 1) * CH], src[:, j, :, :])
                    if j < 3:
                        ins.then_inc(sem("dve_step"), 1)
                        c.add("step")
                dve.wait_ge(sem("dve_step"), c("step"))
                ins.then_inc(sem("u_done"), 1)
                dve.wait_ge(sem("u_done"), q + 1)
                free(V.engine_nop())
                c.add("bank")
            for q in range(4):
                dve.wait_ge(sem("ut_full"), q + 1)
                cp(UT[:, 8 * q:8 * q + 8, :], ps_of(c)[:].rearrange("p (g n) -> p g n", n=NCH)).then_inc(sem("ut_done"), 1)
                dve.wait_ge(sem("ut_done"), q + 1)
                free(V.engine_nop())
                c.add("bank")
            dve.wait_ge(sem("s5_in"), 64)
            step(V.memset(KTp[:, :, 0:ZPAD], 0.0))
            for blk in range(NBLK):
                gs = slice(blk * GB, (blk + 1) * GB)

                def over(a, n):
                    return a.unsqueeze(2).to_broadcast([P, GB, n])

                def taps(a, n):
                    return a.unsqueeze(2).to_broadcast([P, GB, n, CH])

                def power(a, n):
                    return a[:, 0:n, gs].rearrange("p n g -> p g n").unsqueeze(3).to_broadcast([P, GB, n, CH])

                def four(z, n):
                    return z[:, :, 0:n * CH].rearrange("p g (n c) -> p g n c", c=CH)

                fr, fs = over(par["fr"][:, gs], CH), over(par["fs"][:, gs], CH)
                ta, tb = t_a[:, :, 0:CH], t_b[:, :, 0:CH]
                tc, td = t_a[:, :, CH:2 * CH], t_b[:, :, CH:2 * CH]
                step(tt(ta, Bo[:, gs, :], fr, ALU.mult), tt(tb, Bx[:, gs, :], fs, ALU.mult),
                     tt(tc, Bx[:, gs, :], fr, ALU.mult), tt(td, Bo[:, gs, :], fs, ALU.mult))
                step(tt(bbo[:], ta, tb, ALU.add), tt(bbx[:], tc, td, ALU.subtract))
                step(tt(four(t_a, L), taps(bbo[:], L), power(LrR, L), ALU.mult), tt(four(t_b, L), taps(bbx[:], L), power(LsR, L), ALU.mult))
                tt(Gb[:], t_a[:, :, 0:L * CH], t_b[:, :, 0:L * CH], ALU.add).then_inc(sem("gb_done"), 1)
                dve.wait_ge(sem("gb_done"), blk + 1)
                step(tt(four(t_a, TAPS), taps(Co[:, gs, :], TAPS), power(Lr, TAPS), ALU.mult),
                     tt(four(t_b, TAPS), taps(Cx[:, gs, :], TAPS), power(Ls, TAPS), ALU.mult))
                step(tt(Hc[:], t_a[:], t_b[:], ALU.add))
                step(ts_(Hc[:], Hc[:], sgn[:, 1:2], None, ALU.mult))
                step(tt(four(t_a, TAPS), taps(Co[:, gs, :], TAPS), power(Ls, TAPS), ALU.mult),
                     tt(four(t_b, TAPS), taps(Cx[:, gs, :], TAPS), power(Lr, TAPS), ALU.mult))
                tt(Hs[:], t_a[:], t_b[:], ALU.subtract).then_inc(sem("hc_done"), 1)
                dve.wait_ge(sem("hc_done"), blk + 1)
                q_r, q_i = par["t1"][:, gs], par["t2"][:, gs]
                step(V.memset(Er[:, :, 0:1], 1.0), V.memset(Ei[:, :, 0:1], 0.0), cp(q_r, par["er"][:, gs]), cp(q_i, par["ei"][:, gs]))
                n = 1
                while n < NCH:
                    a, b_, d, e = (z[:, :, k:k + n] for z, k in ((t_a, 0), (t_b, 0), (t_a, n), (t_b, n)))
                    step(tt(a, Er[:, :, 0:n], over(q_r, n), ALU.mult), tt(b_, Ei[:, :, 0:n], over(q_i, n), ALU.mult),
                         tt(d, Er[:, :, 0:n], over(q_i, n), ALU.mult), tt(e, Ei[:, :, 0:n], over(q_r, n), ALU.mult))
                    step(tt(Er[:, :, n:2 * n], a, b_, ALU.subtract), tt(Ei[:, :, n:2 * n], d, e, ALU.add),
                         tt(par["t3"][:, 0:GB], q_r, q_r, ALU.mult), tt(par["t3"][:, GB:2 * GB], q_i, q_i, ALU.mult),
                         tt(par["t3"][:, 2 * GB:3 * GB], q_r, q_i, ALU.mult))
                    step(tt(q_r, par["t3"][:, 0:GB], par["t3"][:, GB:2 * GB], ALU.subtract),
                         ts_(q_i, par["t3"][:, 2 * GB:3 * GB], 2.0, None, ALU.mult))
                    n *= 2
                for q in range(2):
                    dve.wait_ge(sem("gb_full"), 2 * blk + q + 1)
                    src = ps_of(c)[:].rearrange("p (g m) -> p g m", m=P)
                    d = Gt[:, 4 * q:4 * q + 4, :]
                    step(cp(d[:, :, 0:P], src), cp(d[:, :, P:P + ST], src[:, :, ST:P]))
                    ts_(d[:, :, P + ST:2 * P], src[:, :, 0:ST], -1.0, None, ALU.mult).then_inc(sem("gt_done"), 1)
                    dve.wait_ge(sem("gt_done"), 2 * blk + q + 1)
                    free(V.engine_nop())
                    c.add("bank")
                for q in range(2):
                    dve.wait_ge(sem("kt_full"), 2 * blk + q + 1)
                    if q == 0 and blk:
                        dve.wait_ge(sem("tz_in"), 16 * L * blk)
                    src = ps_of(c)[0:CH, :].rearrange("p (g m) -> p g m", m=P)
                    g4 = slice(4 * q, 4 * q + 4)
                    step(cp(KTp[:, g4, ZPAD:], src))
                    step(tt(KTp[:, g4, ZPAD:ZPAD + CH], src[:, :, 0:CH], dsk[:, blk * GB + 4 * q:blk * GB + 4 * q + 4, :], ALU.add))
                    free(V.engine_nop())
                    c.add("bank")
                V.engine_nop().then_inc(sem("ktp_done"), 1)
                va = t_a[:, :, 0:NCH]
                vb = t_b[:, :, 0:NCH]
                dve.wait_ge(sem("x_full"), 2 * blk + 1)
                step(tt(va, ps_of(c)[:].rearrange("p (g n) -> p g n", n=NCH), Er[:], ALU.mult))
                c.add("bank")
                dve.wait_ge(sem("x_full"), 2 * blk + 2)
                step(tt(vb, ps_of(c)[:].rearrange("p (g n) -> p g n", n=NCH), Ei[:], ALU.mult))
                c.add("bank")
                free(tt(va, va, vb, ALU.add), 2)
                freed()
                step(*[V.tensor_tensor_scan(wst[:, g, :], par["r8"][:, blk * GB + g:blk * GB + g + 1].to_broadcast([P, NCH]), t_a[:, g, 0:NCH],
                                            0.0, ALU.mult, ALU.add) for g in range(GB)])
                step(tt(va, wst[:], Er[:], ALU.mult))
                tt(vb, wst[:], Ei[:], ALU.mult).then_inc(sem("st_done"), 1)
                dve.wait_ge(sem("y_mm"), blk + 1)
                cp(Y[:, gs, :], ps_of(c)[:].rearrange("p (g n) -> p g n", n=NCH)).then_inc(sem("y_done"), 1)
                dve.wait_ge(sem("y_done"), blk + 1)
                free(V.engine_nop())
                c.add("bank")
            for q in range(8):
                dve.wait_ge(sem("yn_full"), q + 1)
                src = ps_of(c)[0:NCH, :].rearrange("n (g i c) -> n g i c", g=4, i=L)
                dst = ynat[:].rearrange("n i (g c) -> n g i c", c=CH)
                for g in range(4):
                    ins = cp(dst[:, 4 * q + g, :, :], src[:, g, :, :])
                    if g < 3:
                        ins.then_inc(sem("dve_step"), 1)
                        c.add("step")
                dve.wait_ge(sem("dve_step"), c("step"))
                ins.then_inc(sem("yn_done"), 1)
                dve.wait_ge(sem("yn_done"), q + 1)
                free(V.engine_nop())
                c.add("bank")
            for ct in range(4):
                dve.wait_ge(sem("yt_full"), ct + 1)
                cp(yT[:, ct, :].rearrange("p (n i) -> p i n", i=L), ps_of(c)[:].rearrange("p (i n) -> p i n", n=NCH)).then_inc(sem("yt_done"), 1)
                dve.wait_ge(sem("yt_done"), ct + 1)
                free(V.engine_nop())
                c.add("bank")
                dve.wait_ge(sem("y_hi_done"), ct + 1)
                tt(y_lo[:, ct, :], yT[:, ct, :], y_hi[:, ct, :].bitcast(F32), ALU.subtract).then_inc(sem("y_lo_done"), 1)
            split()
            for m in range(4):
                full(m, 4)
                dve.wait_ge(sem("sg_done"), m + 1)
                if m >= 2:
                    dve.wait_ge(sem("mix_lo"), m - 1)
                free(tt(mx_t[:, m % 2, :], sg_t[:, m % 2, :], yT[:, m, :], ALU.mult))
                freed()
                tt(mx_t[:, m % 2, :], mx_t[:, m % 2, :], zs[:, m, :], ALU.mult).then_inc(sem("mx_done"), 1)
                dve.wait_ge(sem("mix_hi"), m + 1)
                tt(h_lo[:, 4 + m, :], mx_t[:, m % 2, :], h_hi[:, 4 + m, :].bitcast(F32), ALU.subtract).then_inc(sem("mix_lo"), 1)
            c.add("slab")
            for s in range(4):
                split()
                for m in range(2):
                    o = 2 * s + m
                    b = full(m)
                    stt(xT[:, o, :], b[:], mod[:, 112 + o:113 + o], xT[:, o, :], ALU.mult, ALU.add).then_inc(sem("x_final"), 1)
                    dve.wait_ge(sem("x_final"), o + 1)
                    free(V.engine_nop())
                c.add("slab")


def kernel(**inputs):
    import numpy as np
    import concourse.bacc as _bacc
    from concourse.bass_utils import run_bass_kernel_spmd as _run

    a = {k: np.asarray(v) for k, v in inputs.items()}
    f = lambda x: np.ascontiguousarray(x, dtype=np.float32)

    def natural(w):
        K, N = w.shape
        return w.reshape(K // 512, 4, 128, N // 512, 512).transpose(3, 0, 2, 1, 4).reshape(-1, 128, SLAB)

    def transposed(w):
        K, N = w.shape
        return w.reshape(8, 128, N // 256, 256).transpose(2, 1, 0, 3).reshape(-1, 128, SLAB)

    def down(w, parts):
        return [transposed(x) for x in np.split(w, parts, axis=0)]

    def ffn(l):
        up = np.split(transposed(a["ffn_w1"][l]), QUARTERS)
        return [x for pair in zip(up, down(a["ffn_w2"][l], QUARTERS)) for x in pair]

    b_in = a["b_w_in"][0]
    u_slabs = np.split(transposed(b_in[:, :SG_HALF]), CHUNKS)
    b_slabs = [x for pair in zip(u_slabs, down(a["b_w_out"][0], CHUNKS)) for x in pair]
    order = [g * 4 + i for i in range(4) for g in range(2)]
    w = a["w_in_2"][0]
    cols = np.cumsum([0, 512] + [128] * 6 + [512, 24, 512, 512])
    q, kcr, vcr, ksl, vsl, kwn, vwn, z_a, g_br, u, z_s = (w[:, cols[i]:cols[i + 1]] for i in range(11))
    heads = lambda m, n: m.reshape(m.shape[0], 8, n)[:, order].reshape(m.shape[0], 8 * n)
    w_out = a["w_out_2"][0]
    w_out = np.concatenate([w_out[:512].reshape(8, 64, D)[order].reshape(512, D), w_out[512:]])
    glu = a["glu_w_2"][0].reshape(4, 128, 512).transpose(1, 0, 2).reshape(1, 128, SLAB)
    slabs = np.concatenate([natural(a["a_w_in"][0]), transposed(a["a_w_out"][0])] + ffn(0)
                           + [natural(b_in[:, SG_HALF:])] + b_slabs + ffn(1)
                           + [natural(heads(q, 64)), natural(np.concatenate([ksl, kwn, vsl, vwn], 1)),
                              transposed(np.concatenate([kcr, vcr], 1)), transposed(heads(z_a, 64)), transposed(z_s), transposed(u)]
                           + down(a["cmp_w1_k_2"][0], 2) + down(a["cmp_w1_v_2"][0], 2) + [glu, transposed(w_out)])
    assert slabs.shape == (N_SLABS, 128, SLAB), slabs.shape

    col = lambda v: v.reshape(-1, 128).T
    ada = lambda m: m.T.reshape(-1, 128, D)
    A = {"slabs": slabs, "ada": np.concatenate([ada(a["ada_w"][0]), ada(a["ada_w"][1]), ada(a["w_ada_2"][0])]),
         "xT": a["x"][0].T.reshape(KT, 128, T).transpose(1, 0, 2), "ident": np.eye(128),
         "norm_g": np.stack([col(a["norm_mix"][0]), col(a["norm_ffn"][0]), col(a["norm_mix"][1]), col(a["norm_ffn"][1]),
                             col(a["norm_g_2"][0])], 1),
         "mod_b": np.concatenate([col(a["ada_b"][0]), col(a["ada_b"][1]), col(a["b_ada_2"][0])], 1),
         "aqk_g": np.stack([np.tile(a["a_q_gain"][0], 2), np.tile(a["a_k_gain"][0], 2)], 1),
         "bv_g": col(a["b_v_gain"][0]), "c": np.concatenate([a["c"], a["c_2"]])}
    p, y = np.arange(128)[:, None], np.arange(T)[None, :]
    bias = a["a_rel_bias"][0][:, np.clip(p - y + 384, -63, 256) + 63]
    bias[:, (p < 64) & (y >= 448)] = -BIG
    A["a_bias"] = bias
    A["b_ws"] = a["b_w_s"][0].transpose(2, 0, 1)
    A["b_bs"] = a["b_b_s"]
    t = np.arange(T)
    tiles = lambda m: m.reshape(TT, 128, -1).transpose(1, 0, 2)
    A["h_cmask"] = tiles(np.where(np.arange(CMP_PAD)[None, :] * 16 + 31 <= t[:, None], 0.0, -BIG))
    A["h_cmask"][:, :, CMP_N] = -BIG
    A["h_flag"] = tiles((t >= 31)[:, None])[:, :, 0]
    A["h_mask"] = np.where(y - 384 <= p, 0.0, -BIG)
    inv = 1.0 / (10000.0 ** (np.arange(0, HD, 2, dtype=np.float32) / HD))
    ang = (t[:, None].astype(np.float32) * inv[None, :].astype(np.float32)).astype(np.float32)
    A["cos"], A["sin"] = tiles(np.cos(ang)), tiles(np.sin(ang))
    rows = lambda v, n=128: np.broadcast_to(v, (n,) + v.shape)
    A["qg_b"] = rows(a["q_norm_g_2"][0])
    ks, kw = a["k_slc_norm_g_2"][0], a["k_win_norm_g_2"][0]
    A["kg_b"] = rows(np.stack([ks, ks, kw, kw]))
    A["kcg_b"] = rows(a["k_cmp_norm_g_2"][0], CMP_PAD)
    A["wg"] = heads(g_br, 3).reshape(KT, 128, 24).transpose(1, 0, 2)
    A["posT"] = np.tile(np.stack([a["cmp_pos_k_2"][0].T, a["cmp_pos_v_2"][0].T], 1), (2, 1, 1))
    A["w2c"] = np.stack([a[f"cmp_w2_{x}_2"][0].reshape(2, 128, 64).transpose(1, 0, 2) for x in "kv"], 1)
    A["glu_b"] = col(a["glu_b_2"][0])
    half = np.repeat([-1.0, 1.0], 64)
    A["sgn"] = np.stack([half, -half], 1)
    A["s5_ar"] = np.tile(a["ssm_a_re_2"][0].T, (2, 1))
    A["s5_ai"] = np.tile(a["ssm_a_im_2"][0].T, (2, 1))
    A["s5_dt"] = rows(a["ssm_log_dt_2"][0])
    b_re, b_im = (a[f"ssm_b_{x}_2"][0].transpose(1, 0, 2) for x in ("re", "im"))
    c_re, c_im = (a[f"ssm_c_{x}_2"][0].transpose(2, 0, 1) for x in ("re", "im"))
    A["Bo"], A["Bx"] = np.concatenate([b_re, b_im]), np.concatenate([b_im, b_re])
    A["Co"], A["Cx"] = np.concatenate([c_re, c_im]), np.concatenate([c_im, c_re])
    dsk = np.zeros((CH, G_ALL, CH), np.float32)
    dsk[np.arange(CH), :, np.arange(CH)] = a["ssm_d_2"][0].reshape(G_ALL, CH).T
    A["dsk"] = dsk

    nc = _bacc.Bacc("TRN2", target_bir_lowering=False, num_devices=1)
    arrays, I = {}, {}
    for name, v in A.items():
        v = f(v)
        arrays[f"in_{name}"] = v
        I[name] = nc.dram_tensor(f"in_{name}", v.shape, F32, kind="ExternalInput").ap()
    out = nc.dram_tensor("out_x", (128, KT, T), F32, kind="ExternalOutput").ap()
    program(nc, I, out)
    r = _run(nc, [arrays], core_ids=[0])
    y = np.asarray(r.results[0]["out_x"])
    return np.ascontiguousarray(y.transpose(1, 0, 2).reshape(D, T).T).reshape(1, T, D)
```

```python
import concourse.bass as bass
from concourse import mybir
from concourse.alu_op_type import AluOpType as ALU
from contextlib import ExitStack
import math

F32 = mybir.dt.float32
F32R = mybir.dt.float32r
ACT = mybir.ActivationFunctionType
AX = mybir.AxisListType

P = 128
T = 512
D = 1024
KT = D // P
TT = T // P
SLAB = 2048
BIG = 1e30
EPS = 1e-6

N_QKV = 12
N_AOUT = 4
N_FFN = 32
N_BV = 12
N_BUO = 24
QUARTERS = 4
CHUNKS = 3
S_QKV = 0
S_AOUT = S_QKV + N_QKV
S_FFN0 = S_AOUT + N_AOUT
S_BV = S_FFN0 + N_FFN
S_BUO = S_BV + N_BV
S_FFN1 = S_BUO + N_BUO
S_HQ = S_FFN1 + N_FFN
S_HKV = S_HQ + 2
S_HCR = S_HKV + 2
S_HCK = S_HCR + 2
S_HCV = S_HCK + 3
S_HU = S_HCV + 4
S_HGLU = S_HU + 2
S_HOUT = S_HGLU + 1
N_SLABS = S_HOUT + 4
ADA_TILES = 48
ADA2_TILES = 24
N_ADA = 2 * ADA_TILES + ADA2_TILES
ADA_FIRST = 12

ADA_QKV = 16

A_HEADS, HD = 16, 64
SG_HALF, SG_GROUPS = 3072, 8
H_HEADS, H_GROUPS, N_BR = 8, 2, 3
CMP_N, CMP_PAD = 31, 32
G_ALL, CH, ST, L = 32, 16, 64, 8
NCH = T // L
GB = 8
NBLK = G_ALL // GB
TAPS = L + 1
ZPAD = (L - 1) * CH


def program(nc, I, out):
    ctx = ExitStack()
    with ctx:
        sems = {}

        def sem(name):
            if name not in sems:
                sems[name] = ctx.enter_context(nc.semaphore(name))
            return sems[name]

        def sb(name, shape, dt=F32):
            return ctx.enter_context(nc.sbuf_tensor(name, shape, dt))

        ARENA = nc.sbuf_base + 31 & ~31
        placed = [0]

        def at(name, offset, shape, dt=F32):
            size = 4 * math.prod(shape[1:])
            assert ARENA + offset + size <= nc.sbuf_usable_end, (name, offset, size)
            return nc.alloc_sbuf_tensor_at(name, shape, dt, offset=ARENA + offset)

        def seq(name, shape, dt=F32):
            o = placed[0]
            placed[0] += 4 * math.prod(shape[1:]) + 31 & ~31
            return at(name, o, shape, dt)

        K = 1024
        placed[0] = 109 * K
        xT = seq("xT", [P, KT, T])
        h_hi = seq("h_hi", [P, KT, T], F32R)
        h_lo = seq("h_lo", [P, KT, T], F32R)
        w_raw = seq("w_raw", [P, 2, SLAB])
        w_hi = seq("w_hi", [P, SLAB], F32R), seq("w_hi1", [P, SLAB], F32R)
        w_lo = seq("w_lo", [P, SLAB], F32R), seq("w_lo1", [P, SLAB], F32R)
        mod = seq("mod", [P, N_ADA])
        mod_b = seq("mod_b", [P, N_ADA])
        mod_s = seq("mod_s", [P, 16])
        norm_g = seq("norm_g", [P, 5, KT])
        mod_a = seq("mod_a", [P, KT])
        ident = seq("ident", [P, P])
        ones = seq("ones", [P, P])
        eps = seq("eps", [P, 1])
        rstd = seq("rstd", [P, 32])
        stat = seq("stat", [P, 32])
        aqk_g = seq("aqk_g", [P, 2])
        bv_g = seq("bv_g", [P, SG_HALF // P])
        neg_max = seq("neg_max", [P, 8])
        row_sum = seq("row_sum", [P, 8])
        row_inv = seq("row_inv", [P, 8])
        vss = seq("vss", [P, TT, 6])
        ada_raw = at("ada_raw", 93 * K, [P, 2, D])
        cond = at("cond", 101 * K, [P, 2, D])
        ada_first = at("ada_first", 44 * K, [P, ADA_FIRST, D])
        sq_x = at("sq_x", 40 * K, [P, 2, T])
        diag = at("diag", 16 * K, [P, TT, P])
        pre = at("pre", 18 * K, [P, KT, T])
        hid_hi = at("hid_hi", 0, [P, KT, T], F32R)
        hid_lo = at("hid_lo", 16 * K, [P, KT, T], F32R)
        relu = at("relu", 32 * K, [P, 2, T])
        relu2 = at("relu2", 36 * K, [P, 2, T])
        a_qT = at("a_qT", 0, [P, A_HEADS // 2, T])
        a_kT = at("a_kT", 16 * K, [P, A_HEADS // 2, T])
        a_v = at("a_v", 32 * K, [P, TT, D])
        a_qn = at("a_qn", 48 * K, [P, 2, TT, 512])
        a_sq = at("a_sq", 64 * K, [P, TT, 512])
        a_o = at("a_o", 76 * K, [P, TT, D])
        a_bias = at("a_bias", 48 * K, [P, 3, T])
        a_s = at("a_s", 54 * K, [P, 3, T])
        a_p = at("a_p", 60 * K, [P, 4, T])
        a_pt = at("a_pt", 68 * K, [P, 3, T])
        b_v = at("b_v", 0, [P, TT, SG_HALF])
        g_hi = at("g_hi", 48 * K, [P, KT, T], F32R)
        g_lo = at("g_lo", 64 * K, [P, KT, T], F32R)
        b_ws = at("b_ws", 80 * K, [P, SG_GROUPS, P])
        b_bs = at("b_bs", 84 * K, [P, SG_GROUPS, P])
        b_u = at("b_u", 88 * K, [P, T])
        b_vm = at("b_vm", 90 * K, [P, T])
        za = at("za", 0, [P, 4, T])
        zs = at("zs", 8 * K, [P, 4, T])
        uT = at("uT", 16 * K, [P, 4, T])
        hq = at("hq", 24 * K, [P, 4, T])
        hqr = at("hqr", 32 * K, [P, 4, T])
        hk = at("hk", 40 * K, [P, 2, T])
        hv = at("hv", 44 * K, [P, TT, 256])
        h_p = at("h_p", 48 * K, [P, 4, T])
        h_pt = at("h_pt", 56 * K, [P, 3, T])
        h_s = at("h_s", 62 * K, [P, 3, T])
        h_o = at("h_o", 72 * K, [P, TT, 512])
        h_qn = at("h_qn", 48 * K, [P, TT, 512])
        h_sq = at("h_sq", 56 * K, [P, TT, 512])
        h_qr = at("h_qr", 56 * K, [P, TT, 512])
        h_kn = at("h_kn", 64 * K, [P, TT, 256])
        h_kr = at("h_kr", 68 * K, [P, TT, 256])
        h_t1 = at("h_t1", 72 * K, [P, TT, 8, 32])
        h_t2 = at("h_t2", 76 * K, [P, TT, 8, 32])
        crT = at("crT", 72 * K, [P, 2, T])
        bl_hi = at("bl_hi", 76 * K, [P, 16, 2 * CMP_PAD], F32R)
        bl_lo = at("bl_lo", 80 * K, [P, 16, 2 * CMP_PAD], F32R)
        bl = at("bl", 84 * K, [P, 16, 2 * CMP_PAD])
        h_mask = at("h_mask", 88 * K, [P, T])
        placed[0] = 93 * K
        h_cmask = seq("h_cmask", [P, TT, CMP_PAD])
        h_gts = seq("h_gts", [P, TT, N_BR * H_HEADS])
        h_flag = seq("h_flag", [P, TT])
        kcT = seq("kcT", [P, CMP_PAD])
        vc = seq("vc", [CMP_PAD, H_GROUPS, HD])
        wbr = seq("wbr", [P, 4])
        cos = seq("cos", [P, TT, 32])
        sin = seq("sin", [P, TT, 32])
        qg_b = seq("qg_b", [P, HD])
        kg_b = seq("kg_b", [P, 4, HD])
        wg = seq("wg", [P, KT, 24])
        wg_hi = seq("wg_hi", [P, KT, 24], F32R)
        wg_lo = seq("wg_lo", [P, KT, 24], F32R)
        posT = seq("posT", [P, 2, 32])
        w2c = seq("w2c", [P, 2, 2, HD])
        hdn = seq("hdn", [P, 2, 2, 2 * CMP_PAD])
        kcn = seq("kcn", [CMP_PAD, H_GROUPS, HD])
        kcsq = seq("kcsq", [CMP_PAD, H_GROUPS, HD])
        kcg_b = seq("kcg_b", [CMP_PAD, HD])
        kst = seq("kst", [CMP_PAD, 4])
        PAR = ["ar", "ai", "dt", "xr", "th", "kk", "r1", "sn", "cs", "h2", "nr", "d2", "fr", "fs",
               "t1", "t2", "t3", "r8", "er", "ei"]
        par = {x: seq("s5_" + x, [P, G_ALL]) for x in PAR}
        Lr = seq("Lr", [P, TAPS, G_ALL])
        Ls = seq("Ls", [P, TAPS, G_ALL])
        LrR = at("LrR", 89 * K, [P, L, G_ALL])
        LsR = at("LsR", 92 * K, [P, L, G_ALL])
        glu_b = seq("glu_b", [P, 4])
        sgn = seq("sgn", [P, 2])
        assert placed[0] <= 109 * K, placed
        U = at("U", 24 * K, [NCH, G_ALL, L * CH])
        UT = at("UT", 40 * K, [P, G_ALL, NCH])
        Y = at("Y", 48 * K, [P, G_ALL, NCH])
        placed[0] = 24 * K
        t_a = seq("t_a", [P, GB, TAPS * CH])
        t_b = seq("t_b", [P, GB, TAPS * CH])
        Gb = seq("Gb", [P, GB, L * CH])
        wst = seq("wst", [P, GB, NCH])
        bbo = seq("bbo", [P, GB, CH])
        bbx = seq("bbx", [P, GB, CH])
        assert placed[0] <= 40 * K
        placed[0] = 56 * K
        Hc = seq("Hc", [P, GB, TAPS * CH])
        Hs = seq("Hs", [P, GB, TAPS * CH])
        Gt = seq("Gt", [P, GB, 2 * P])
        Tz = seq("Tz", [P, GB, L * CH])
        Er = seq("Er", [P, GB, NCH])
        Ei = seq("Ei", [P, GB, NCH])
        KTp = seq("KTp", [CH, GB, ZPAD + L * CH])
        assert placed[0] <= 89 * K, placed
        placed[0] = 0
        Bo = seq("Bo", [P, G_ALL, CH])
        Bx = seq("Bx", [P, G_ALL, CH])
        Co = seq("Co", [P, G_ALL, CH])
        Cx = seq("Cx", [P, G_ALL, CH])
        dsk = at("dsk", 90 * K, [CH, G_ALL, CH])
        ynat = at("ynat", 56 * K, [NCH, L, T])
        yT = at("yT", 72 * K, [P, 4, T])
        y_hi = at("y_hi", 80 * K, [P, 4, T], F32R)
        y_lo = at("y_lo", 32 * K, [P, 4, T], F32R)
        sg_t = at("sg_t", 24 * K, [P, 2, T])
        mx_t = at("mx_t", 28 * K, [P, 2, T])

        ps = [ctx.enter_context(nc.psum_tensor(f"ps{b}", [P, 512], F32)) for b in range(8)]
        block = ctx.enter_context(nc.Block())

        class Count:

            def __init__(self):
                self.at, self.turn, self.reg = {}, {}, None

            def __call__(self, name, more=0):
                n = self.at.get(name, 0) + more
                return n if self.reg is None or not self.turn.get(name) else self.reg * self.turn[name] + n

            def add(self, name, n=1):
                self.at[name] = self.at.get(name, 0) + n
                return self(name)

            def base(self, name):
                return self.at.get(name, 0)

            def loop(self, eng, turns, turn):
                self.turn, before = turn, dict(self.at)
                with eng.Fori(0, turns) as reg:
                    self.reg = reg
                    yield reg
                for name, n in self.at.items():
                    assert n - before.get(name, 0) == turn.get(name, 0), (name, n - before.get(name, 0), turn.get(name, 0))
                    self.at[name] = before.get(name, 0) + turns * turn.get(name, 0)
                self.reg, self.turn = None, {}

        def ps_of(c):
            return ps[c.base("bank") % 8]

        def wait(eng, name, value):
            if not isinstance(value, int) or value > 0:
                eng.wait_ge(sem(name), value)

        A_WALK = [("p", 0), ("p", 1), ("x", 0), ("p", 2), ("x", 1), ("p", 3), ("x", 2), ("v", 0), ("x", 3)]
        UNITS_A = [(h, it) for h in range(A_HEADS) for it in range(TT)]
        UNITS_H = [(i, g, it, br) for i in range(4) for g in range(H_GROUPS) for it in range(TT) for br in range(N_BR)]
        NUA, NUH = len(UNITS_A), len(UNITS_H)

        class Side:

            def __init__(self, per, uses):
                self.per, self.uses, self.steps = per, uses, -(-KT // per) + 1

            def tiles(self, s):
                u, r = divmod(s, self.steps)
                return (u, range(r * self.per, min(KT, (r + 1) * self.per))) if u < 2 * self.uses else (0, ())

            def copy(self, s):
                u, r = divmod(s, self.steps)
                return u if r == self.steps - 1 and u < 2 * self.uses else None

            def slab(self, s):
                return s % (self.uses * self.steps) == 0 and s < 2 * self.uses * self.steps

        SIDE_A, SIDE_H = Side(3, TT), Side(2, 2)

        @block.sync
        def _(sp):
            for name, tile in (("xT", xT), ("ident", ident), ("norm_g", norm_g), ("mod_b", mod_b), ("aqk_g", aqk_g), ("bv_g", bv_g)):
                sp.dma_start(tile[:], I[name]).then_inc(sem("consts_in"), 16)
            q = ADA_FIRST // 4
            for i in range(4):
                sp.dma_start(ada_first[:, q * i:q * (i + 1), :], I["ada"][q * i:q * (i + 1)].rearrange("k p d -> p k d"))\
                  .then_inc(sem(f"first_in{i}"), 16)
            for s in range(2):
                sp.dma_start(w_raw[:, s, :], I["slabs"][s]).then_inc(sem(f"raw_in{s}"), 16)
            with sp.Fori(1, N_SLABS // 2) as i:
                for s in range(2):
                    sp.wait_ge(sem("lo_done"), i * 2 + (s - 1))
                    sp.dma_start(w_raw[:, s, :], I["slabs"][i * 2 + s]).then_inc(sem(f"raw_in{s}"), 16)
            for m in range(KT):
                sp.wait_ge(sem("x_final"), m + 1)
                sp.dma_start(out[:, m, :], xT[:, m, :]).then_inc(sem("stored"), 16)
            sp.wait_ge(sem("stored"), 16 * KT)

        @block.gpsimd
        def _(gp):
            for s in range(2):
                gp.dma_start(cond[:, s, :], I["c"][s:s + 1, :].to_broadcast([P, D])).then_inc(sem("c_in"), 16)
            gp.memset(ones[:], 1.0).then_inc(sem("ones_set"), 1)
            gp.memset(eps[:], EPS).then_inc(sem("ones_set"), 1)

            def ada(k0, k1):
                for k in range(k0, k1):
                    if k >= ADA_FIRST + 2:
                        gp.wait_ge(sem("ada_used"), k - 1)
                    gp.dma_start(ada_raw[:, k % 2, :], I["ada"][k]).then_inc(sem(f"ada_in{k % 2}"), 16)

            ada(ADA_FIRST, 16 + ADA_QKV)
            gp.wait_ge(sem("acc_free"), 2 + 4 * len(A_WALK))
            for h in range(A_HEADS + 2):
                if h < A_HEADS:
                    if h >= 3:
                        gp.wait_ge(sem("s_done"), TT * (h - 2))
                    gp.dma_start(a_bias[:, h % 3, :], I["a_bias"][h]).then_inc(sem(f"bias_in{h % 3}"), 16)
                if h >= 2:
                    ada(16 + ADA_QKV + h - 2, 16 + ADA_QKV + h - 1)
            with gp.Fori(0, ADA_TILES // 2) as i:
                for s in range(2):
                    gp.wait_ge(sem("ada_used"), i * 2 + (ADA_TILES + s - 1))
                    gp.dma_start(ada_raw[:, s, :], I["ada"][i * 2 + (ADA_TILES + s)]).then_inc(sem(f"ada_in{s}"), 16)
            gp.wait_ge(sem("slab_used"), S_BV)
            gp.dma_start(b_ws[:], I["b_ws"]).then_inc(sem("bws_in"), 16)
            gp.dma_start(b_bs[:], I["b_bs"][0:1].to_broadcast([P, SG_GROUPS, P])).then_inc(sem("bws_in"), 16)
            with gp.Fori(0, ADA2_TILES // 2) as i:
                for s in range(2):
                    gp.wait_ge(sem("ada_used"), i * 2 + (2 * ADA_TILES + s - 1))
                    gp.dma_start(ada_raw[:, s, :], I["ada"][i * 2 + (2 * ADA_TILES + s)]).then_inc(sem(f"ada_in{s}"), 16)
            gp.wait_ge(sem("ada_used"), N_ADA)

            small = [("h_cmask", h_cmask), ("h_flag", h_flag), ("cos", cos), ("sin", sin), ("qg_b", qg_b), ("kg_b", kg_b),
                     ("wg", wg), ("posT", posT), ("w2c", w2c), ("kcg_b", kcg_b), ("h_mask", h_mask), ("glu_b", glu_b),
                     ("sgn", sgn), ("s5_ar", par["ar"]), ("s5_ai", par["ai"]), ("s5_dt", par["dt"]), ("dsk", dsk)]
            for name, tile in small:
                gp.dma_start(tile[:], I[name]).then_inc(sem("h_in"), 16)
            gp.wait_ge(sem("hx_done"), 4)
            for name, tile in (("Bo", Bo), ("Bx", Bx), ("Co", Co), ("Cx", Cx)):
                gp.dma_start(tile[:], I[name]).then_inc(sem("s5_in"), 16)
            for b in range(NBLK):
                gp.wait_ge(sem("ktp_done"), b + 1)
                if b:
                    gp.wait_ge(sem("y_mm"), b)
                for j in range(L):
                    gp.dma_start(Tz[CH * j:CH * (j + 1), :, :], KTp[:, :, ZPAD - CH * j:ZPAD - CH * j + L * CH])\
                      .then_inc(sem("tz_in"), 16)

        @block.tensor
        def _(pe):
            c = Count()
            mm = nc.tensor.matmul

            def bank(full=False):
                wait(pe, "acc_free", c("bank", -7))
                b = ps_of(c)
                c.add("bank")
                return b

            def three(o, w, x, start, stop, weights_move=False):
                for n, (a, b) in enumerate(((0, 0), (0, 1), (1, 0))):
                    l, r = (x[a], w[b]) if weights_move else (w[a], x[b])
                    last = mm(o, l, r, start=start and n == 0, stop=stop and n == 2)
                return last

            def slab_t(x, nk=KT, tiles=2, ready=None, first=True, final=True, after=None, banks=None, n=T):
                s = c.base("slab") % 2
                wait(pe, "lo_done", c("slab", 1))
                for m in range(tiles):
                    b = banks[m] if banks else bank()
                    for k in range(nk):
                        if ready and m == 0:
                            pe.wait_ge(sem(ready[0]), c(ready[1], k + 1))
                        if x is H and c.reg is None:
                            h_ready(k)
                        cols = slice((k * tiles + m) * P, (k * tiles + m + 1) * P)
                        last = three(b[:, 0:n], (w_hi[s][:, cols], w_lo[s][:, cols]), (x[0](k), x[1](k)),
                                     first and k == 0, final and k == nk - 1)
                    last.then_inc(sem("slab_used" if m == tiles - 1 else "acc_full"), 1)
                    if after:
                        after(m)
                if ready:
                    c.add(ready[1], nk)
                c.add("slab")

            def tile_of(hi, lo):
                return (lambda k: hi[:, k, :]), (lambda k: lo[:, k, :])

            H = tile_of(h_hi, h_lo)

            def panel_natural():
                bs = [bank() for _ in range(TT)]
                for half in range(2):
                    s = c.base("slab") % 2
                    wait(pe, "lo_done", c("slab", 1))
                    for t in range(TT):
                        ts = slice(t * P, (t + 1) * P)
                        for kk in range(4):
                            k, cols = 4 * half + kk, slice(kk * 512, (kk + 1) * 512)
                            h_ready(k)
                            last = three(bs[t][:], (w_hi[s][:, cols], w_lo[s][:, cols]), (h_hi[:, k, ts], h_lo[:, k, ts]),
                                         k == 0, k == KT - 1, weights_move=True)
                        if t == TT - 1:
                            last.then_inc(sem("slab_used"), 1)
                        elif half:
                            last.then_inc(sem("acc_full"), 1)
                    c.add("slab")

            def sums(k):
                if k == 0:
                    c.add("norm")
                    norm_bank[0] = bank()
                pe.wait_ge(sem("nsq"), KT * (c.base("norm") - 1) + k + 1)
                for t in range(TT):
                    last = mm(norm_bank[0][:, t:t + 1], sq_x[:, k % 2, t * P:(t + 1) * P], ones[:, 0:1], start=k == 0 and t == 0,
                              stop=k == KT - 1, skip_group_check=True)
                last.then_inc(sem("nsum"), 1)

            norm_bank = [None]

            def spread():
                pe.wait_ge(sem("ndiag"), TT * c("norm"))
                b = bank()
                for t in range(TT):
                    last = mm(b[:, t * P:(t + 1) * P], ones[:], diag[:, t, :], start=True, stop=True)
                last.then_inc(sem("nbc"), 1)
                h_base[0] = KT * (c.base("norm") - 1)
                h_seen[0] = 0

            h_base, h_seen = [0], [0]

            def h_ready(k):
                if h_seen[0] <= k:
                    pe.wait_ge(sem("nlo"), h_base[0] + k + 1)
                    h_seen[0] = k + 1

            def down_and_sums(x, ready=None):
                for s in range(4):
                    def after(m, s=s):
                        if 2 * s + m >= 2:
                            sums(2 * s + m - 2)
                    slab_t(x, ready=ready if s == 0 else None, after=after)
                sums(KT - 2)
                sums(KT - 1)
                spread()

            def transposes(src, signal, parts=P):
                b, col = bank(), 0
                for a in src:
                    w = a.shape[0]
                    last = nc.tensor.transpose(b[0:a.shape[-1], col:col + w], a, ident[0:w, 0:w])
                    col += w
                last.then_inc(sem(signal), 1)

            def attention(units, score, value, pre, extra=lambda s: None):
                U = len(units)
                for s in range(U + 4):
                    if s < U:
                        if s >= 3:
                            pe.wait_ge(sem(pre + "s_done"), s - 2)
                        q, k, n = score(units[s])
                        mm(ps[s % 3][:, 0:n], q, k, start=True, stop=True).then_inc(sem(pre + "s_full"), 1)
                    u = s - 3
                    if 0 <= u < U:
                        pe.wait_ge(sem(pre + "p_ready"), u + 1)
                        if u >= 2:
                            pe.wait_ge(sem(pre + "pt_ready"), u - 1)
                        n = score(units[u])[2]
                        b, pt = ps[3 + u % 2], (a_p if pre == "" else h_p)
                        for j in range(0, n, P):
                            w = min(P, n)
                            last = nc.tensor.transpose(b[0:w, j:j + P], pt[:, u % 4, j:j + w], ident[:])
                        last.then_inc(sem(pre + "t_full"), 1)
                    u = s - 4
                    if 0 <= u < U:
                        pe.wait_ge(sem(pre + "pt_ready"), u + 1)
                        if u >= 2:
                            pe.wait_ge(sem(pre + "o_done"), u - 1)
                        n = score(units[u])[2]
                        pt, nb = (a_pt if pre == "" else h_pt), max(1, n // P)
                        for j in range(nb):
                            w = min(P, n)
                            last = mm(ps[5 + u % 2][:, 0:HD], pt[0:w, u % 3, j * P:(j + 1) * P], value(units[u], j), start=j == 0, stop=j == nb - 1)
                        last.then_inc(sem(pre + "o_full"), 1)
                    extra(s)

            def side(plan, s, pair, base=[0]):
                u, ks = plan.tiles(s)
                sl = c.base("slab") % 2
                if plan.slab(s):
                    wait(pe, "lo_done", c("slab", 1))
                for k in ks:
                    if k == 0:
                        wait(pe, "side_free", base[0])
                        base[0] += 1
                    o, w, x, move = pair(u, k, sl)
                    last = three(o, w, x, k == 0, k == KT - 1, weights_move=move)
                    if k == KT - 1:
                        last.then_inc(sem("slab_used" if u % plan.uses == plan.uses - 1 else "acc_full"), 1)
                        if u % plan.uses == plan.uses - 1:
                            c.add("slab")

            def ffn(norm_next=True):
                turn, hid = dict(slab=8, bank=16, hid=KT), tile_of(hid_hi, hid_lo)
                for _ in range(4):
                    slab_t(H)
                for s in range(4):
                    slab_t(hid, ready=("hid_lo_done", "hid") if s == 0 else None)
                for _ in c.loop(pe, QUARTERS - 2, turn):
                    for _ in range(4):
                        slab_t(H)
                    for s in range(4):
                        slab_t(hid, ready=("hid_lo_done", "hid") if s == 0 else None)
                for _ in range(4):
                    slab_t(H)
                down_and_sums(hid, ready=("hid_lo_done", "hid"))

            pe.wait_ge(sem("consts_in"), 96)
            pe.wait_ge(sem("ones_set"), 2)
            for k in range(KT):
                sums(k)
            spread()
            for kind, p in A_WALK:
                if kind != "x":
                    panel_natural()
                else:
                    pe.wait_ge(sem("qn_done"), p + 1)
                    for b in range(4):
                        transposes([a_qn[:, p % 2, t, b * P:(b + 1) * P] for t in range(TT)], "xp_full")
            pe.wait_ge(sem("acc_free"), c("bank"))

            def score_a(u):
                h, it = u
                r = slice(HD * (h % 2), HD * (h % 2) + HD)
                return a_qT[r, h // 2, it * P:(it + 1) * P], a_kT[r, h // 2, 0:P * (it + 1)], P * (it + 1)

            def value_a(u, j):
                if u == (8, 0):
                    pe.wait_ge(sem("side_free"), 2 * TT)
                return a_v[:, j, u[0] * HD:(u[0] + 1) * HD]

            def pair_a(u, k, sl):
                t, cols = u % TT, slice(k * 256, (k + 1) * 256)
                return (ps[7][:, 0:256], (w_hi[sl][:, cols], w_lo[sl][:, cols]),
                        (h_hi[:, k, t * P:(t + 1) * P], h_lo[:, k, t * P:(t + 1) * P]), True)

            attention(UNITS_A, score_a, value_a, "", lambda s: side(SIDE_A, s, pair_a))
            pe.wait_ge(sem("o_done"), NUA)
            for i in range(KT):
                transposes([a_o[:, t, i * P:(i + 1) * P] for t in range(TT)], "xo_full")
            pe.wait_ge(sem("xo_lo"), KT)
            down_and_sums(H)
            ffn()

            for _ in range(6):
                panel_natural()
            pe.wait_ge(sem("bws_masked"), 1)
            for ch in range(CHUNKS):
                for s in range(4):
                    def mix(m):
                        gm = KT * ch + 2 * s + m
                        if gm == 0:
                            pe.wait_ge(sem("bv_scaled"), TT)
                        b = bank()
                        for t in range(TT):
                            last = mm(b[:, t * P:(t + 1) * P], b_v[:, t, gm * P:(gm + 1) * P], b_ws[:, gm // 3, :], start=True, stop=True)
                        last.then_inc(sem("mix_full"), 1)
                    slab_t(H, after=mix)
                if ch < CHUNKS - 1:
                    for s in range(4):
                        slab_t(tile_of(g_hi, g_lo), ready=("g_lo_done", "g") if s == 0 else None)
                else:
                    down_and_sums(tile_of(g_hi, g_lo), ready=("g_lo_done", "g"))
            ffn()

            panel_natural()
            panel_natural()
            pe.wait_ge(sem("wg_split"), 1)
            b = bank()
            for t in range(TT):
                for k in range(KT):
                    last = three(b[:, t * 24:(t + 1) * 24], (wg_hi[:, k, :], wg_lo[:, k, :]),
                                 (h_hi[:, k, t * P:(t + 1) * P], h_lo[:, k, t * P:(t + 1) * P]), k == 0, k == KT - 1, weights_move=True)
            last.then_inc(sem("gates_full"), 1)
            slab_t(H)
            slab_t(H)
            pe.wait_ge(sem("hq_done"), 1)
            for i in range(4):
                transposes([h_qn[:, t, i * P:(i + 1) * P] for t in range(TT)], "hx_full")
            for i in range(4):
                transposes([h_qr[:, t, i * P:(i + 1) * P] for t in range(TT)], "hx_full")
            pe.wait_ge(sem("hk_done"), 1)
            for i in range(2):
                transposes([h_kr[:, t, i * P:(i + 1) * P] for t in range(TT)], "hx_full")
            for kind in range(2):
                pe.wait_ge(sem("bl_done"), kind + 1)
                bs = [bank(), bank()]
                for s in range(2):
                    x = (lambda k, s=s: bl_hi[:, 8 * s + k, :]), (lambda k, s=s: bl_lo[:, 8 * s + k, :])
                    slab_t(x, banks=bs, first=s == 0, final=s == 1, n=2 * CMP_PAD)
                slab_t(H)
            pe.wait_ge(sem("hdn_done"), 2)
            b = bank()
            for kind in range(2):
                for g in range(H_GROUPS):
                    for m in range(2):
                        col = (kind * 2 + g) * HD
                        last = mm(b[0:CMP_PAD, col:col + HD], hdn[:, kind, m, g * CMP_PAD:(g + 1) * CMP_PAD], w2c[:, kind, m, :],
                                  start=m == 0, stop=m == 1)
            last.then_inc(sem("kc_full"), 1)
            slab_t(H)
            pe.wait_ge(sem("kcn_done"), 1)
            transposes([kcn[:].rearrange("n g d -> n (g d)")], "kct_full")
            pe.wait_ge(sem("acc_free"), c("bank"))

            def score_h(u):
                i, g, it, br = u
                r, ts = slice(HD * g, HD * g + HD), slice(it * P, (it + 1) * P)
                if br == 0:
                    return hq[r, i, ts], kcT[r, :], CMP_PAD
                return hqr[r, i, ts], hk[r, br - 1, 0:P * (it + 1)], P * (it + 1)

            def value_h(u, j):
                i, g, it, br = u
                return vc[:, g, :] if br == 0 else hv[:, j, (br - 1) * P + g * HD:(br - 1) * P + (g + 1) * HD]

            def pair_h(u, k, sl):
                cols = slice((2 * k + u % 2) * P, (2 * k + u % 2 + 1) * P)
                return ps[7][:], (w_hi[sl][:, cols], w_lo[sl][:, cols]), (h_hi[:, k, :], h_lo[:, k, :]), False

            attention(UNITS_H, score_h, value_h, "h", lambda s: side(SIDE_H, s, pair_h))
            pe.wait_ge(sem("ho_done"), NUH)
            for i in range(4):
                transposes([h_o[:, t, i * P:(i + 1) * P] for t in range(TT)], "hxo_full")

            pe.wait_ge(sem("hx_done"), 4)
            for ct in range(4):
                for jj in range(2):
                    transposes([uT[:, ct, :].rearrange("p (n j) -> p j n", j=L)[:, 4 * jj + j, :] for j in range(4)], "u_full")
            pe.wait_ge(sem("u_done"), 8)
            for q in range(4):
                transposes([U[:, 8 * q + g, :] for g in range(8)], "ut_full")
            pe.wait_ge(sem("ut_done"), 4)
            for blk in range(NBLK):
                pe.wait_ge(sem("gb_done"), blk + 1)
                for q in range(2):
                    transposes([Gb[:, 4 * q + g, :] for g in range(4)], "gb_full")
                pe.wait_ge(sem("hc_done"), blk + 1)
                for q in range(2):
                    b = bank()
                    for g in range(4):
                        last = mm(b[0:CH, g * P:(g + 1) * P], bbo[:, 4 * q + g, :], Hc[:, 4 * q + g, 0:L * CH], start=True, stop=True)
                    last.then_inc(sem("kt_full"), 1)
                pe.wait_ge(sem("gt_done"), 2 * (blk + 1))
                for q in range(2):
                    b = bank()
                    for g in range(GB):
                        last = mm(b[:, g * NCH:(g + 1) * NCH], Gt[:, g, q * P:(q + 1) * P], UT[:, blk * GB + g, :], start=True, stop=True)
                    last.then_inc(sem("x_full"), 1)
                pe.wait_ge(sem("tz_in"), 16 * L * (blk + 1))
                pe.wait_ge(sem("st_done"), blk + 1)
                b = bank()
                for g in range(GB):
                    o, o1 = b[:, g * NCH:(g + 1) * NCH], b[:, g * NCH + 1:(g + 1) * NCH]
                    mm(o, Tz[:, g, :], UT[:, blk * GB + g, :], start=True, stop=False)
                    mm(o1, Hc[:, g, CH:], t_a[:, g, 0:NCH - 1], start=False, stop=False)
                    last = mm(o1, Hs[:, g, CH:], t_b[:, g, 0:NCH - 1], start=False, stop=True)
                last.then_inc(sem("y_mm"), 1)
            pe.wait_ge(sem("y_done"), NBLK)
            for q in range(8):
                transposes([Y[:, 4 * q + g, :] for g in range(4)], "yn_full")
            pe.wait_ge(sem("yn_gelu"), 1)
            for ct in range(4):
                transposes([ynat[:, i, ct * P:(ct + 1) * P] for i in range(L)], "yt_full")
            pe.wait_ge(sem("y_lo_done"), 4)
            slab_t(tile_of(y_hi, y_lo), nk=4, tiles=4)
            pe.wait_ge(sem("mix_lo"), 4)
            pe.wait_ge(sem("hx_done"), 4)
            for _ in range(4):
                slab_t(H)

        @block.scalar
        def _(act):
            c = Count()
            A = nc.scalar.activation

            def split():
                n = c.base("split")
                if c.reg is None and n >= N_SLABS:
                    return
                s = n % 2
                act.wait_ge(sem(f"raw_in{s}"), (c("split", -s) if c.reg is None else c("split", -s)) * 8 + 16)
                wait(act, "slab_used", c("split", -1))
                A(w_hi[s][:], w_raw[:, s, :], ACT.Copy).then_inc(sem("hi_done"), 1)
                c.add("split")

            def full(m, tiles=2):
                if m == tiles - 1:
                    act.wait_ge(sem("slab_used"), c("slab", 1))
                else:
                    act.wait_ge(sem("acc_full"), c.add("full"))
                b = ps_of(c)
                c.add("bank")
                return b

            def skip_t(tiles=2):
                split()
                c.add("full", tiles - 1)
                c.add("bank", tiles)
                c.add("slab")

            def natural(use):
                split()
                c.add("slab")
                split()
                for t in range(TT):
                    use(t, full(t, TT)) if use else (c.add("bank"), c.add("full", t < TT - 1))
                c.add("slab")

            def square(k, frees):
                if k == 0:
                    c.add("norm")
                wait(act, "acc_free", frees)
                n = KT * (c.base("norm") - 1) + k
                if n >= 2:
                    act.wait_ge(sem("nsum"), n - 1)
                A(sq_x[:, k % 2, :], xT[:, k, :], ACT.Square).then_inc(sem("nsq"), 1)

            def down_and_squares():
                frees = c.base("bank")
                for s in range(4):
                    split()
                    square(2 * s, frees + 2 * s + 1)
                    square(2 * s + 1, frees + 2 * s + 2)
                    c.add("full")
                    c.add("bank", 2)
                    c.add("slab")

            def norm(shift):
                n = c.base("norm")
                act.wait_ge(sem("nsum"), KT * n)
                b = ps[(c.base("bank") - 5) % 8] if c.base("bank") else ps[0]
                A(stat[:, 0:TT], b[:, 0:TT], ACT.Sqrt, bias=eps[:], scale=1.0 / D).then_inc(sem("nstd"), 1)
                c.add("bank", 2)
                for k in range(KT):
                    if k < KT - 1:
                        act.wait_ge(sem("npre"), (KT - 1) * (n - 1) + k + 1)
                    else:
                        act.wait_ge(sem("acc_free"), c("bank"))
                    A(h_hi[:, k, :], pre[:, k, :], ACT.Identity, bias=mod[:, shift + k:shift + k + 1]).then_inc(sem("nhi"), 1)

            def side(plan, s, place, base=[0]):
                if plan.slab(s):
                    split()
                u = plan.copy(s)
                if u is not None:
                    if u % plan.uses == plan.uses - 1:
                        c.add("slab")
                        act.wait_ge(sem("slab_used"), c("slab"))
                    else:
                        act.wait_ge(sem("acc_full"), c.add("full"))
                    o = place(u)
                    A(o, ps[7][:, 0:o.shape[-1]], ACT.Copy).then_inc(sem("side_free"), 1)

            def attention(units, width, pre, plan, place):
                U = len(units)
                S, Pm, PT = (a_s, a_p, a_pt) if pre == "" else (h_s, h_p, h_pt)
                for s in range(U + 3):
                    side(plan, s, place)
                    u = s - 3
                    if 0 <= u < U:
                        n = width(units[u])
                        w = min(P, n)
                        act.wait_ge(sem(pre + "t_full"), u + 1)
                        if u >= 3:
                            act.wait_ge(sem(pre + "o_full"), u - 2)
                        A(PT[0:w, u % 3, 0:max(P, n)], ps[3 + u % 2][0:w, 0:max(P, n)], ACT.Copy).then_inc(sem(pre + "pt_ready"), 1)
                    if s < U:
                        n = width(units[s])
                        act.wait_ge(sem(pre + "s_done"), s + 1)
                        if s >= 4:
                            act.wait_ge(sem(pre + "t_full"), s - 3)
                        if s >= 8:
                            act.wait_ge(sem(pre + "inv_done"), s - 7)
                        A(Pm[:, s % 4, 0:n], S[:, s % 3, 0:n], ACT.Exp, bias=neg_max[:, s % 8:s % 8 + 1], scale=-1.0,
                          accum_out=row_sum[:, s % 8:s % 8 + 1]).then_inc(sem(pre + "p_ready"), 1)

            def ffn():
                turn = dict(slab=8, split=8, bank=16, full=8)
                for part in range(3):
                    for _ in (c.loop(act, QUARTERS - 2, turn) if part == 1 else range(1)):
                        for s in range(4):
                            split()
                            for m in range(2):
                                g = 2 * s + m
                                b = full(m)
                                A(relu[:, g % 2, :], b[:], ACT.Relu).then_inc(sem("relu_done"), 1)
                                if g:
                                    high(g - 1, 1)
                            c.add("slab")
                        high(KT - 1, 0)
                        if part < 2:
                            for s in range(4):
                                skip_t()
                        else:
                            down_and_squares()

            def high(g, behind):
                act.wait_ge(sem("acc_free"), c("bank", -behind))
                A(hid_hi[:, g, :], relu2[:, g % 2, :], ACT.Copy).then_inc(sem("hid_hi_done"), 1)

            act.wait_ge(sem("c_in"), 32)
            for s in range(2):
                A(cond[:, s, :], cond[:, s, :], ACT.Silu).then_inc(sem("cond_done"), 1)
            act.wait_ge(sem("consts_in"), 96)
            act.wait_ge(sem("ones_set"), 2)
            for k in range(KT):
                square(k, 0)
            split()
            norm(0)
            for kind, p in A_WALK:
                if kind == "p":
                    def square_a(t, b):
                        wait(act, "a_red", p)
                        A(a_sq[:, t, :], b[:], ACT.Square).then_inc(sem("a_sq_done"), 1)
                    natural(square_a)
                    act.wait_ge(sem("a_red"), p + 1)
                    A(rstd[:], stat[:], ACT.Sqrt, bias=eps[:], scale=1.0 / HD).then_inc(sem("a_std"), 1)
                elif kind == "v":
                    natural(None)
                else:
                    c.add("bank", 4)
            attention(UNITS_A, lambda u: P * (u[1] + 1), "", SIDE_A,
                      lambda u: a_v[:, u % TT, 512 + 256 * (u // TT):768 + 256 * (u // TT)])
            for i in range(KT):
                act.wait_ge(sem("xo_full"), i + 1)
                A(h_hi[:, i, :], ps_of(c)[:], ACT.Copy).then_inc(sem("xo_hi"), 1)
                c.add("bank")
            down_and_squares()
            norm(24)
            ffn()

            norm(48)
            for p in range(6):
                natural(lambda t, b: A(b_v[:, t, p * 512:(p + 1) * 512], b[:], ACT.Gelu).then_inc(sem("bv_done"), 1))
            act.wait_ge(sem("v_red"), 1)
            A(stat[:, 0:TT], stat[:, 0:TT], ACT.Sqrt, bias=eps[:], scale=1.0 / SG_HALF).then_inc(sem("v_std"), 1)
            for ch in range(CHUNKS):
                for s in range(4):
                    split()
                    for m in range(2):
                        b = full(m)
                        wait(act, "acc_free", c("bank", -1))
                        A(b_u[:], b[:], ACT.Gelu).then_inc(sem("bu_done"), 1)
                        c.add("bank")
                        act.wait_ge(sem("acc_free"), c("bank"))
                        A(g_hi[:, 2 * s + m, :], b_vm[:], ACT.Copy).then_inc(sem("g_hi_done"), 1)
                    c.add("slab")
                if ch < CHUNKS - 1:
                    for _ in range(4):
                        skip_t()
                else:
                    down_and_squares()
            norm(72)
            ffn()

            norm(96)

            def square_q(t, b):
                A(h_sq[:, t, :], b[:], ACT.Square).then_inc(sem("h_sq_done"), 1)
            natural(square_q)
            act.wait_ge(sem("h_red"), 1)
            A(rstd[:], stat[:], ACT.Sqrt, bias=eps[:], scale=1.0 / HD).then_inc(sem("h_std"), 1)
            act.wait_ge(sem("hq_done"), 1)

            def square_k(t, b):
                A(h_t1[:, t, :, :], b[:, 0:256].rearrange("p (a b) -> p a b", b=32), ACT.Square).then_inc(sem("h_sq_done"), 1)
            natural(square_k)
            act.wait_ge(sem("h_red"), 2)
            A(rstd[:, 0:16], stat[:, 0:16], ACT.Sqrt, bias=eps[:], scale=1.0 / HD).then_inc(sem("h_std"), 1)
            c.add("bank")
            act.wait_ge(sem("gates_copied"), 1)
            A(h_gts[:], h_gts[:], ACT.Sigmoid).then_inc(sem("gts_done"), 1)
            skip_t()
            skip_t()
            c.add("bank", 10)
            for kind in range(2):
                for _ in range(2):
                    split()
                    c.add("slab")
                c.add("full", 2)
                c.add("bank", 2)
                act.wait_ge(sem("hdn_copied"), kind + 1)
                A(hdn[:, kind, :, :], hdn[:, kind, :, :], ACT.Gelu_apprx_tanh).then_inc(sem("hdn_done"), 1)
                skip_t()
            act.wait_ge(sem("kc_red"), 1)
            A(kst[:, 0:2], kst[:, 0:2], ACT.Sqrt, bias=eps[0:CMP_PAD, :], scale=1.0 / HD).then_inc(sem("kc_std"), 1)
            skip_t()
            c.add("bank", 2)
            act.wait_ge(sem("z_copied"), 1)
            A(za[:], za[:], ACT.Silu).then_inc(sem("z_done"), 1)
            A(zs[:], zs[:], ACT.Silu).then_inc(sem("z_done"), 1)
            attention(UNITS_H, lambda u: CMP_PAD if u[3] == 0 else P * (u[2] + 1), "h", SIDE_H,
                      lambda u: uT[:, u, :])
            for i in range(4):
                act.wait_ge(sem("hxo_gated"), i + 1)
                A(h_hi[:, i, :], h_pt[:, i % 2, :], ACT.Copy).then_inc(sem("hxo_hi"), 1)
                c.add("bank")
            A(par["dt"][:], par["dt"][:], ACT.Exp).then_inc(sem("dt_done"), 1)
            act.wait_ge(sem("ang_done"), 1)
            A(par["r1"][:], par["xr"][:], ACT.Exp).then_inc(sem("trig_done"), 1)
            A(par["r8"][:], par["xr"][:], ACT.Exp, scale=float(L)).then_inc(sem("trig_done"), 1)
            A(par["sn"][:], par["th"][:], ACT.Sin).then_inc(sem("trig_done"), 1)
            A(par["h2"][:], par["th"][:], ACT.Sin, scale=0.5).then_inc(sem("trig_done"), 1)
            act.wait_ge(sem("yn_done"), 8)
            A(ynat[:], ynat[:], ACT.Gelu_apprx_tanh).then_inc(sem("yn_gelu"), 1)
            c.add("bank", 8 + 4 + NBLK * 7 + 8)
            for ct in range(4):
                act.wait_ge(sem("yt_done"), ct + 1)
                A(y_hi[:, ct, :], yT[:, ct, :], ACT.Copy).then_inc(sem("y_hi_done"), 1)
                c.add("bank")
            split()
            for m in range(4):
                b = full(m, 4)
                if m >= 2:
                    act.wait_ge(sem("acc_free"), c("bank", -2))
                A(sg_t[:, m % 2, :], b[:], ACT.Sigmoid, bias=glu_b[:, m:m + 1]).then_inc(sem("sg_done"), 1)
                act.wait_ge(sem("mx_done"), m + 1)
                A(h_hi[:, 4 + m, :], mx_t[:, m % 2, :], ACT.Copy).then_inc(sem("mix_hi"), 1)
            c.add("slab")
            for _ in range(4):
                skip_t()

        @block.vector
        def _(dve):
            c = Count()
            V = nc.vector
            tt, ts_, stt, cp = V.tensor_tensor, V.tensor_scalar, V.scalar_tensor_tensor, V.tensor_copy

            def step(ins, *more):
                for i in (ins, *more):
                    i.then_inc(sem("dve_step"), 1)
                    c.add("step")
                dve.wait_ge(sem("dve_step"), c("step"))

            def split():
                n = c.base("split")
                if c.reg is None and n >= N_SLABS:
                    return
                s = n % 2
                dve.wait_ge(sem("hi_done"), c("split", 1))
                tt(w_lo[s][:], w_raw[:, s, :], w_hi[s][:].bitcast(F32), ALU.subtract).then_inc(sem("lo_done"), 1)
                c.add("split")

            def full(m, tiles=2):
                if m == tiles - 1:
                    dve.wait_ge(sem("slab_used"), c("slab", 1))
                else:
                    dve.wait_ge(sem("acc_full"), c.add("full"))
                b = ps_of(c)
                c.add("bank")
                return b

            def free(ins, n=1):
                ins.then_inc(sem("acc_free"), n)

            def freed():
                dve.wait_ge(sem("acc_free"), c("bank"))

            def ada(n, which):
                for _ in range(n):
                    o, s = c.base("ada") - ada_base[0], c.base("ada") % 2
                    first = c.reg is None and c.base("ada") < ADA_FIRST
                    if first:
                        dve.wait_ge(sem(f"first_in{c.base('ada') * 4 // ADA_FIRST}"), 16)
                    else:
                        dve.wait_ge(sem(f"ada_in{s}"), c("ada", -s - ADA_FIRST) * 8 + 16)
                    w = ada_first[:, c.base("ada"), :] if first else ada_raw[:, s, :]
                    V.tensor_tensor_reduce(out=w, in0=w, in1=cond[:, which, :], scale=1.0, scalar=0.0, op0=ALU.mult, op1=ALU.add,
                                           accum_out=mod_s[:, o:o + 1]).then_inc(sem("ada_used"), 1)
                    c.add("ada")

            ada_base = [0]

            def ada_put():
                n, first = c.base("ada") - ada_base[0], c("ada", ada_base[0] - c.base("ada"))
                dve.wait_ge(sem("ada_used"), c("ada"))
                tt(mod[:, bass.ds(first, n)], mod_s[:, 0:n], mod_b[:, bass.ds(first, n)], ALU.add).then_inc(sem("mod_done"), 1)
                c.add("mod")
                dve.wait_ge(sem("mod_done"), c("mod"))
                ada_base[0] = c.base("ada")

            def residual(g, extra=lambda s: None, norm_next=False):
                for s in range(4):
                    split()
                    extra(s)
                    for m in range(2):
                        o = 2 * s + m
                        if norm_next and o == 3:
                            c.add("bank")
                        b = full(m)
                        free(stt(xT[:, o, :], b[:], mod[:, g + o:g + o + 1], xT[:, o, :], ALU.mult, ALU.add))
                    c.add("slab")

            def natural(use):
                split()
                c.add("slab")
                split()
                for t in range(TT):
                    use(t, full(t, TT))
                c.add("slab")

            def norm(i, shift):
                n = c.add("norm")
                step(stt(mod_a[:], mod[:, shift + 8:shift + 16], 1.0, norm_g[:, i, :], ALU.add, ALU.mult))
                dve.wait_ge(sem("nstd"), n)
                free(V.reciprocal(rstd[:, 0:TT], stat[:, 0:TT]))
                freed()
                for t in range(TT):
                    ts_(diag[:, t, :], ident[:], rstd[:, t:t + 1], None, ALU.mult).then_inc(sem("ndiag"), 1)
                dve.wait_ge(sem("nbc"), n)
                b = ps_of(c)
                c.add("bank")
                for k in range(KT):
                    ins = stt(pre[:, k, :], xT[:, k, :], mod_a[:, k:k + 1], b[:], ALU.mult, ALU.mult)
                    if k < KT - 1:
                        ins.then_inc(sem("npre"), 1)
                    else:
                        free(ins)
                for k in range(KT):
                    dve.wait_ge(sem("nhi"), KT * (n - 1) + k + 1)
                    stt(h_lo[:, k, :], pre[:, k, :], mod[:, shift + k:shift + k + 1], h_hi[:, k, :].bitcast(F32), ALU.add, ALU.subtract)\
                        .then_inc(sem("nlo"), 1)

            def attention(units, width, mask, combine, pre, plan):
                U = len(units)
                S = a_s if pre == "" else h_s
                for s in range(U + 4):
                    if s < U:
                        n = width(units[s])
                        dve.wait_ge(sem(pre + "s_full"), s + 1)
                        if s >= 3:
                            dve.wait_ge(sem(pre + "p_ready"), s - 2)
                        V.tensor_tensor_reduce(out=S[:, s % 3, 0:n], in0=ps[s % 3][:, 0:n], in1=mask(units[s]), scale=-1.0,
                                               scalar=3e38, op0=ALU.add, op1=ALU.min, accum_out=neg_max[:, s % 8:s % 8 + 1])\
                         .then_inc(sem(pre + "s_done"), 1)
                    if plan.slab(s):
                        split()
                    u = s - 4
                    if 0 <= u < U:
                        dve.wait_ge(sem(pre + "p_ready"), u + 1)
                        V.reciprocal(row_inv[:, u % 8:u % 8 + 1], row_sum[:, u % 8:u % 8 + 1]).then_inc(sem(pre + "inv_done"), 1)
                        dve.wait_ge(sem(pre + "inv_done"), u + 1)
                        combine(u, units[u])

            def ffn(g, tiles, which):
                turn = dict(slab=8, split=8, bank=16, full=8, hid=KT, ada=tiles, mod=1)
                share = [(tiles * (s + 1)) // 8 - tiles * s // 8 for s in range(8)]
                for part in range(3):
                    ada_base[0] = c.base("ada")
                    for _ in (c.loop(dve, QUARTERS - 2, turn) if part == 1 else range(1)):
                        quarter(g, share, which, part == 2)

            def quarter(g, share, which, last):
                    for s in range(4):
                        split()
                        for m in range(2):
                            o = 2 * s + m
                            b = full(m)
                            dve.wait_ge(sem("relu_done"), c("hid", o + 1))
                            if o >= 2:
                                dve.wait_ge(sem("hid_lo_done"), c("hid", o - 1))
                            free(stt(relu2[:, o % 2, :], b[:], 0.0, relu[:, o % 2, :], ALU.max, ALU.mult))
                            if o:
                                low(o - 1)
                        c.add("slab")
                        ada(share[s], which)
                    low(KT - 1)
                    c.add("hid", KT)
                    residual(g, lambda s: ada(share[4 + s], which), last)
                    ada_put()

            def low(o):
                dve.wait_ge(sem("hid_hi_done"), c("hid", o + 1))
                tt(hid_lo[:, o, :], relu2[:, o % 2, :], hid_hi[:, o, :].bitcast(F32), ALU.subtract).then_inc(sem("hid_lo_done"), 1)

            dve.wait_ge(sem("consts_in"), 96)
            dve.wait_ge(sem("ones_set"), 2)
            dve.wait_ge(sem("cond_done"), 2)
            split()
            ada(16, 0)
            ada_put()
            c.add("bank")
            norm(0, 0)
            for kind, p in A_WALK:
                if kind == "p":
                    banks = {}
                    natural(lambda t, b: banks.setdefault(t, b))
                    dve.wait_ge(sem("a_sq_done"), TT * (p + 1))
                    V.tensor_reduce(stat[:], a_sq[:].rearrange("p t (h d) -> p (t h) d", d=HD), AX.X, ALU.add).then_inc(sem("a_red"), 1)
                    dve.wait_ge(sem("a_std"), p + 1)
                    step(V.reciprocal(stat[:], rstd[:]))
                    for t in range(TT):
                        free(tt(a_qn[:, p % 2, t, :].rearrange("p (h d) -> p h d", d=HD), banks[t][:].rearrange("p (h d) -> p h d", d=HD),
                                stat[:, 8 * t:8 * t + 8].unsqueeze(2).to_broadcast([P, 8, HD]), ALU.mult))
                    freed()
                    V.engine_nop().then_inc(sem("qn_done"), 1)
                    ada(3, 0)
                elif kind == "v":
                    natural(lambda t, b: free(cp(a_v[:, t, p * 512:(p + 1) * 512], b[:])))
                    ada(4, 0)
                else:
                    for i in range(4):
                        dve.wait_ge(sem("xp_full"), 4 * p + i + 1)
                        o = (a_qT if p < 2 else a_kT)[:, 4 * (p % 2) + i, :]
                        free(ts_(o, ps_of(c)[:], aqk_g[:, p // 2:p // 2 + 1], HD ** -0.5 if p < 2 else 1.0, ALU.mult, ALU.mult))
                        c.add("bank")

            ada_put()

            def mask_a(u):
                h, it = u
                if it == 0:
                    dve.wait_ge(sem(f"bias_in{h % 3}"), 16 * (h // 3 + 1))
                return a_bias[:, h % 3, P * (TT - 1 - it):T]

            def combine_a(u, unit):
                h, it = unit
                dve.wait_ge(sem("o_full"), u + 1)
                ts_(a_o[:, it, h * HD:(h + 1) * HD], ps[5 + u % 2][:, 0:HD], row_inv[:, u % 8:u % 8 + 1], None, ALU.mult).then_inc(sem("o_done"), 1)
                if it == 1:
                    ada(1, 0)
                if it == TT - 1 and h % 8 == 7:
                    ada_put()

            attention(UNITS_A, lambda u: P * (u[1] + 1), mask_a, combine_a, "", SIDE_A)
            c.add("slab", 2)
            c.add("full", 2 * (TT - 1))
            for i in range(KT):
                dve.wait_ge(sem("xo_hi"), i + 1)
                tt(h_lo[:, i, :], ps_of(c)[:], h_hi[:, i, :].bitcast(F32), ALU.subtract).then_inc(sem("xo_lo"), 1)
                dve.wait_ge(sem("xo_lo"), i + 1)
                free(V.engine_nop())
                c.add("bank")
            residual(16, norm_next=True)
            norm(1, 24)
            ffn(40, 12, 0)

            norm(2, 48)
            dve.wait_ge(sem("bws_in"), 32)
            V.memset(b_ws[HD:P, :, 0:HD], 0.0).then_inc(sem("bws_masked"), 1)
            for p in range(6):
                def sq(t, b):
                    dve.wait_ge(sem("bv_done"), TT * p + t + 1)
                    v = b_v[:, t, p * 512:(p + 1) * 512]
                    free(V.tensor_tensor_reduce(out=b[:], in0=v, in1=v, scale=1.0, scalar=0.0, op0=ALU.mult, op1=ALU.add,
                                                accum_out=vss[:, t, p:p + 1]))
                natural(sq)
            freed()
            V.tensor_reduce(stat[:, 0:TT], vss[:], AX.X, ALU.add).then_inc(sem("v_red"), 1)
            dve.wait_ge(sem("v_std"), 1)
            step(V.reciprocal(rstd[:, 0:TT], stat[:, 0:TT]))
            for t in range(TT):
                ts_(b_v[:, t, :], b_v[:, t, :], rstd[:, t:t + 1], None, ALU.mult).then_inc(sem("bv_scaled"), 1)
            for ch in range(CHUNKS):
                for s in range(4):
                    split()
                    for m in range(2):
                        gm = KT * ch + 2 * s + m
                        full(m)
                        dve.wait_ge(sem("mix_full"), gm + 1)
                        b = ps_of(c)
                        c.add("bank")
                        if gm:
                            dve.wait_ge(sem("g_lo_done"), gm)
                        stt(b_vm[:].rearrange("p (n i) -> p n i", i=P), b[:].rearrange("p (n i) -> p n i", i=P), bv_g[:, gm:gm + 1],
                            b_bs[:, gm // 3, :].unsqueeze(1).to_broadcast([P, TT, P]), ALU.mult, ALU.add).then_inc(sem("bvm_done"), 1)
                        dve.wait_ge(sem("bvm_done"), gm + 1)
                        dve.wait_ge(sem("bu_done"), gm + 1)
                        free(tt(b_vm[:], b_vm[:], b_u[:], ALU.mult), 2)
                        dve.wait_ge(sem("g_hi_done"), gm + 1)
                        tt(g_lo[:, 2 * s + m, :], b_vm[:], g_hi[:, 2 * s + m, :].bitcast(F32), ALU.subtract).then_inc(sem("g_lo_done"), 1)
                    c.add("slab")
                residual(64, norm_next=ch == CHUNKS - 1)
            norm(3, 72)
            ffn(88, 6, 1)

            norm(4, 96)
            N_SMALL = 17
            banks = {}
            natural(lambda t, b: banks.setdefault(t, b))
            dve.wait_ge(sem("h_sq_done"), TT)
            V.tensor_reduce(stat[:], h_sq[:].rearrange("p t (h d) -> p (t h) d", d=HD), AX.X, ALU.add).then_inc(sem("h_red"), 1)
            dve.wait_ge(sem("h_std"), 1)
            step(V.reciprocal(stat[:], rstd[:]))
            for t in range(TT):
                free(tt(h_qn[:, t, :].rearrange("p (h d) -> p h d", d=HD), banks[t][:].rearrange("p (h d) -> p h d", d=HD),
                        stat[:, 8 * t:8 * t + 8].unsqueeze(2).to_broadcast([P, 8, HD]), ALU.mult))
            freed()
            dve.wait_ge(sem("h_in"), 16 * N_SMALL)
            step(*[tt(h_qn[:, t, :].rearrange("p (h d) -> p h d", d=HD), h_qn[:, t, :].rearrange("p (h d) -> p h d", d=HD),
                      qg_b[:].unsqueeze(1).to_broadcast([P, 8, HD]), ALU.mult) for t in range(TT)])

            def rope(src, dst, heads, signal):
                x = src[:].rearrange("p t (h d) -> p t h d", d=HD)
                o = dst[:].rearrange("p t (h d) -> p t h d", d=HD)
                x1, x2, o1, o2 = x[:, :, :, 0:32], x[:, :, :, 32:HD], o[:, :, :, 0:32], o[:, :, :, 32:HD]
                co = cos[:].unsqueeze(2).to_broadcast([P, TT, heads, 32])
                si = sin[:].unsqueeze(2).to_broadcast([P, TT, heads, 32])
                a, b = h_t1[:, :, 0:heads, :], h_t2[:, :, 0:heads, :]
                step(tt(a, x1, co, ALU.mult), tt(b, x2, si, ALU.mult))
                step(tt(o1, a, b, ALU.subtract))
                step(tt(a, x2, co, ALU.mult), tt(b, x1, si, ALU.mult))
                tt(o2, a, b, ALU.add).then_inc(sem(signal), 1)
                dve.wait_ge(sem(signal), 1)

            rope(h_qn, h_qr, 8, "hq_done")
            step(cp(wg_hi[:], wg[:]))
            tt(wg_lo[:], wg[:], wg_hi[:].bitcast(F32), ALU.subtract).then_inc(sem("wg_split"), 1)
            banks = {}
            natural(lambda t, b: banks.setdefault(t, b))
            dve.wait_ge(sem("h_sq_done"), 2 * TT)
            V.tensor_reduce(stat[:, 0:16], h_t1[:].rearrange("p t a b -> p (t a b)").rearrange("p (n d) -> p n d", d=HD), AX.X, ALU.add)\
             .then_inc(sem("h_red"), 1)
            dve.wait_ge(sem("h_std"), 2)
            step(V.reciprocal(stat[:, 0:16], rstd[:, 0:16]))
            for t in range(TT):
                step(tt(h_kn[:, t, :].rearrange("p (h d) -> p h d", d=HD), banks[t][:, 0:256].rearrange("p (h d) -> p h d", d=HD),
                        stat[:, 4 * t:4 * t + 4].unsqueeze(2).to_broadcast([P, 4, HD]), ALU.mult))
                free(cp(hv[:, t, :], banks[t][:, 256:512]))
            step(*[tt(h_kn[:, t, :].rearrange("p (h d) -> p h d", d=HD), h_kn[:, t, :].rearrange("p (h d) -> p h d", d=HD),
                      kg_b[:], ALU.mult) for t in range(TT)])
            rope(h_kn, h_kr, 4, "hk_done")
            dve.wait_ge(sem("gates_full"), 1)
            b = ps_of(c)
            c.add("bank")
            step(cp(h_gts[:], b[:, 0:TT * 24].rearrange("p (t n) -> p t n", n=24)))
            V.engine_nop().then_inc(sem("gates_copied"), 1)
            free(V.engine_nop())

            def half(tile, k):
                split()
                for m in range(2):
                    b = full(m)
                    free(cp(tile[:, 2 * k + m, :], b[:]))
                c.add("slab")

            def blocks(kind):
                ins = []
                src = crT[:, kind, :].rearrange("p (n l) -> p l n", l=16)
                for lp in range(2):
                    for g in range(H_GROUPS):
                        r = slice(HD * g, HD * g + HD)
                        for half_ in range(2):
                            ins.append(tt(bl[HD * lp:HD * lp + HD, 8 * half_:8 * half_ + 8, CMP_PAD * g:CMP_PAD * g + CMP_N],
                                          src[r, :, half_:half_ + CMP_N].rearrange("p (a b) n -> p a b n", b=2)[:, :, lp, :],
                                          posT[r, kind, 16 * half_:16 * half_ + 16].rearrange("p (a b) -> p a b", b=2)[:, :, lp].unsqueeze(2)
                                          .to_broadcast([HD, 8, CMP_N]), ALU.add))
                step(*ins)

            def split_blocks(kind):
                step(cp(bl_hi[:], bl[:]))
                tt(bl_lo[:], bl[:], bl_hi[:].bitcast(F32), ALU.subtract).then_inc(sem("bl_done"), 1)
                dve.wait_ge(sem("bl_done"), kind + 1)

            half(crT, 0)
            freed()
            step(V.memset(bl[:], 0.0))
            blocks(0)
            split_blocks(0)
            half(za, 0)
            for i in range(8):
                dve.wait_ge(sem("hx_full"), i + 1)
                free(ts_((hq if i < 4 else hqr)[:, i % 4, :], ps_of(c)[:], HD ** -0.5, None, ALU.mult))
                c.add("bank")
            for i in range(2):
                dve.wait_ge(sem("hx_full"), 9 + i)
                free(cp(hk[:, i, :], ps_of(c)[:]))
                c.add("bank")
            for kind in range(2):
                split()
                c.add("slab")
                c.add("full", 1)
                if kind == 0:
                    blocks(1)
                split()
                for m in range(2):
                    b = full(m)
                    free(cp(hdn[:, kind, m, :], b[:, 0:2 * CMP_PAD]))
                freed()
                V.engine_nop().then_inc(sem("hdn_copied"), 1)
                c.add("slab")
                if kind == 0:
                    split_blocks(1)
                    half(za, 1)
                else:
                    half(zs, 0)
            dve.wait_ge(sem("kc_full"), 1)
            b = ps_of(c)
            c.add("bank")
            step(cp(kcn[:], b[0:CMP_PAD, 0:2 * HD].rearrange("n (g d) -> n g d", d=HD)),
                 cp(vc[:], b[0:CMP_PAD, 2 * HD:4 * HD].rearrange("n (g d) -> n g d", d=HD)))
            free(tt(kcsq[:], kcn[:], kcn[:], ALU.mult))
            freed()
            V.tensor_reduce(kst[:, 0:2], kcsq[:], AX.X, ALU.add).then_inc(sem("kc_red"), 1)
            dve.wait_ge(sem("kc_std"), 1)
            step(V.reciprocal(kst[:, 2:4], kst[:, 0:2]))
            step(tt(kcn[:], kcn[:], kst[:, 2:4].unsqueeze(2).to_broadcast([CMP_PAD, 2, HD]), ALU.mult))
            tt(kcn[:], kcn[:], kcg_b[:].unsqueeze(1).to_broadcast([CMP_PAD, 2, HD]), ALU.mult).then_inc(sem("kcn_done"), 1)
            half(zs, 1)
            freed()
            V.engine_nop().then_inc(sem("z_copied"), 1)
            dve.wait_ge(sem("kct_full"), 1)
            free(cp(kcT[:], ps_of(c)[:, 0:CMP_PAD]))
            c.add("bank")
            dve.wait_ge(sem("gts_done"), 1)

            def mask_h(u):
                i, g, it, br = u
                return h_cmask[:, it, :] if br == 0 else h_mask[:, P * (TT - 1 - it):T]

            def combine_h(u, unit):
                i, g, it, br = unit
                hp = 2 * i + g
                w = wbr[:, u % 4:u % 4 + 1]
                step(stt(w, row_inv[:, u % 8:u % 8 + 1], h_flag[:, it:it + 1] if br == 0 else 1.0,
                         h_gts[:, it, N_BR * hp + br:N_BR * hp + br + 1], ALU.mult, ALU.mult))
                dve.wait_ge(sem("ho_full"), u + 1)
                o, p_ = h_o[:, it, hp * HD:(hp + 1) * HD], ps[5 + u % 2][:, 0:HD]
                if br == 0:
                    ins = ts_(o, p_, w, None, ALU.mult)
                else:
                    dve.wait_ge(sem("ho_done"), u)
                    ins = stt(o, p_, w, o, ALU.mult, ALU.add)
                ins.then_inc(sem("ho_done"), 1)

            attention(UNITS_H, lambda u: CMP_PAD if u[3] == 0 else P * (u[2] + 1), mask_h, combine_h, "h", SIDE_H)
            c.add("slab", 2)
            c.add("full", 2)
            dve.wait_ge(sem("z_done"), 2)
            dve.wait_ge(sem("ho_done"), NUH)
            for i in range(4):
                dve.wait_ge(sem("hxo_full"), i + 1)
                tt(h_pt[:, i % 2, :], ps_of(c)[:], za[:, i, :], ALU.mult).then_inc(sem("hxo_gated"), 1)
                dve.wait_ge(sem("hxo_hi"), i + 1)
                tt(h_lo[:, i, :], h_pt[:, i % 2, :], h_hi[:, i, :].bitcast(F32), ALU.subtract).then_inc(sem("hx_done"), 1)
                dve.wait_ge(sem("hx_done"), i + 1)
                free(V.engine_nop())
                c.add("bank")

            p_ = {k: v[:] for k, v in par.items()}

            def m_(o, a, b, op=ALU.mult):
                return tt(p_[o], p_[a], p_[b], op)

            dve.wait_ge(sem("dt_done"), 1)
            step(m_("xr", "ar", "dt"), m_("th", "ai", "dt"))
            MAGIC, C1 = 12582912.0, 6.28125
            C2 = 2 * math.pi - C1
            PI_DOWN = 3.1415925
            step(ts_(p_["kk"], p_["th"], 1 / (2 * math.pi), MAGIC, ALU.mult, ALU.add))
            step(ts_(p_["kk"], p_["kk"], MAGIC, None, ALU.subtract))
            step(stt(p_["t1"], p_["kk"], -C1, p_["th"], ALU.mult, ALU.add))
            step(stt(p_["th"], p_["kk"], -C2, p_["t1"], ALU.mult, ALU.add))
            ts_(p_["th"], p_["th"], PI_DOWN, -PI_DOWN, ALU.min, ALU.max).then_inc(sem("ang_done"), 1)
            dve.wait_ge(sem("trig_done"), 4)
            step(m_("t1", "h2", "h2"))
            step(ts_(p_["cs"], p_["t1"], -2.0, 1.0, ALU.mult, ALU.add))
            step(V.memset(Lr[:, 0, :], 1.0), V.memset(Ls[:, 0, :], 0.0),
                 tt(Lr[:, 1, :], p_["r1"], p_["cs"], ALU.mult), tt(Ls[:, 1, :], p_["r1"], p_["sn"], ALU.mult))
            for lo, n in ((2, 1), (3, 2), (5, 4)):
                wide = lambda a: a.unsqueeze(1).to_broadcast([P, n, G_ALL])
                br_, bi_ = wide(Lr[:, lo - 1, :]), wide(Ls[:, lo - 1, :])
                a_r, a_i = Lr[:, 1:1 + n, :], Ls[:, 1:1 + n, :]
                v = [z[:].rearrange("p a b -> p (a b)")[:, 0:n * G_ALL].rearrange("p (a b) -> p a b", b=G_ALL)
                     for z in (t_a, t_b, Er, Ei)]
                step(tt(v[0], a_r, br_, ALU.mult), tt(v[1], a_i, bi_, ALU.mult), tt(v[2], a_r, bi_, ALU.mult), tt(v[3], a_i, br_, ALU.mult))
                step(tt(Lr[:, lo:lo + n, :], v[0], v[1], ALU.subtract), tt(Ls[:, lo:lo + n, :], v[2], v[3], ALU.add))
            step(ts_(p_["nr"], Lr[:, 1, :], 1.0, None, ALU.subtract), m_("t1", "ar", "ar"), m_("t2", "ai", "ai"))
            step(m_("t3", "t1", "t2", ALU.add))
            step(V.reciprocal(p_["d2"], p_["t3"]))
            step(m_("t1", "nr", "ar"), tt(p_["t2"], Ls[:, 1, :], p_["ai"], ALU.mult))
            step(m_("t3", "t1", "t2", ALU.add))
            step(m_("fr", "t3", "d2"))
            step(tt(p_["t1"], Ls[:, 1, :], p_["ar"], ALU.mult), m_("t2", "nr", "ai"))
            step(m_("t3", "t1", "t2", ALU.subtract))
            step(m_("fs", "t3", "d2"))
            step(ts_(p_["fs"], p_["fs"], sgn[:, 0:1], None, ALU.mult), ts_(Ls[:], Ls[:], sgn[:, 0:1], None, ALU.mult))
            step(*[cp(o[:, j, :], i_[:, L - 1 - j, :]) for o, i_ in ((LrR, Lr), (LsR, Ls)) for j in range(L)])
            step(cp(p_["er"], p_["cs"]), cp(p_["ei"], p_["sn"]))
            for _ in range(3):
                step(m_("t1", "er", "er"), m_("t2", "ei", "ei"), m_("t3", "er", "ei"))
                step(m_("er", "t1", "t2", ALU.subtract), ts_(p_["ei"], p_["t3"], 2.0, None, ALU.mult))

            for q in range(8):
                dve.wait_ge(sem("u_full"), q + 1)
                ct, jj = q // 2, q % 2
                src = ps_of(c)[0:NCH, :].rearrange("n (j g c) -> n j g c", j=4, g=8)
                for j in range(4):
                    ins = cp(U[:, 8 * ct:8 * ct + 8, (4 * jj + j) * CH:(4 * jj + j + 1) * CH], src[:, j, :, :])
                    if j < 3:
                        ins.then_inc(sem("dve_step"), 1)
                        c.add("step")
                dve.wait_ge(sem("dve_step"), c("step"))
                ins.then_inc(sem("u_done"), 1)
                dve.wait_ge(sem("u_done"), q + 1)
                free(V.engine_nop())
                c.add("bank")
            for q in range(4):
                dve.wait_ge(sem("ut_full"), q + 1)
                cp(UT[:, 8 * q:8 * q + 8, :], ps_of(c)[:].rearrange("p (g n) -> p g n", n=NCH)).then_inc(sem("ut_done"), 1)
                dve.wait_ge(sem("ut_done"), q + 1)
                free(V.engine_nop())
                c.add("bank")
            dve.wait_ge(sem("s5_in"), 64)
            step(V.memset(KTp[:, :, 0:ZPAD], 0.0))
            for blk in range(NBLK):
                gs = slice(blk * GB, (blk + 1) * GB)

                def over(a, n):
                    return a.unsqueeze(2).to_broadcast([P, GB, n])

                def taps(a, n):
                    return a.unsqueeze(2).to_broadcast([P, GB, n, CH])

                def power(a, n):
                    return a[:, 0:n, gs].rearrange("p n g -> p g n").unsqueeze(3).to_broadcast([P, GB, n, CH])

                def four(z, n):
                    return z[:, :, 0:n * CH].rearrange("p g (n c) -> p g n c", c=CH)

                fr, fs = over(par["fr"][:, gs], CH), over(par["fs"][:, gs], CH)
                ta, tb = t_a[:, :, 0:CH], t_b[:, :, 0:CH]
                tc, td = t_a[:, :, CH:2 * CH], t_b[:, :, CH:2 * CH]
                step(tt(ta, Bo[:, gs, :], fr, ALU.mult), tt(tb, Bx[:, gs, :], fs, ALU.mult),
                     tt(tc, Bx[:, gs, :], fr, ALU.mult), tt(td, Bo[:, gs, :], fs, ALU.mult))
                step(tt(bbo[:], ta, tb, ALU.add), tt(bbx[:], tc, td, ALU.subtract))
                step(tt(four(t_a, L), taps(bbo[:], L), power(LrR, L), ALU.mult), tt(four(t_b, L), taps(bbx[:], L), power(LsR, L), ALU.mult))
                tt(Gb[:], t_a[:, :, 0:L * CH], t_b[:, :, 0:L * CH], ALU.add).then_inc(sem("gb_done"), 1)
                dve.wait_ge(sem("gb_done"), blk + 1)
                step(tt(four(t_a, TAPS), taps(Co[:, gs, :], TAPS), power(Lr, TAPS), ALU.mult),
                     tt(four(t_b, TAPS), taps(Cx[:, gs, :], TAPS), power(Ls, TAPS), ALU.mult))
                step(tt(Hc[:], t_a[:], t_b[:], ALU.add))
                step(ts_(Hc[:], Hc[:], sgn[:, 1:2], None, ALU.mult))
                step(tt(four(t_a, TAPS), taps(Co[:, gs, :], TAPS), power(Ls, TAPS), ALU.mult),
                     tt(four(t_b, TAPS), taps(Cx[:, gs, :], TAPS), power(Lr, TAPS), ALU.mult))
                tt(Hs[:], t_a[:], t_b[:], ALU.subtract).then_inc(sem("hc_done"), 1)
                dve.wait_ge(sem("hc_done"), blk + 1)
                q_r, q_i = par["t1"][:, gs], par["t2"][:, gs]
                step(V.memset(Er[:, :, 0:1], 1.0), V.memset(Ei[:, :, 0:1], 0.0), cp(q_r, par["er"][:, gs]), cp(q_i, par["ei"][:, gs]))
                n = 1
                while n < NCH:
                    a, b_, d, e = (z[:, :, k:k + n] for z, k in ((t_a, 0), (t_b, 0), (t_a, n), (t_b, n)))
                    step(tt(a, Er[:, :, 0:n], over(q_r, n), ALU.mult), tt(b_, Ei[:, :, 0:n], over(q_i, n), ALU.mult),
                         tt(d, Er[:, :, 0:n], over(q_i, n), ALU.mult), tt(e, Ei[:, :, 0:n], over(q_r, n), ALU.mult))
                    step(tt(Er[:, :, n:2 * n], a, b_, ALU.subtract), tt(Ei[:, :, n:2 * n], d, e, ALU.add),
                         tt(par["t3"][:, 0:GB], q_r, q_r, ALU.mult), tt(par["t3"][:, GB:2 * GB], q_i, q_i, ALU.mult),
                         tt(par["t3"][:, 2 * GB:3 * GB], q_r, q_i, ALU.mult))
                    step(tt(q_r, par["t3"][:, 0:GB], par["t3"][:, GB:2 * GB], ALU.subtract),
                         ts_(q_i, par["t3"][:, 2 * GB:3 * GB], 2.0, None, ALU.mult))
                    n *= 2
                for q in range(2):
                    dve.wait_ge(sem("gb_full"), 2 * blk + q + 1)
                    src = ps_of(c)[:].rearrange("p (g m) -> p g m", m=P)
                    d = Gt[:, 4 * q:4 * q + 4, :]
                    step(cp(d[:, :, 0:P], src), cp(d[:, :, P:P + ST], src[:, :, ST:P]))
                    ts_(d[:, :, P + ST:2 * P], src[:, :, 0:ST], -1.0, None, ALU.mult).then_inc(sem("gt_done"), 1)
                    dve.wait_ge(sem("gt_done"), 2 * blk + q + 1)
                    free(V.engine_nop())
                    c.add("bank")
                for q in range(2):
                    dve.wait_ge(sem("kt_full"), 2 * blk + q + 1)
                    if q == 0 and blk:
                        dve.wait_ge(sem("tz_in"), 16 * L * blk)
                    src = ps_of(c)[0:CH, :].rearrange("p (g m) -> p g m", m=P)
                    g4 = slice(4 * q, 4 * q + 4)
                    step(cp(KTp[:, g4, ZPAD:], src))
                    step(tt(KTp[:, g4, ZPAD:ZPAD + CH], src[:, :, 0:CH], dsk[:, blk * GB + 4 * q:blk * GB + 4 * q + 4, :], ALU.add))
                    free(V.engine_nop())
                    c.add("bank")
                V.engine_nop().then_inc(sem("ktp_done"), 1)
                va = t_a[:, :, 0:NCH]
                vb = t_b[:, :, 0:NCH]
                dve.wait_ge(sem("x_full"), 2 * blk + 1)
                step(tt(va, ps_of(c)[:].rearrange("p (g n) -> p g n", n=NCH), Er[:], ALU.mult))
                c.add("bank")
                dve.wait_ge(sem("x_full"), 2 * blk + 2)
                step(tt(vb, ps_of(c)[:].rearrange("p (g n) -> p g n", n=NCH), Ei[:], ALU.mult))
                c.add("bank")
                free(tt(va, va, vb, ALU.add), 2)
                freed()
                step(*[V.tensor_tensor_scan(wst[:, g, :], par["r8"][:, blk * GB + g:blk * GB + g + 1].to_broadcast([P, NCH]), t_a[:, g, 0:NCH],
                                            0.0, ALU.mult, ALU.add) for g in range(GB)])
                step(tt(va, wst[:], Er[:], ALU.mult))
                tt(vb, wst[:], Ei[:], ALU.mult).then_inc(sem("st_done"), 1)
                dve.wait_ge(sem("y_mm"), blk + 1)
                cp(Y[:, gs, :], ps_of(c)[:].rearrange("p (g n) -> p g n", n=NCH)).then_inc(sem("y_done"), 1)
                dve.wait_ge(sem("y_done"), blk + 1)
                free(V.engine_nop())
                c.add("bank")
            for q in range(8):
                dve.wait_ge(sem("yn_full"), q + 1)
                src = ps_of(c)[0:NCH, :].rearrange("n (g i c) -> n g i c", g=4, i=L)
                dst = ynat[:].rearrange("n i (g c) -> n g i c", c=CH)
                for g in range(4):
                    ins = cp(dst[:, 4 * q + g, :, :], src[:, g, :, :])
                    if g < 3:
                        ins.then_inc(sem("dve_step"), 1)
                        c.add("step")
                dve.wait_ge(sem("dve_step"), c("step"))
                ins.then_inc(sem("yn_done"), 1)
                dve.wait_ge(sem("yn_done"), q + 1)
                free(V.engine_nop())
                c.add("bank")
            for ct in range(4):
                dve.wait_ge(sem("yt_full"), ct + 1)
                cp(yT[:, ct, :].rearrange("p (n i) -> p i n", i=L), ps_of(c)[:].rearrange("p (i n) -> p i n", n=NCH)).then_inc(sem("yt_done"), 1)
                dve.wait_ge(sem("yt_done"), ct + 1)
                free(V.engine_nop())
                c.add("bank")
                dve.wait_ge(sem("y_hi_done"), ct + 1)
                tt(y_lo[:, ct, :], yT[:, ct, :], y_hi[:, ct, :].bitcast(F32), ALU.subtract).then_inc(sem("y_lo_done"), 1)
            split()
            for m in range(4):
                full(m, 4)
                dve.wait_ge(sem("sg_done"), m + 1)
                if m >= 2:
                    dve.wait_ge(sem("mix_lo"), m - 1)
                free(tt(mx_t[:, m % 2, :], sg_t[:, m % 2, :], yT[:, m, :], ALU.mult))
                freed()
                tt(mx_t[:, m % 2, :], mx_t[:, m % 2, :], zs[:, m, :], ALU.mult).then_inc(sem("mx_done"), 1)
                dve.wait_ge(sem("mix_hi"), m + 1)
                tt(h_lo[:, 4 + m, :], mx_t[:, m % 2, :], h_hi[:, 4 + m, :].bitcast(F32), ALU.subtract).then_inc(sem("mix_lo"), 1)
            c.add("slab")
            for s in range(4):
                split()
                for m in range(2):
                    o = 2 * s + m
                    b = full(m)
                    stt(xT[:, o, :], b[:], mod[:, 112 + o:113 + o], xT[:, o, :], ALU.mult, ALU.add).then_inc(sem("x_final"), 1)
                    dve.wait_ge(sem("x_final"), o + 1)
                    free(V.engine_nop())
                c.add("slab")


def kernel(**inputs):
    import numpy as np
    import concourse.bacc as _bacc
    from concourse.bass_utils import run_bass_kernel_spmd as _run

    a = {k: np.asarray(v) for k, v in inputs.items()}
    f = lambda x: np.ascontiguousarray(x, dtype=np.float32)

    def natural(w):
        K, N = w.shape
        return w.reshape(K // 512, 4, 128, N // 512, 512).transpose(3, 0, 2, 1, 4).reshape(-1, 128, SLAB)

    def transposed(w):
        K, N = w.shape
        return w.reshape(8, 128, N // 256, 256).transpose(2, 1, 0, 3).reshape(-1, 128, SLAB)

    def down(w, parts):
        return [transposed(x) for x in np.split(w, parts, axis=0)]

    def ffn(l):
        up = np.split(transposed(a["ffn_w1"][l]), QUARTERS)
        return [x for pair in zip(up, down(a["ffn_w2"][l], QUARTERS)) for x in pair]

    b_in = a["b_w_in"][0]
    u_slabs = np.split(transposed(b_in[:, :SG_HALF]), CHUNKS)
    b_slabs = [x for pair in zip(u_slabs, down(a["b_w_out"][0], CHUNKS)) for x in pair]
    order = [g * 4 + i for i in range(4) for g in range(2)]
    w = a["w_in_2"][0]
    cols = np.cumsum([0, 512] + [128] * 6 + [512, 24, 512, 512])
    q, kcr, vcr, ksl, vsl, kwn, vwn, z_a, g_br, u, z_s = (w[:, cols[i]:cols[i + 1]] for i in range(11))
    heads = lambda m, n: m.reshape(m.shape[0], 8, n)[:, order].reshape(m.shape[0], 8 * n)
    w_out = a["w_out_2"][0]
    w_out = np.concatenate([w_out[:512].reshape(8, 64, D)[order].reshape(512, D), w_out[512:]])
    glu = a["glu_w_2"][0].reshape(4, 128, 512).transpose(1, 0, 2).reshape(1, 128, SLAB)
    a_in = a["a_w_in"][0]
    za = transposed(heads(z_a, 64))
    slabs = np.concatenate([natural(a_in[:, :2560]), transposed(a_in[:, 2560:]), transposed(a["a_w_out"][0])] + ffn(0)
                           + [natural(b_in[:, SG_HALF:])] + b_slabs + ffn(1)
                           + [natural(heads(q, 64)), natural(np.concatenate([ksl, kwn, vsl, vwn], 1)),
                              transposed(np.concatenate([kcr, vcr], 1)), za[:1]] + down(a["cmp_w1_k_2"][0], 2) + [za[1:]]
                           + down(a["cmp_w1_v_2"][0], 2) + [transposed(z_s), transposed(u), glu, transposed(w_out)])
    assert slabs.shape == (N_SLABS, 128, SLAB), slabs.shape

    col = lambda v: v.reshape(-1, 128).T
    ada = lambda m: m.T.reshape(-1, 128, D)
    A = {"slabs": slabs, "ada": np.concatenate([ada(a["ada_w"][0]), ada(a["ada_w"][1]), ada(a["w_ada_2"][0])]),
         "xT": a["x"][0].T.reshape(KT, 128, T).transpose(1, 0, 2), "ident": np.eye(128),
         "norm_g": np.stack([col(a["norm_mix"][0]), col(a["norm_ffn"][0]), col(a["norm_mix"][1]), col(a["norm_ffn"][1]),
                             col(a["norm_g_2"][0])], 1),
         "mod_b": np.concatenate([col(a["ada_b"][0]), col(a["ada_b"][1]), col(a["b_ada_2"][0])], 1),
         "aqk_g": np.stack([np.tile(a["a_q_gain"][0], 2), np.tile(a["a_k_gain"][0], 2)], 1),
         "bv_g": col(a["b_v_gain"][0]), "c": np.concatenate([a["c"], a["c_2"]])}
    p, y = np.arange(128)[:, None], np.arange(T)[None, :]
    bias = a["a_rel_bias"][0][:, np.clip(p - y + 384, -63, 256) + 63]
    bias[:, (p < 64) & (y >= 448)] = -BIG
    A["a_bias"] = bias
    A["b_ws"] = a["b_w_s"][0].transpose(2, 0, 1)
    A["b_bs"] = a["b_b_s"]
    t = np.arange(T)
    tiles = lambda m: m.reshape(TT, 128, -1).transpose(1, 0, 2)
    A["h_cmask"] = tiles(np.where(np.arange(CMP_PAD)[None, :] * 16 + 31 <= t[:, None], 0.0, -BIG))
    A["h_cmask"][:, :, CMP_N] = -BIG
    A["h_flag"] = tiles((t >= 31)[:, None])[:, :, 0]
    A["h_mask"] = np.where(y - 384 <= p, 0.0, -BIG)
    inv = 1.0 / (10000.0 ** (np.arange(0, HD, 2, dtype=np.float32) / HD))
    ang = (t[:, None].astype(np.float32) * inv[None, :].astype(np.float32)).astype(np.float32)
    A["cos"], A["sin"] = tiles(np.cos(ang)), tiles(np.sin(ang))
    rows = lambda v, n=128: np.broadcast_to(v, (n,) + v.shape)
    A["qg_b"] = rows(a["q_norm_g_2"][0])
    ks, kw = a["k_slc_norm_g_2"][0], a["k_win_norm_g_2"][0]
    A["kg_b"] = rows(np.stack([ks, ks, kw, kw]))
    A["kcg_b"] = rows(a["k_cmp_norm_g_2"][0], CMP_PAD)
    A["wg"] = heads(g_br, 3).reshape(KT, 128, 24).transpose(1, 0, 2)
    A["posT"] = np.tile(np.stack([a["cmp_pos_k_2"][0].T, a["cmp_pos_v_2"][0].T], 1), (2, 1, 1))
    A["w2c"] = np.stack([a[f"cmp_w2_{x}_2"][0].reshape(2, 128, 64).transpose(1, 0, 2) for x in "kv"], 1)
    A["glu_b"] = col(a["glu_b_2"][0])
    half = np.repeat([-1.0, 1.0], 64)
    A["sgn"] = np.stack([half, -half], 1)
    A["s5_ar"] = np.tile(a["ssm_a_re_2"][0].T, (2, 1))
    A["s5_ai"] = np.tile(a["ssm_a_im_2"][0].T, (2, 1))
    A["s5_dt"] = rows(a["ssm_log_dt_2"][0])
    b_re, b_im = (a[f"ssm_b_{x}_2"][0].transpose(1, 0, 2) for x in ("re", "im"))
    c_re, c_im = (a[f"ssm_c_{x}_2"][0].transpose(2, 0, 1) for x in ("re", "im"))
    A["Bo"], A["Bx"] = np.concatenate([b_re, b_im]), np.concatenate([b_im, b_re])
    A["Co"], A["Cx"] = np.concatenate([c_re, c_im]), np.concatenate([c_im, c_re])
    dsk = np.zeros((CH, G_ALL, CH), np.float32)
    dsk[np.arange(CH), :, np.arange(CH)] = a["ssm_d_2"][0].reshape(G_ALL, CH).T
    A["dsk"] = dsk

    nc = _bacc.Bacc("TRN2", target_bir_lowering=False, num_devices=1)
    arrays, I = {}, {}
    for name, v in A.items():
        v = f(v)
        arrays[f"in_{name}"] = v
        I[name] = nc.dram_tensor(f"in_{name}", v.shape, F32, kind="ExternalInput").ap()
    out = nc.dram_tensor("out_x", (128, KT, T), F32, kind="ExternalOutput").ap()
    program(nc, I, out)
    r = _run(nc, [arrays], core_ids=[0])
    y = np.asarray(r.results[0]["out_x"])
    return np.ascontiguousarray(y.transpose(1, 0, 2).reshape(D, T).T).reshape(1, T, D)
```

```python
import concourse.bass as bass
from concourse import mybir
from concourse.alu_op_type import AluOpType as ALU
from contextlib import ExitStack
import math

F32 = mybir.dt.float32
F32R = mybir.dt.float32r
ACT = mybir.ActivationFunctionType
AX = mybir.AxisListType

P = 128
T = 512
D = 1024
KT = D // P
TT = T // P
SLAB = 2048
BIG = 1e30
EPS = 1e-6

N_QKV = 12
N_AOUT = 4
N_FFN = 32
N_BV = 12
N_BUO = 24
QUARTERS = 4
CHUNKS = 3
S_QKV = 0
S_AOUT = S_QKV + N_QKV
S_FFN0 = S_AOUT + N_AOUT
S_BV = S_FFN0 + N_FFN
S_BUO = S_BV + N_BV
S_FFN1 = S_BUO + N_BUO
S_HQ = S_FFN1 + N_FFN
S_HKV = S_HQ + 2
S_HCR = S_HKV + 2
S_HCK = S_HCR + 2
S_HCV = S_HCK + 3
S_HU = S_HCV + 4
S_HGLU = S_HU + 2
S_HOUT = S_HGLU + 1
N_SLABS = S_HOUT + 4
ADA_TILES = 48
ADA2_TILES = 24
N_ADA = 2 * ADA_TILES + ADA2_TILES
ADA_FIRST = 12

ADA_QKV = 16

A_HEADS, HD = 16, 64
SG_HALF, SG_GROUPS = 3072, 8
H_HEADS, H_GROUPS, N_BR = 8, 2, 3
CMP_N, CMP_PAD = 31, 32
G_ALL, CH, ST, L = 32, 16, 64, 8
NCH = T // L
GB = 8
NBLK = G_ALL // GB
TAPS = L + 1
ZPAD = (L - 1) * CH
S5_IN = 3 * GB + 4 * GB * CH + 2
TAB = dict(Hc=GB * TAPS * CH, Hs=GB * TAPS * CH, Gt=GB * 2 * P, Er=GB * NCH, Ei=GB * NCH, r8=GB)
TAB_W = sum(TAB.values())


def program(nc, I, out, tab_d, tz_d):
    ctx = ExitStack()
    with ctx:
        sems = {}

        def sem(name):
            if name not in sems:
                sems[name] = ctx.enter_context(nc.semaphore(name))
            return sems[name]

        def sb(name, shape, dt=F32):
            return ctx.enter_context(nc.sbuf_tensor(name, shape, dt))

        ARENA = nc.sbuf_base + 31 & ~31
        placed = [0]

        def at(name, offset, shape, dt=F32):
            size = 4 * math.prod(shape[1:])
            assert ARENA + offset + size <= nc.sbuf_usable_end, (name, offset, size)
            return nc.alloc_sbuf_tensor_at(name, shape, dt, offset=ARENA + offset)

        def seq(name, shape, dt=F32):
            o = placed[0]
            placed[0] += 4 * math.prod(shape[1:]) + 31 & ~31
            return at(name, o, shape, dt)

        K = 1024
        placed[0] = 109 * K
        xT = seq("xT", [P, KT, T])
        h_hi = seq("h_hi", [P, KT, T], F32R)
        h_lo = seq("h_lo", [P, KT, T], F32R)
        assert placed[0] == 157 * K
        w_raw = seq("w_raw", [P, 2, SLAB])
        w_hi = seq("w_hi", [P, SLAB], F32R), seq("w_hi1", [P, SLAB], F32R)
        w_lo = seq("w_lo", [P, SLAB], F32R), seq("w_lo1", [P, SLAB], F32R)
        mod = seq("mod", [P, N_ADA])
        mod_b = seq("mod_b", [P, N_ADA])
        mod_s = seq("mod_s", [P, 16])
        norm_g = seq("norm_g", [P, 5, KT])
        mod_a = seq("mod_a", [P, KT])
        ident = seq("ident", [P, P])
        ones = seq("ones", [P, P])
        eps = seq("eps", [P, 1])
        rstd = seq("rstd", [P, 32])
        stat = seq("stat", [P, 32])
        aqk_g = seq("aqk_g", [P, 2])
        bv_g = seq("bv_g", [P, SG_HALF // P])
        neg_max = seq("neg_max", [P, 8])
        row_sum = seq("row_sum", [P, 8])
        row_inv = seq("row_inv", [P, 8])
        vss = seq("vss", [P, TT, 6])
        ada_raw = at("ada_raw", 93 * K, [P, 2, D])
        cond = at("cond", 101 * K, [P, 2, D])
        ada_first = at("ada_first", 44 * K, [P, ADA_FIRST, D])
        sq_x = at("sq_x", 40 * K, [P, 2, T])
        diag = at("diag", 16 * K, [P, TT, P])
        pre = at("pre", 18 * K, [P, KT, T])
        hid_hi = at("hid_hi", 0, [P, KT, T], F32R)
        hid_lo = at("hid_lo", 16 * K, [P, KT, T], F32R)
        relu = at("relu", 32 * K, [P, 2, T])
        relu2 = at("relu2", 36 * K, [P, 2, T])
        a_qT = at("a_qT", 0, [P, A_HEADS // 2, T])
        a_kT = at("a_kT", 16 * K, [P, A_HEADS // 2, T])
        a_v = at("a_v", 32 * K, [P, TT, D])
        a_qn = at("a_qn", 48 * K, [P, 2, TT, 512])
        a_sq = at("a_sq", 64 * K, [P, TT, 512])
        a_o = at("a_o", 76 * K, [P, TT, D])
        a_bias = at("a_bias", 48 * K, [P, 3, T])
        a_s = at("a_s", 54 * K, [P, 3, T])
        a_p = at("a_p", 60 * K, [P, 4, T])
        a_pt = at("a_pt", 68 * K, [P, 3, T])
        b_v = at("b_v", 0, [P, TT, SG_HALF])
        g_hi = at("g_hi", 48 * K, [P, KT, T], F32R)
        g_lo = at("g_lo", 64 * K, [P, KT, T], F32R)
        b_ws = at("b_ws", 80 * K, [P, SG_GROUPS, P])
        b_bs = at("b_bs", 84 * K, [P, SG_GROUPS, P])
        b_u = at("b_u", 88 * K, [P, T])
        b_vm = at("b_vm", 90 * K, [P, T])
        za = at("za", 0, [P, 4, T])
        zs = at("zs", 8 * K, [P, 4, T])
        uT = at("uT", 16 * K, [P, 4, T])
        hq = at("hq", 24 * K, [P, 4, T])
        hqr = at("hqr", 32 * K, [P, 4, T])
        hk = at("hk", 40 * K, [P, 2, T])
        hv = at("hv", 44 * K, [P, TT, 256])
        h_p = at("h_p", 48 * K, [P, 4, T])
        h_pt = at("h_pt", 56 * K, [P, 3, T])
        h_s = at("h_s", 62 * K, [P, 3, T])
        h_o = at("h_o", 72 * K, [P, TT, 512])
        h_qn = at("h_qn", 48 * K, [P, TT, 512])
        h_sq = at("h_sq", 56 * K, [P, TT, 512])
        h_qr = at("h_qr", 56 * K, [P, TT, 512])
        h_kn = at("h_kn", 64 * K, [P, TT, 256])
        h_kr = at("h_kr", 68 * K, [P, TT, 256])
        h_t1 = at("h_t1", 72 * K, [P, TT, 8, 32])
        h_t2 = at("h_t2", 76 * K, [P, TT, 8, 32])
        crT = at("crT", 72 * K, [P, 2, T])
        bl_hi = at("bl_hi", 76 * K, [P, 16, 2 * CMP_PAD], F32R)
        bl_lo = at("bl_lo", 80 * K, [P, 16, 2 * CMP_PAD], F32R)
        bl = at("bl", 84 * K, [P, 16, 2 * CMP_PAD])
        h_mask = at("h_mask", 88 * K, [P, T])
        placed[0] = 93 * K
        h_cmask = seq("h_cmask", [P, TT, CMP_PAD])
        h_gts = seq("h_gts", [P, TT, N_BR * H_HEADS])
        h_flag = seq("h_flag", [P, TT])
        kcT = seq("kcT", [P, CMP_PAD])
        vc = seq("vc", [CMP_PAD, H_GROUPS, HD])
        wbr = seq("wbr", [P, 4])
        cos = seq("cos", [P, TT, 32])
        sin = seq("sin", [P, TT, 32])
        qg_b = seq("qg_b", [P, HD])
        kg_b = seq("kg_b", [P, 4, HD])
        wg = seq("wg", [P, KT, 24])
        wg_hi = seq("wg_hi", [P, KT, 24], F32R)
        wg_lo = seq("wg_lo", [P, KT, 24], F32R)
        posT = seq("posT", [P, 2, 32])
        w2c = seq("w2c", [P, 2, 2, HD])
        hdn = seq("hdn", [P, 2, 2, 2 * CMP_PAD])
        kcn = seq("kcn", [CMP_PAD, H_GROUPS, HD])
        kcsq = seq("kcsq", [CMP_PAD, H_GROUPS, HD])
        kcg_b = seq("kcg_b", [CMP_PAD, HD])
        kst = seq("kst", [CMP_PAD, 4])
        glu_b = seq("glu_b", [P, 4])
        assert placed[0] <= 109 * K, placed
        placed[0] = 44 * K
        s5_in = seq("s5_in", [P, S5_IN])
        s5_tab = seq("s5_tab", [P, TAB_W])
        PAR = ["xr", "th", "kk", "r1", "sn", "cs", "h2", "nr", "d2", "fr", "fs", "t1", "t2", "t3", "er", "ei"]
        par = {x: seq("s5_" + x, [P, GB]) for x in PAR}
        Lr = seq("Lr", [P, TAPS, GB])
        Ls = seq("Ls", [P, TAPS, GB])
        Lr1 = seq("Lr1", [P, TAPS, GB])
        Ls1 = seq("Ls1", [P, TAPS, GB])
        LrR = seq("LrR", [P, L, GB])
        LsR = seq("LsR", [P, L, GB])
        t_a = seq("t_a", [P, GB, TAPS * CH])
        t_b = seq("t_b", [P, GB, TAPS * CH])
        Gb = seq("Gb", [P, GB, L * CH])
        bbo = seq("bbo", [P, GB, CH])
        bbx = seq("bbx", [P, GB, CH])
        KTp = seq("KTp", [CH, GB, ZPAD + L * CH])
        dsk = seq("dsk", [CH, GB, CH])
        assert placed[0] <= 93 * K, placed

        def parts(tile, sizes):
            o, cut = 0, {}
            for name, n in sizes.items():
                cut[name] = tile[:, o:o + n]
                o += n
            return cut

        def tables(tile):
            cut = parts(tile, TAB)
            return {name: v if name == "r8" else v.rearrange("p (g n) -> p g n", g=GB) for name, v in cut.items()}

        s5_i = parts(s5_in, dict(ar=GB, ai=GB, dt=GB, Bo=GB * CH, Bx=GB * CH, Co=GB * CH, Cx=GB * CH, sgn=2))
        s5_i = {n: v.rearrange("p (g c) -> p g c", c=CH) if n[0] in "BC" else v for n, v in s5_i.items()}
        tab = tables(s5_tab)
        s5_t = at("s5_t0", 125 * K, [P, TAB_W]), at("s5_t1", 16 * K, [P, TAB_W])
        Tz = at("Tz0", 125 * K + 4 * TAB_W, [P, GB, L * CH]), at("Tz1", 16 * K + 4 * TAB_W, [P, GB, L * CH])
        U = at("U", 125 * K, [NCH, G_ALL, L * CH])
        UT = at("UT", 80 * K, [P, G_ALL, NCH])
        y_nat = at("y_nat0", 0, [NCH, 2, L, P]), at("y_nat1", 72 * K, [NCH, 2, L, P])
        v_a = at("v_a", 42 * K, [P, GB, NCH])
        v_b = at("v_b", 44 * K, [P, GB, NCH])
        v_c = at("v_c", 90 * K, [P, GB, NCH])
        wst = at("wst", 88 * K, [P, GB, NCH])
        h_gate = at("h_gate", 42496, [P, 2, T])
        o_hi = at("o_hi", 46 * K, [P, 4, T], F32R)
        o_lo = at("o_lo", 54 * K, [P, 4, T], F32R)
        yT = at("yT", 62 * K, [P, 4, T])
        y_hi = at("y_hi", 80 * K, [P, 4, T], F32R)
        y_lo = at("y_lo", 32 * K, [P, 4, T], F32R)
        sg_t = at("sg_t", 24 * K, [P, 2, T])
        mx_t = at("mx_t", 28 * K, [P, 2, T])

        ps = [ctx.enter_context(nc.psum_tensor(f"ps{b}", [P, 512], F32)) for b in range(8)]
        block = ctx.enter_context(nc.Block())

        class Count:

            def __init__(self):
                self.at, self.turn, self.reg = {}, {}, None

            def __call__(self, name, more=0):
                n = self.at.get(name, 0) + more
                return n if self.reg is None or not self.turn.get(name) else self.reg * self.turn[name] + n

            def add(self, name, n=1):
                self.at[name] = self.at.get(name, 0) + n
                return self(name)

            def base(self, name):
                return self.at.get(name, 0)

            def loop(self, eng, turns, turn):
                self.turn, before = turn, dict(self.at)
                with eng.Fori(0, turns) as reg:
                    self.reg = reg
                    yield reg
                for name, n in self.at.items():
                    assert n - before.get(name, 0) == turn.get(name, 0), (name, n - before.get(name, 0), turn.get(name, 0))
                    self.at[name] = before.get(name, 0) + turns * turn.get(name, 0)
                self.reg, self.turn = None, {}

        def ps_of(c):
            return ps[c.base("bank") % 8]

        def wait(eng, name, value):
            if not isinstance(value, int) or value > 0:
                eng.wait_ge(sem(name), value)

        A_WALK = [("p", 0), ("p", 1), ("x", 0), ("p", 2), ("x", 1), ("p", 3), ("x", 2), ("v", 0), ("x", 3)]
        UNITS_A = [(h, it) for h in range(A_HEADS) for it in range(TT)]
        UNITS_H = [(i, g, it, br) for i in range(4) for g in range(H_GROUPS) for it in range(TT) for br in range(N_BR)]
        NUA, NUH = len(UNITS_A), len(UNITS_H)

        class Side:

            def __init__(self, per, uses):
                self.per, self.uses, self.steps = per, uses, -(-KT // per) + 1

            def tiles(self, s):
                u, r = divmod(s, self.steps)
                return (u, range(r * self.per, min(KT, (r + 1) * self.per))) if u < 2 * self.uses else (0, ())

            def copy(self, s):
                u, r = divmod(s, self.steps)
                return u if r == self.steps - 1 and u < 2 * self.uses else None

            def slab(self, s):
                return s % (self.uses * self.steps) == 0 and s < 2 * self.uses * self.steps

        SIDE_A, SIDE_H = Side(3, TT), Side(2, 2)
        U_STEP, U_USES = 22, 12

        def u_use(s):
            v, r = divmod(s - U_STEP, 3)
            return v if r == 0 and 0 <= v < U_USES else None

        @block.sync
        def _(sp):
            q = ADA_FIRST // 4
            for i in range(4):
                sp.dma_start(ada_first[:, q * i:q * (i + 1), :], I["ada"][q * i:q * (i + 1)].rearrange("k p d -> p k d"))\
                  .then_inc(sem(f"first_in{i}"), 16)
                if i == 1:
                    for name, tile in (("xT", xT), ("ident", ident), ("norm_g", norm_g), ("mod_b", mod_b), ("aqk_g", aqk_g),
                                       ("bv_g", bv_g)):
                        sp.dma_start(tile[:], I[name]).then_inc(sem("consts_in"), 16)
            for s in range(2):
                sp.dma_start(w_raw[:, s, :], I["slabs"][s]).then_inc(sem(f"raw_in{s}"), 16)
            with sp.Fori(1, N_SLABS // 2) as i:
                for s in range(2):
                    sp.wait_ge(sem("lo_done"), i * 2 + (s - 1))
                    sp.dma_start(w_raw[:, s, :], I["slabs"][i * 2 + s]).then_inc(sem(f"raw_in{s}"), 16)
            for m in range(KT):
                sp.wait_ge(sem("x_final"), m + 1)
                sp.dma_start(out[:, m, :], xT[:, m, :]).then_inc(sem("stored"), 16)
            sp.wait_ge(sem("stored"), 16 * KT)

        @block.gpsimd
        def _(gp):
            for s in range(2):
                gp.dma_start(cond[:, s, :], I["c"][s:s + 1, :].to_broadcast([P, D])).then_inc(sem("c_in"), 16)
            gp.memset(ones[:], 1.0).then_inc(sem("ones_set"), 1)
            gp.memset(eps[:], EPS).then_inc(sem("ones_set"), 1)

            def ada(k0, k1):
                for k in range(k0, k1):
                    if k >= ADA_FIRST + 2:
                        gp.wait_ge(sem("ada_used"), k - 1)
                    gp.dma_start(ada_raw[:, k % 2, :], I["ada"][k]).then_inc(sem(f"ada_in{k % 2}"), 16)

            ada(ADA_FIRST, 16 + ADA_QKV)
            gp.wait_ge(sem("acc_free"), 2 + 4 * len(A_WALK))
            for h in range(A_HEADS + 2):
                if h < A_HEADS:
                    if h >= 3:
                        gp.wait_ge(sem("s_done"), TT * (h - 2))
                    gp.dma_start(a_bias[:, h % 3, :], I["a_bias"][h]).then_inc(sem(f"bias_in{h % 3}"), 16)
                if h >= 2:
                    ada(16 + ADA_QKV + h - 2, 16 + ADA_QKV + h - 1)
            with gp.Fori(0, ADA_TILES // 2) as i:
                for s in range(2):
                    gp.wait_ge(sem("ada_used"), i * 2 + (ADA_TILES + s - 1))
                    gp.dma_start(ada_raw[:, s, :], I["ada"][i * 2 + (ADA_TILES + s)]).then_inc(sem(f"ada_in{s}"), 16)
            gp.wait_ge(sem("slab_used"), S_BV)
            gp.dma_start(b_ws[:], I["b_ws"]).then_inc(sem("bws_in"), 16)
            gp.dma_start(b_bs[:], I["b_bs"][0:1].to_broadcast([P, SG_GROUPS, P])).then_inc(sem("bws_in"), 16)
            gp.wait_ge(sem("slab_used"), S_FFN1)
            tiles = ADA2_TILES // QUARTERS
            with gp.Fori(0, NBLK) as blk:
                gp.dma_start(s5_in[:], I["s5_in"][blk]).then_inc(sem("s5_in"), 16)
                gp.dma_start(dsk[:], I["dsk"][blk]).then_inc(sem("s5_in"), 16)
                for j in range(tiles):
                    gp.wait_ge(sem("ada_used"), blk * tiles + (2 * ADA_TILES + j - 1))
                    gp.dma_start(ada_raw[:, j % 2, :], I["ada"][blk * tiles + (2 * ADA_TILES + j)]).then_inc(sem(f"ada_in{j % 2}"), 16)
                gp.wait_ge(sem("ktp_done"), blk + 1)
                for j in range(L):
                    gp.dma_start(tz_d[blk][CH * j:CH * (j + 1)], KTp[:, :, ZPAD - CH * j:ZPAD - CH * j + L * CH])\
                      .then_inc(sem("s5_stored"), 16)
                gp.wait_ge(sem("tab_done"), blk + 1)
                gp.dma_start(tab_d[blk], s5_tab[:]).then_inc(sem("s5_stored"), 16)
            gp.wait_ge(sem("ada_used"), N_ADA)
            gp.wait_ge(sem("s5_stored"), 16 * (L + 1) * NBLK)
            small = [("h_cmask", h_cmask), ("h_flag", h_flag), ("cos", cos), ("sin", sin), ("qg_b", qg_b), ("kg_b", kg_b),
                     ("wg", wg), ("posT", posT), ("w2c", w2c), ("kcg_b", kcg_b), ("h_mask", h_mask), ("glu_b", glu_b)]
            for name, tile in small:
                gp.dma_start(tile[:], I[name]).then_inc(sem("h_in"), 16)
            for b in range(NBLK):
                if b == 0:
                    gp.wait_ge(sem("side_free"), 2 * (SIDE_A.uses + SIDE_H.uses) + U_USES)
                elif b == 1:
                    gp.wait_ge(sem("ho_done"), NUH)
                else:
                    gp.wait_ge(sem("y_mm"), 2 * (b - 1))
                gp.dma_start(s5_t[b % 2][:], tab_d[b]).then_inc(sem(f"tab_in{b % 2}"), 16)
                gp.dma_start(Tz[b % 2][:], tz_d[b]).then_inc(sem(f"tab_in{b % 2}"), 16)

        @block.tensor
        def _(pe):
            c = Count()
            mm = nc.tensor.matmul

            def bank(full=False):
                wait(pe, "acc_free", c("bank", -7))
                b = ps_of(c)
                c.add("bank")
                return b

            def three(o, w, x, start, stop, weights_move=False):
                for n, (a, b) in enumerate(((0, 0), (0, 1), (1, 0))):
                    l, r = (x[a], w[b]) if weights_move else (w[a], x[b])
                    last = mm(o, l, r, start=start and n == 0, stop=stop and n == 2)
                return last

            def slab_t(x, nk=KT, tiles=2, ready=None, first=True, final=True, after=None, banks=None, n=T):
                s = c.base("slab") % 2
                wait(pe, "lo_done", c("slab", 1))
                for m in range(tiles):
                    b = banks[m] if banks else bank()
                    for k in range(nk):
                        if ready and m == 0:
                            pe.wait_ge(sem(ready[0]), c(ready[1], k + 1))
                        if x is H and c.reg is None:
                            h_ready(k)
                        cols = slice((k * tiles + m) * P, (k * tiles + m + 1) * P)
                        last = three(b[:, 0:n], (w_hi[s][:, cols], w_lo[s][:, cols]), (x[0](k), x[1](k)),
                                     first and k == 0, final and k == nk - 1)
                    last.then_inc(sem("slab_used" if m == tiles - 1 else "acc_full"), 1)
                    if after:
                        after(m)
                if ready:
                    c.add(ready[1], nk)
                c.add("slab")

            def tile_of(hi, lo):
                return (lambda k: hi[:, k, :]), (lambda k: lo[:, k, :])

            H = tile_of(h_hi, h_lo)

            def panel_natural():
                bs = [bank() for _ in range(TT)]
                for half in range(2):
                    s = c.base("slab") % 2
                    wait(pe, "lo_done", c("slab", 1))
                    for t in range(TT):
                        ts = slice(t * P, (t + 1) * P)
                        for kk in range(4):
                            k, cols = 4 * half + kk, slice(kk * 512, (kk + 1) * 512)
                            h_ready(k)
                            last = three(bs[t][:], (w_hi[s][:, cols], w_lo[s][:, cols]), (h_hi[:, k, ts], h_lo[:, k, ts]),
                                         k == 0, k == KT - 1, weights_move=True)
                        if t == TT - 1:
                            last.then_inc(sem("slab_used"), 1)
                        elif half:
                            last.then_inc(sem("acc_full"), 1)
                    c.add("slab")

            def sums(k):
                if k == 0:
                    c.add("norm")
                    norm_bank[0] = bank()
                pe.wait_ge(sem("nsq"), KT * (c.base("norm") - 1) + k + 1)
                for t in range(TT):
                    last = mm(norm_bank[0][:, t:t + 1], sq_x[:, k % 2, t * P:(t + 1) * P], ones[:, 0:1], start=k == 0 and t == 0,
                              stop=k == KT - 1, skip_group_check=True)
                last.then_inc(sem("nsum"), 1)

            norm_bank = [None]

            def spread():
                pe.wait_ge(sem("ndiag"), TT * c("norm"))
                b = bank()
                for t in range(TT):
                    last = mm(b[:, t * P:(t + 1) * P], ones[:], diag[:, t, :], start=True, stop=True)
                last.then_inc(sem("nbc"), 1)
                h_base[0] = KT * (c.base("norm") - 1)
                h_seen[0] = 0

            h_base, h_seen = [0], [0]

            def h_ready(k):
                if h_seen[0] <= k:
                    pe.wait_ge(sem("nlo"), h_base[0] + k + 1)
                    h_seen[0] = k + 1

            def down_and_sums(x, ready=None, stage=None):
                for s in range(4):
                    def after(m, s=s):
                        if 2 * s + m >= 2:
                            sums(2 * s + m - 2)
                    if stage:
                        stage(4 + s)
                    slab_t(x, ready=ready if s == 0 else None, after=after)
                sums(KT - 2)
                sums(KT - 1)
                spread()

            def transposes(src, signal, parts=P):
                b, col = bank(), 0
                for a in src:
                    w = a.shape[0]
                    last = nc.tensor.transpose(b[0:a.shape[-1], col:col + w], a, ident[0:w, 0:w])
                    col += w
                last.then_inc(sem(signal), 1)

            def attention(units, score, value, pre, extra=lambda s: None):
                U = len(units)
                for s in range(U + 4):
                    if s < U:
                        if s >= 3:
                            pe.wait_ge(sem(pre + "s_done"), s - 2)
                        q, k, n = score(units[s])
                        mm(ps[s % 3][:, 0:n], q, k, start=True, stop=True).then_inc(sem(pre + "s_full"), 1)
                    u = s - 3
                    if 0 <= u < U:
                        pe.wait_ge(sem(pre + "p_ready"), u + 1)
                        if u >= 2:
                            pe.wait_ge(sem(pre + "pt_ready"), u - 1)
                        n = score(units[u])[2]
                        b, pt = ps[3 + u % 2], (a_p if pre == "" else h_p)
                        for j in range(0, n, P):
                            w = min(P, n)
                            last = nc.tensor.transpose(b[0:w, j:j + P], pt[:, u % 4, j:j + w], ident[:])
                        last.then_inc(sem(pre + "t_full"), 1)
                    u = s - 4
                    if 0 <= u < U:
                        pe.wait_ge(sem(pre + "pt_ready"), u + 1)
                        if u >= 2:
                            pe.wait_ge(sem(pre + "o_done"), u - 1)
                        n = score(units[u])[2]
                        pt, nb = (a_pt if pre == "" else h_pt), max(1, n // P)
                        for j in range(nb):
                            w = min(P, n)
                            last = mm(ps[5 + u % 2][:, 0:HD], pt[0:w, u % 3, j * P:(j + 1) * P], value(units[u], j), start=j == 0, stop=j == nb - 1)
                        last.then_inc(sem(pre + "o_full"), 1)
                    extra(s)

            base = [0]

            def side(plan, s, pair):
                u, ks = plan.tiles(s)
                sl = c.base("slab") % 2
                if plan.slab(s):
                    wait(pe, "lo_done", c("slab", 1))
                for k in ks:
                    if k == 0:
                        wait(pe, "side_free", base[0])
                        base[0] += 1
                    o, w, x, move = pair(u, k, sl)
                    last = three(o, w, x, k == 0, k == KT - 1, weights_move=move)
                    if k == KT - 1:
                        last.then_inc(sem("slab_used" if u % plan.uses == plan.uses - 1 else "acc_full"), 1)
                        if u % plan.uses == plan.uses - 1:
                            c.add("slab")

            def s5_stage(s):
                if s == 4:
                    pe.wait_ge(sem("gb_done"), c("blk", 1))
                    for q in range(4):
                        transposes([Gb[:, 2 * q + g, :] for g in range(2)], "gb_full")
                elif s == 5:
                    pe.wait_ge(sem("hc_done"), c("blk", 1))
                    for q in range(4):
                        b = bank()
                        for g in range(2):
                            last = mm(b[0:CH, g * P:(g + 1) * P], bbo[:, 2 * q + g, :], tab["Hc"][:, 2 * q + g, 0:L * CH],
                                      start=True, stop=True)
                        last.then_inc(sem("kt_full"), 1)

            def ffn(stage=None):
                turn = dict(slab=8, bank=24 if stage else 16, hid=KT, blk=1 if stage else 0)
                hid = tile_of(hid_hi, hid_lo)
                for part in range(3):
                    for _ in (c.loop(pe, QUARTERS - 2, turn) if part == 1 else range(1)):
                        for _ in range(4):
                            slab_t(H)
                        if part == 2:
                            down_and_sums(hid, ready=("hid_lo_done", "hid"), stage=stage)
                        else:
                            for s in range(4):
                                if stage:
                                    stage(4 + s)
                                slab_t(hid, ready=("hid_lo_done", "hid") if s == 0 else None)
                        c.add("blk", 1 if stage else 0)

            pe.wait_ge(sem("consts_in"), 96)
            pe.wait_ge(sem("ones_set"), 2)
            for k in range(KT):
                sums(k)
            spread()
            for kind, p in A_WALK:
                if kind != "x":
                    panel_natural()
                else:
                    pe.wait_ge(sem("qn_done"), p + 1)
                    for b in range(4):
                        transposes([a_qn[:, p % 2, t, b * P:(b + 1) * P] for t in range(TT)], "xp_full")
            pe.wait_ge(sem("acc_free"), c("bank"))

            def score_a(u):
                h, it = u
                r = slice(HD * (h % 2), HD * (h % 2) + HD)
                return a_qT[r, h // 2, it * P:(it + 1) * P], a_kT[r, h // 2, 0:P * (it + 1)], P * (it + 1)

            def value_a(u, j):
                if u == (8, 0):
                    pe.wait_ge(sem("side_free"), 2 * TT)
                return a_v[:, j, u[0] * HD:(u[0] + 1) * HD]

            def pair_a(u, k, sl):
                t, cols = u % TT, slice(k * 256, (k + 1) * 256)
                return (ps[7][:, 0:256], (w_hi[sl][:, cols], w_lo[sl][:, cols]),
                        (h_hi[:, k, t * P:(t + 1) * P], h_lo[:, k, t * P:(t + 1) * P]), True)

            attention(UNITS_A, score_a, value_a, "", lambda s: side(SIDE_A, s, pair_a))
            pe.wait_ge(sem("o_done"), NUA)
            for i in range(KT):
                transposes([a_o[:, t, i * P:(i + 1) * P] for t in range(TT)], "xo_full")
            pe.wait_ge(sem("xo_lo"), KT)
            down_and_sums(H)
            ffn()

            for _ in range(6):
                panel_natural()
            pe.wait_ge(sem("bws_masked"), 1)
            for ch in range(CHUNKS):
                for s in range(4):
                    def mix(m):
                        gm = KT * ch + 2 * s + m
                        if gm == 0:
                            pe.wait_ge(sem("bv_scaled"), TT)
                        b = bank()
                        for t in range(TT):
                            last = mm(b[:, t * P:(t + 1) * P], b_v[:, t, gm * P:(gm + 1) * P], b_ws[:, gm // 3, :], start=True, stop=True)
                        last.then_inc(sem("mix_full"), 1)
                    slab_t(H, after=mix)
                if ch < CHUNKS - 1:
                    for s in range(4):
                        slab_t(tile_of(g_hi, g_lo), ready=("g_lo_done", "g") if s == 0 else None)
                else:
                    down_and_sums(tile_of(g_hi, g_lo), ready=("g_lo_done", "g"))
            ffn(s5_stage)

            panel_natural()
            panel_natural()
            pe.wait_ge(sem("wg_split"), 1)
            b = bank()
            for t in range(TT):
                for k in range(KT):
                    last = three(b[:, t * 24:(t + 1) * 24], (wg_hi[:, k, :], wg_lo[:, k, :]),
                                 (h_hi[:, k, t * P:(t + 1) * P], h_lo[:, k, t * P:(t + 1) * P]), k == 0, k == KT - 1, weights_move=True)
            last.then_inc(sem("gates_full"), 1)
            slab_t(H)
            slab_t(H)
            pe.wait_ge(sem("hq_done"), 1)
            for i in range(4):
                transposes([h_qn[:, t, i * P:(i + 1) * P] for t in range(TT)], "hx_full")
            for i in range(4):
                transposes([h_qr[:, t, i * P:(i + 1) * P] for t in range(TT)], "hx_full")
            pe.wait_ge(sem("hk_done"), 1)
            for i in range(2):
                transposes([h_kr[:, t, i * P:(i + 1) * P] for t in range(TT)], "hx_full")
            for kind in range(2):
                pe.wait_ge(sem("bl_done"), kind + 1)
                bs = [bank(), bank()]
                for s in range(2):
                    x = (lambda k, s=s: bl_hi[:, 8 * s + k, :]), (lambda k, s=s: bl_lo[:, 8 * s + k, :])
                    slab_t(x, banks=bs, first=s == 0, final=s == 1, n=2 * CMP_PAD)
                slab_t(H)
            pe.wait_ge(sem("hdn_done"), 2)
            b = bank()
            for kind in range(2):
                for g in range(H_GROUPS):
                    for m in range(2):
                        col = (kind * 2 + g) * HD
                        last = mm(b[0:CMP_PAD, col:col + HD], hdn[:, kind, m, g * CMP_PAD:(g + 1) * CMP_PAD], w2c[:, kind, m, :],
                                  start=m == 0, stop=m == 1)
            last.then_inc(sem("kc_full"), 1)
            slab_t(H)
            pe.wait_ge(sem("kcn_done"), 1)
            transposes([kcn[:].rearrange("n g d -> n (g d)")], "kct_full")
            pe.wait_ge(sem("acc_free"), c("bank"))

            def score_h(u):
                i, g, it, br = u
                r, ts = slice(HD * g, HD * g + HD), slice(it * P, (it + 1) * P)
                if br == 0:
                    return hq[r, i, ts], kcT[r, :], CMP_PAD
                return hqr[r, i, ts], hk[r, br - 1, 0:P * (it + 1)], P * (it + 1)

            def value_h(u, j):
                i, g, it, br = u
                return vc[:, g, :] if br == 0 else hv[:, j, (br - 1) * P + g * HD:(br - 1) * P + (g + 1) * HD]

            def pair_h(u, k, sl):
                cols = slice((2 * k + u % 2) * P, (2 * k + u % 2 + 1) * P)
                return ps[7][:], (w_hi[sl][:, cols], w_lo[sl][:, cols]), (h_hi[:, k, :], h_lo[:, k, :]), False

            def beside_h(s):
                side(SIDE_H, s, pair_h)
                v = u_use(s)
                if v is None:
                    return
                pe.wait_ge(sem("side_free"), base[0])
                base[0] += 1
                if v < 8:
                    src = [uT[:, v // 2, :].rearrange("p (n j) -> p j n", j=L)[:, 4 * (v % 2) + j, :] for j in range(4)]
                else:
                    src = [U[:, 8 * (v - 8) + g, :] for g in range(8)]
                col = 0
                for a in src:
                    w = a.shape[0]
                    last = nc.tensor.transpose(ps[7][0:a.shape[-1], col:col + w], a, ident[0:w, 0:w])
                    col += w
                last.then_inc(sem("u_full"), 1)

            attention(UNITS_H, score_h, value_h, "h", beside_h)
            pe.wait_ge(sem("ho_done"), NUH)
            for i in range(4):
                transposes([h_o[:, t, i * P:(i + 1) * P] for t in range(TT)], "hxo_full")

            pe.wait_ge(sem("side_free"), base[0])

            def states(blk):
                t = tables(s5_t[blk % 2])
                pe.wait_ge(sem(f"tab_in{blk % 2}"), 32 * (blk // 2 + 1))
                for q in range(2):
                    b = bank()
                    for g in range(GB):
                        last = mm(b[:, g * NCH:(g + 1) * NCH], t["Gt"][:, g, q * P:(q + 1) * P], UT[:, blk * GB + g, :], start=True, stop=True)
                    last.then_inc(sem("x_full"), 1)

            states(0)
            for blk in range(NBLK):
                t = tables(s5_t[blk % 2])
                pe.wait_ge(sem("st_done"), blk + 1)
                for q in range(2):
                    b = bank()
                    for g in range(4 * q, 4 * q + 4):
                        o = b[0:NCH, (g % 4) * P:(g % 4 + 1) * P]
                        mm(o, UT[:, blk * GB + g, :], Tz[blk % 2][:, g, :], start=True, stop=False)
                        mm(o, v_a[:, g, :], t["Hc"][:, g, CH:], start=False, stop=False)
                        last = mm(o, v_b[:, g, :], t["Hs"][:, g, CH:], start=False, stop=True)
                    last.then_inc(sem("y_mm"), 1)
                if blk + 1 < NBLK:
                    states(blk + 1)
            for ct in range(4):
                pe.wait_ge(sem("yn_gelu"), 2 * (ct + 1))
                transposes([y_nat[ct // 2][:, ct % 2, i, :] for i in range(L)], "yt_full")
            pe.wait_ge(sem("y_lo_done"), 4)
            slab_t(tile_of(y_hi, y_lo), nk=4, tiles=4)
            pe.wait_ge(sem("mix_lo"), 4)
            pe.wait_ge(sem("hx_done"), 4)
            mix = (lambda k: o_hi[:, k, :] if k < 4 else h_hi[:, k, :]), (lambda k: o_lo[:, k, :] if k < 4 else h_lo[:, k, :])
            for _ in range(4):
                slab_t(mix)

        @block.scalar
        def _(act):
            c = Count()
            A = nc.scalar.activation

            def split():
                n = c.base("split")
                if c.reg is None and n >= N_SLABS:
                    return
                s = n % 2
                act.wait_ge(sem(f"raw_in{s}"), (c("split", -s) if c.reg is None else c("split", -s)) * 8 + 16)
                wait(act, "slab_used", c("split", -1))
                A(w_hi[s][:], w_raw[:, s, :], ACT.Copy).then_inc(sem("hi_done"), 1)
                c.add("split")

            def full(m, tiles=2):
                if m == tiles - 1:
                    act.wait_ge(sem("slab_used"), c("slab", 1))
                else:
                    act.wait_ge(sem("acc_full"), c.add("full"))
                b = ps_of(c)
                c.add("bank")
                return b

            def skip_t(tiles=2):
                split()
                c.add("full", tiles - 1)
                c.add("bank", tiles)
                c.add("slab")

            def natural(use):
                split()
                c.add("slab")
                natural_end(use)

            def natural_end(use):
                split()
                for t in range(TT):
                    use(t, full(t, TT)) if use else (c.add("bank"), c.add("full", t < TT - 1))
                c.add("slab")

            def square(k, frees):
                if k == 0:
                    c.add("norm")
                wait(act, "acc_free", frees)
                n = KT * (c.base("norm") - 1) + k
                if n >= 2:
                    act.wait_ge(sem("nsum"), n - 1)
                A(sq_x[:, k % 2, :], xT[:, k, :], ACT.Square).then_inc(sem("nsq"), 1)

            def down_and_squares(stage=None):
                for s in range(4):
                    split()
                    if stage:
                        stage(4 + s)
                    for m in range(2):
                        if s == 1 and m == 1:
                            sum_bank[0] = ps_of(c)
                            c.add("bank")
                        c.add("bank")
                        square(2 * s + m, c.base("bank") - (2 * s + m >= 3))
                    c.add("full")
                    c.add("slab")

            sum_bank = [ps[0]]

            def norm(shift):
                n = c.base("norm")
                act.wait_ge(sem("nsum"), KT * n)
                A(stat[:, 0:TT], sum_bank[0][:, 0:TT], ACT.Sqrt, bias=eps[:], scale=1.0 / D).then_inc(sem("nstd"), 1)
                c.add("bank")
                for k in range(KT):
                    if k < KT - 1:
                        act.wait_ge(sem("npre"), (KT - 1) * (n - 1) + k + 1)
                    else:
                        act.wait_ge(sem("acc_free"), c("bank"))
                    A(h_hi[:, k, :], pre[:, k, :], ACT.Identity, bias=mod[:, shift + k:shift + k + 1]).then_inc(sem("nhi"), 1)

            def side(plan, s, place):
                if plan.slab(s):
                    split()
                u = plan.copy(s)
                if u is not None:
                    if u % plan.uses == plan.uses - 1:
                        c.add("slab")
                        act.wait_ge(sem("slab_used"), c("slab"))
                    else:
                        act.wait_ge(sem("acc_full"), c.add("full"))
                    o = place(u)
                    A(o, ps[7][:, 0:o.shape[-1]], ACT.Copy).then_inc(sem("side_free"), 1)

            def u_copy(v):
                act.wait_ge(sem("u_full"), v + 1)
                if v < 8:
                    o = U[:, 8 * (v // 2):8 * (v // 2) + 8, 64 * (v % 2):64 * (v % 2) + 64].rearrange("n g (j c) -> n j g c", c=CH)
                    A(o, ps[7][0:NCH, :].rearrange("n (j g c) -> n j g c", j=4, g=8), ACT.Copy).then_inc(sem("side_free"), 1)
                else:
                    A(UT[:, 8 * (v - 8):8 * (v - 8) + 8, :], ps[7][:].rearrange("p (g n) -> p g n", n=NCH), ACT.Copy).then_inc(sem("side_free"), 1)

            def attention(units, width, pre, plan, place):
                n_units = len(units)
                S, Pm, PT = (a_s, a_p, a_pt) if pre == "" else (h_s, h_p, h_pt)
                for s in range(n_units + 3):
                    side(plan, s, place)
                    if pre == "h" and u_use(s - 1) is not None:
                        u_copy(u_use(s - 1))
                    u = s - 3
                    if 0 <= u < n_units:
                        n = width(units[u])
                        w = min(P, n)
                        act.wait_ge(sem(pre + "t_full"), u + 1)
                        if u >= 3:
                            act.wait_ge(sem(pre + "o_full"), u - 2)
                        A(PT[0:w, u % 3, 0:max(P, n)], ps[3 + u % 2][0:w, 0:max(P, n)], ACT.Copy).then_inc(sem(pre + "pt_ready"), 1)
                    if s < n_units:
                        n = width(units[s])
                        act.wait_ge(sem(pre + "s_done"), s + 1)
                        if s >= 4:
                            act.wait_ge(sem(pre + "t_full"), s - 3)
                        if s >= 8:
                            act.wait_ge(sem(pre + "inv_done"), s - 7)
                        A(Pm[:, s % 4, 0:n], S[:, s % 3, 0:n], ACT.Exp, bias=neg_max[:, s % 8:s % 8 + 1], scale=-1.0,
                          accum_out=row_sum[:, s % 8:s % 8 + 1]).then_inc(sem(pre + "p_ready"), 1)

            def s5_stage(s):
                if s == 0:
                    act.wait_ge(sem("s5_in"), c("blk", 1) * 32)
                    A(s5_i["dt"], s5_i["dt"], ACT.Exp).then_inc(sem("dt_done"), 1)
                elif s == 1:
                    act.wait_ge(sem("ang_done"), c("blk", 1))
                    wait(act, "s5_stored", c("blk") * (16 * (L + 1)))
                    A(par["r1"][:], par["xr"][:], ACT.Exp).then_inc(sem("trig_done"), 1)
                    A(tab["r8"], par["xr"][:], ACT.Exp, scale=float(L)).then_inc(sem("trig_done"), 1)
                    A(par["sn"][:], par["th"][:], ACT.Sin).then_inc(sem("trig_done"), 1)
                    A(par["h2"][:], par["th"][:], ACT.Sin, scale=0.5).then_inc(sem("trig_done"), 1)
                elif s == 4:
                    for q in range(4):
                        act.wait_ge(sem("gb_full"), c("blk") * 4 + (q + 1))
                        src = ps_of(c)[:, 0:2 * P].rearrange("p (g m) -> p g m", m=P)
                        o = tab["Gt"][:, 2 * q:2 * q + 2, :]
                        A(o[:, :, 0:P], src, ACT.Copy)
                        A(o[:, :, P:P + ST], src[:, :, ST:P], ACT.Copy)
                        A(o[:, :, P + ST:2 * P], src[:, :, 0:ST], ACT.Copy, scale=-1.0).then_inc(sem("gt_done"), 1)
                        c.add("bank")
                elif s == 5:
                    c.add("bank", 4)

            def ffn(stage=None):
                turn = dict(slab=8, split=8, bank=24 if stage else 16, full=8, blk=1 if stage else 0)
                for part in range(3):
                    for _ in (c.loop(act, QUARTERS - 2, turn) if part == 1 else range(1)):
                        for s in range(4):
                            split()
                            if stage:
                                stage(s)
                            for m in range(2):
                                g = 2 * s + m
                                b = full(m)
                                A(relu[:, g % 2, :], b[:], ACT.Relu).then_inc(sem("relu_done"), 1)
                                if g:
                                    high(g - 1, 1)
                            c.add("slab")
                        high(KT - 1, 0)
                        if part == 2:
                            down_and_squares(stage)
                        else:
                            for s in range(4):
                                if stage:
                                    stage(4 + s)
                                skip_t()
                        c.add("blk", 1 if stage else 0)

            def high(g, behind):
                act.wait_ge(sem("acc_free"), c("bank", -behind))
                A(hid_hi[:, g, :], relu2[:, g % 2, :], ACT.Copy).then_inc(sem("hid_hi_done"), 1)

            act.wait_ge(sem("c_in"), 32)
            for s in range(2):
                A(cond[:, s, :], cond[:, s, :], ACT.Silu).then_inc(sem("cond_done"), 1)
            act.wait_ge(sem("consts_in"), 96)
            act.wait_ge(sem("ones_set"), 2)
            for k in range(KT):
                square(k, 0)
            split()
            c.add("bank")
            norm(0)
            for kind, p in A_WALK:
                if kind == "p":
                    def square_a(t, b):
                        wait(act, "a_red", p)
                        A(a_sq[:, t, :], b[:], ACT.Square).then_inc(sem("a_sq_done"), 1)
                    natural(square_a)
                    act.wait_ge(sem("a_red"), p + 1)
                    A(rstd[:], stat[:], ACT.Sqrt, bias=eps[:], scale=1.0 / HD).then_inc(sem("a_std"), 1)
                elif kind == "v":
                    natural(None)
                else:
                    c.add("bank", 4)
            attention(UNITS_A, lambda u: P * (u[1] + 1), "", SIDE_A,
                      lambda u: a_v[:, u % TT, 512 + 256 * (u // TT):768 + 256 * (u // TT)])
            for i in range(KT):
                act.wait_ge(sem("xo_full"), i + 1)
                A(h_hi[:, i, :], ps_of(c)[:], ACT.Copy).then_inc(sem("xo_hi"), 1)
                c.add("bank")
            down_and_squares()
            norm(24)
            ffn()

            norm(48)
            for p in range(6):
                natural(lambda t, b: A(b_v[:, t, p * 512:(p + 1) * 512], b[:], ACT.Gelu).then_inc(sem("bv_done"), 1))
            act.wait_ge(sem("v_red"), 1)
            A(stat[:, 0:TT], stat[:, 0:TT], ACT.Sqrt, bias=eps[:], scale=1.0 / SG_HALF).then_inc(sem("v_std"), 1)
            for ch in range(CHUNKS):
                for s in range(4):
                    split()
                    for m in range(2):
                        b = full(m)
                        wait(act, "acc_free", c("bank", -1))
                        A(b_u[:], b[:], ACT.Gelu).then_inc(sem("bu_done"), 1)
                        c.add("bank")
                        act.wait_ge(sem("acc_free"), c("bank"))
                        A(g_hi[:, 2 * s + m, :], b_vm[:], ACT.Copy).then_inc(sem("g_hi_done"), 1)
                    c.add("slab")
                if ch < CHUNKS - 1:
                    for _ in range(4):
                        skip_t()
                else:
                    down_and_squares()
            norm(72)
            ffn(s5_stage)

            norm(96)

            def square_q(t, b):
                A(h_sq[:, t, :], b[:], ACT.Square).then_inc(sem("h_sq_done"), 1)
            act.wait_ge(sem("s5_stored"), 16 * (L + 1) * NBLK)
            natural(square_q)
            act.wait_ge(sem("h_red"), 1)
            A(rstd[:], stat[:], ACT.Sqrt, bias=eps[:], scale=1.0 / HD).then_inc(sem("h_std"), 1)
            split()
            c.add("slab")
            act.wait_ge(sem("hq_done"), 1)

            def square_k(t, b):
                A(h_t1[:, t, :, :], b[:, 0:256].rearrange("p (a b) -> p a b", b=32), ACT.Square).then_inc(sem("h_sq_done"), 1)
            natural_end(square_k)
            act.wait_ge(sem("h_red"), 2)
            A(rstd[:, 0:16], stat[:, 0:16], ACT.Sqrt, bias=eps[:], scale=1.0 / HD).then_inc(sem("h_std"), 1)
            c.add("bank")
            act.wait_ge(sem("gates_copied"), 1)
            A(h_gts[:], h_gts[:], ACT.Sigmoid).then_inc(sem("gts_done"), 1)
            skip_t()
            skip_t()
            c.add("bank", 10)
            for kind in range(2):
                for _ in range(2):
                    split()
                    c.add("slab")
                c.add("full", 2)
                c.add("bank", 2)
                act.wait_ge(sem("hdn_copied"), kind + 1)
                A(hdn[:, kind, :, :], hdn[:, kind, :, :], ACT.Gelu_apprx_tanh).then_inc(sem("hdn_done"), 1)
                skip_t()
            act.wait_ge(sem("kc_red"), 1)
            A(kst[:, 0:2], kst[:, 0:2], ACT.Sqrt, bias=eps[0:CMP_PAD, :], scale=1.0 / HD).then_inc(sem("kc_std"), 1)
            skip_t()
            c.add("bank", 2)
            act.wait_ge(sem("z_copied"), 1)
            A(za[:], za[:], ACT.Silu).then_inc(sem("z_done"), 1)
            A(zs[:], zs[:], ACT.Silu).then_inc(sem("z_done"), 1)
            attention(UNITS_H, lambda u: CMP_PAD if u[3] == 0 else P * (u[2] + 1), "h", SIDE_H,
                      lambda u: uT[:, u, :])
            for i in range(4):
                act.wait_ge(sem("hxo_gated"), i + 1)
                A(o_hi[:, i, :], h_gate[:, i % 2, :], ACT.Copy).then_inc(sem("hxo_hi"), 1)
                c.add("bank")
            for blk in range(NBLK):
                c.add("bank", 2)
                for q in range(2):
                    act.wait_ge(sem("y_mm"), 2 * blk + q + 1)
                    o = y_nat[blk // 2][:, blk % 2, :, 64 * q:64 * q + 64].rearrange("n i (g c) -> n g i c", c=CH)
                    A(o, ps_of(c)[0:NCH, :].rearrange("n (g i c) -> n g i c", g=4, i=L), ACT.Gelu_apprx_tanh).then_inc(sem("yn_gelu"), 1)
                    c.add("bank")
            for ct in range(4):
                act.wait_ge(sem("yt_done"), ct + 1)
                A(y_hi[:, ct, :], yT[:, ct, :], ACT.Copy).then_inc(sem("y_hi_done"), 1)
                c.add("bank")
            split()
            for m in range(4):
                b = full(m, 4)
                if m >= 2:
                    act.wait_ge(sem("acc_free"), c("bank", -2))
                A(sg_t[:, m % 2, :], b[:], ACT.Sigmoid, bias=glu_b[:, m:m + 1]).then_inc(sem("sg_done"), 1)
                act.wait_ge(sem("mx_done"), m + 1)
                A(h_hi[:, 4 + m, :], mx_t[:, m % 2, :], ACT.Copy).then_inc(sem("mix_hi"), 1)
            c.add("slab")
            for _ in range(4):
                skip_t()

        @block.vector
        def _(dve):
            c = Count()
            V = nc.vector
            tt, ts_, stt, cp = V.tensor_tensor, V.tensor_scalar, V.scalar_tensor_tensor, V.tensor_copy

            def step(ins, *more):
                for i in (ins, *more):
                    i.then_inc(sem("dve_step"), 1)
                    c.add("step")
                dve.wait_ge(sem("dve_step"), c("step"))

            def split():
                n = c.base("split")
                if c.reg is None and n >= N_SLABS:
                    return
                s = n % 2
                dve.wait_ge(sem("hi_done"), c("split", 1))
                tt(w_lo[s][:], w_raw[:, s, :], w_hi[s][:].bitcast(F32), ALU.subtract).then_inc(sem("lo_done"), 1)
                c.add("split")

            def full(m, tiles=2):
                if m == tiles - 1:
                    dve.wait_ge(sem("slab_used"), c("slab", 1))
                else:
                    dve.wait_ge(sem("acc_full"), c.add("full"))
                b = ps_of(c)
                c.add("bank")
                return b

            def free(ins, n=1):
                ins.then_inc(sem("acc_free"), n)

            def freed():
                dve.wait_ge(sem("acc_free"), c("bank"))

            def ada(n, which):
                for _ in range(n):
                    o, s = c.base("ada") - ada_base[0], c.base("ada") % 2
                    first = c.reg is None and c.base("ada") < ADA_FIRST
                    if first:
                        dve.wait_ge(sem(f"first_in{c.base('ada') * 4 // ADA_FIRST}"), 16)
                    else:
                        dve.wait_ge(sem(f"ada_in{s}"), c("ada", -s - ADA_FIRST) * 8 + 16)
                    w = ada_first[:, c.base("ada"), :] if first else ada_raw[:, s, :]
                    V.tensor_tensor_reduce(out=w, in0=w, in1=cond[:, which, :], scale=1.0, scalar=0.0, op0=ALU.mult, op1=ALU.add,
                                           accum_out=mod_s[:, o:o + 1]).then_inc(sem("ada_used"), 1)
                    c.add("ada")

            ada_base = [0]

            def ada_put():
                n, first = c.base("ada") - ada_base[0], c("ada", ada_base[0] - c.base("ada"))
                dve.wait_ge(sem("ada_used"), c("ada"))
                tt(mod[:, bass.ds(first, n)], mod_s[:, 0:n], mod_b[:, bass.ds(first, n)], ALU.add).then_inc(sem("mod_done"), 1)
                c.add("mod")
                dve.wait_ge(sem("mod_done"), c("mod"))
                ada_base[0] = c.base("ada")

            def residual(g, extra=lambda s: None, norm_next=False):
                for s in range(4):
                    split()
                    extra(s)
                    for m in range(2):
                        o = 2 * s + m
                        if norm_next and o == 3:
                            c.add("bank")
                        b = full(m)
                        free(stt(xT[:, o, :], b[:], mod[:, g + o:g + o + 1], xT[:, o, :], ALU.mult, ALU.add))
                    c.add("slab")

            def natural(use, tiles=0):
                split()
                c.add("slab")
                ada(tiles, 0)
                natural_end(use)

            def natural_end(use):
                split()
                for t in range(TT):
                    use(t, full(t, TT))
                c.add("slab")

            def norm(i, shift):
                n = c.add("norm")
                step(stt(mod_a[:], mod[:, shift + 8:shift + 16], 1.0, norm_g[:, i, :], ALU.add, ALU.mult))
                dve.wait_ge(sem("nstd"), n)
                free(V.reciprocal(rstd[:, 0:TT], stat[:, 0:TT]))
                freed()
                for t in range(TT):
                    ts_(diag[:, t, :], ident[:], rstd[:, t:t + 1], None, ALU.mult).then_inc(sem("ndiag"), 1)
                dve.wait_ge(sem("nbc"), n)
                b = ps_of(c)
                c.add("bank")
                for k in range(KT + 2):
                    if k < KT:
                        ins = stt(pre[:, k, :], xT[:, k, :], mod_a[:, k:k + 1], b[:], ALU.mult, ALU.mult)
                        if k < KT - 1:
                            ins.then_inc(sem("npre"), 1)
                        else:
                            free(ins)
                    if k >= 2:
                        o = k - 2
                        dve.wait_ge(sem("nhi"), KT * (n - 1) + o + 1)
                        stt(h_lo[:, o, :], pre[:, o, :], mod[:, shift + o:shift + o + 1], h_hi[:, o, :].bitcast(F32), ALU.add, ALU.subtract)\
                            .then_inc(sem("nlo"), 1)

            def attention(units, width, mask, combine, pre, plan):
                U = len(units)
                S = a_s if pre == "" else h_s
                for s in range(U + 4):
                    if s < U:
                        n = width(units[s])
                        dve.wait_ge(sem(pre + "s_full"), s + 1)
                        if s >= 3:
                            dve.wait_ge(sem(pre + "p_ready"), s - 2)
                        V.tensor_tensor_reduce(out=S[:, s % 3, 0:n], in0=ps[s % 3][:, 0:n], in1=mask(units[s]), scale=-1.0,
                                               scalar=3e38, op0=ALU.add, op1=ALU.min, accum_out=neg_max[:, s % 8:s % 8 + 1])\
                         .then_inc(sem(pre + "s_done"), 1)
                    if plan.slab(s):
                        split()
                    u = s - 4
                    if 0 <= u < U:
                        dve.wait_ge(sem(pre + "p_ready"), u + 1)
                        V.reciprocal(row_inv[:, u % 8:u % 8 + 1], row_sum[:, u % 8:u % 8 + 1]).then_inc(sem(pre + "inv_done"), 1)
                        dve.wait_ge(sem(pre + "inv_done"), u + 1)
                        combine(u, units[u])

            def ffn(g, tiles, which, stage=None):
                turn = dict(slab=8, split=8, bank=24 if stage else 16, full=8, hid=KT, ada=tiles, mod=1, blk=1 if stage else 0)
                share = [(tiles * (s + 1)) // 8 - tiles * s // 8 for s in range(8)]
                steps = c.base("step")
                for part in range(3):
                    if part == 1:
                        turn["step"] = c.base("step") - steps
                    ada_base[0] = c.base("ada")
                    for _ in (c.loop(dve, QUARTERS - 2, turn) if part == 1 else range(1)):
                        quarter(g, share, which, part == 2, stage)

            def quarter(g, share, which, last, stage):
                def beside(s):
                    if stage:
                        stage(s)
                    ada(share[s], which)

                for s in range(4):
                    split()
                    beside(s)
                    for m in range(2):
                        o = 2 * s + m
                        b = full(m)
                        dve.wait_ge(sem("relu_done"), c("hid", o + 1))
                        if o >= 2:
                            dve.wait_ge(sem("hid_lo_done"), c("hid", o - 1))
                        free(stt(relu2[:, o % 2, :], b[:], 0.0, relu[:, o % 2, :], ALU.max, ALU.mult))
                        if o:
                            low(o - 1)
                    c.add("slab")
                low(KT - 1)
                c.add("hid", KT)
                residual(g, lambda s: beside(4 + s), last)
                ada_put()
                c.add("blk", 1 if stage else 0)

            def low(o):
                dve.wait_ge(sem("hid_hi_done"), c("hid", o + 1))
                tt(hid_lo[:, o, :], relu2[:, o % 2, :], hid_hi[:, o, :].bitcast(F32), ALU.subtract).then_inc(sem("hid_lo_done"), 1)

            p_ = {k: v[:] for k, v in par.items()}
            p_.update((k, s5_i[k]) for k in ("ar", "ai", "dt"))

            def m_(o, a, b, op=ALU.mult):
                return tt(p_[o], p_[a], p_[b], op)

            def over(a, n):
                return a.unsqueeze(2).to_broadcast([P, GB, n])

            def taps(a, n):
                return a.unsqueeze(2).to_broadcast([P, GB, n, CH])

            def power(a, n):
                return a[:, 0:n, :].rearrange("p n g -> p g n").unsqueeze(3).to_broadcast([P, GB, n, CH])

            def four(z, n):
                return z[:, :, 0:n * CH].rearrange("p g (n c) -> p g n c", c=CH)

            def angles():
                MAGIC, C1 = 12582912.0, 6.28125
                C2 = 2 * math.pi - C1
                PI_DOWN = 3.1415925
                dve.wait_ge(sem("dt_done"), c("blk", 1))
                step(m_("xr", "ar", "dt"), m_("th", "ai", "dt"))
                step(ts_(p_["kk"], p_["th"], 1 / (2 * math.pi), MAGIC, ALU.mult, ALU.add))
                step(ts_(p_["kk"], p_["kk"], MAGIC, None, ALU.subtract))
                step(stt(p_["t1"], p_["kk"], -C1, p_["th"], ALU.mult, ALU.add))
                step(stt(p_["th"], p_["kk"], -C2, p_["t1"], ALU.mult, ALU.add))
                ts_(p_["th"], p_["th"], PI_DOWN, -PI_DOWN, ALU.min, ALU.max).then_inc(sem("ang_done"), 1)

            def powers():
                dve.wait_ge(sem("trig_done"), c("blk", 1) * 4)
                step(m_("t1", "h2", "h2"))
                step(ts_(p_["cs"], p_["t1"], -2.0, 1.0, ALU.mult, ALU.add))
                step(V.memset(Lr[:, 0, :], 1.0), V.memset(Ls[:, 0, :], 0.0), cp(p_["er"], p_["cs"]), cp(p_["ei"], p_["sn"]),
                     tt(Lr[:, 1, :], p_["r1"], p_["cs"], ALU.mult), tt(Ls[:, 1, :], p_["r1"], p_["sn"], ALU.mult))
                for lo, n in ((2, 1), (3, 2), (5, 4)):
                    wide = lambda a: a.unsqueeze(1).to_broadcast([P, n, GB])
                    br_, bi_ = wide(Lr[:, lo - 1, :]), wide(Ls[:, lo - 1, :])
                    a_r, a_i = Lr[:, 1:1 + n, :], Ls[:, 1:1 + n, :]
                    v = [t_a[:, k, 0:n * GB].rearrange("p (a b) -> p a b", b=GB) for k in range(4)]
                    step(tt(v[0], a_r, br_, ALU.mult), tt(v[1], a_i, bi_, ALU.mult), tt(v[2], a_r, bi_, ALU.mult), tt(v[3], a_i, br_, ALU.mult),
                         m_("t1", "er", "er"), m_("t2", "ei", "ei"), m_("t3", "er", "ei"))
                    step(tt(Lr[:, lo:lo + n, :], v[0], v[1], ALU.subtract), tt(Ls[:, lo:lo + n, :], v[2], v[3], ALU.add),
                         m_("er", "t1", "t2", ALU.subtract), ts_(p_["ei"], p_["t3"], 2.0, None, ALU.mult))

            def factors():
                step(ts_(p_["nr"], Lr[:, 1, :], 1.0, None, ALU.subtract), m_("t1", "ar", "ar"), m_("t2", "ai", "ai"))
                step(m_("t3", "t1", "t2", ALU.add))
                step(V.reciprocal(p_["d2"], p_["t3"]), m_("t1", "nr", "ar"), tt(p_["t2"], Ls[:, 1, :], p_["ai"], ALU.mult),
                     tt(p_["r1"], Ls[:, 1, :], p_["ar"], ALU.mult), m_("h2", "nr", "ai"))
                step(m_("t3", "t1", "t2", ALU.add), m_("kk", "r1", "h2", ALU.subtract))
                step(m_("fr", "t3", "d2"), stt(p_["fs"], p_["kk"], s5_i["sgn"][:, 0:1], p_["d2"], ALU.mult, ALU.mult),
                     ts_(Lr1[:], Lr[:], s5_i["sgn"][:, 1:2], None, ALU.mult), ts_(Ls1[:], Ls[:], -1.0, None, ALU.mult))
                step(ts_(Ls[:], Ls[:], s5_i["sgn"][:, 0:1], None, ALU.mult))
                fr, fs = over(p_["fr"], CH), over(p_["fs"], CH)
                ta, tb = t_a[:, :, 0:CH], t_b[:, :, 0:CH]
                tc, td = t_a[:, :, CH:2 * CH], t_b[:, :, CH:2 * CH]
                step(tt(ta, s5_i["Bo"], fr, ALU.mult), tt(tb, s5_i["Bx"], fs, ALU.mult),
                     tt(tc, s5_i["Bx"], fr, ALU.mult), tt(td, s5_i["Bo"], fs, ALU.mult),
                     *[cp(o[:, j, :], i_[:, L - 1 - j, :]) for o, i_ in ((LrR, Lr), (LsR, Ls)) for j in range(L)])
                step(tt(bbo[:], ta, tb, ALU.add), tt(bbx[:], tc, td, ALU.subtract))
                step(tt(four(t_a, L), taps(bbo[:], L), power(LrR, L), ALU.mult), tt(four(t_b, L), taps(bbx[:], L), power(LsR, L), ALU.mult))
                tt(Gb[:], t_a[:, :, 0:L * CH], t_b[:, :, 0:L * CH], ALU.add).then_inc(sem("gb_done"), 1)
                dve.wait_ge(sem("gb_done"), c("blk", 1))

            def h_cos():
                wait(dve, "s5_stored", c("blk") * (16 * (L + 1)))
                step(tt(four(t_a, TAPS), taps(s5_i["Co"], TAPS), power(Lr1, TAPS), ALU.mult))
                dve.wait_ge(sem("gt_done"), c("blk") * 4 + 4)
                free(tt(four(t_b, TAPS), taps(s5_i["Cx"], TAPS), power(Ls1, TAPS), ALU.mult), 4)
                c.add("bank", 4)
                freed()
                tt(tab["Hc"], t_a[:], t_b[:], ALU.add).then_inc(sem("hc_done"), 1)
                dve.wait_ge(sem("hc_done"), c("blk", 1))

            def k_and_hs():
                step(V.memset(KTp[:, :, 0:ZPAD], 0.0))
                for q in range(4):
                    dve.wait_ge(sem("kt_full"), c("blk") * 4 + (q + 1))
                    src = ps_of(c)[0:CH, 0:2 * P].rearrange("p (g m) -> p g m", m=P)
                    g2 = slice(2 * q, 2 * q + 2)
                    step(cp(KTp[:, g2, ZPAD + CH:], src[:, :, CH:]))
                    free(tt(KTp[:, g2, ZPAD:ZPAD + CH], src[:, :, 0:CH], dsk[:, g2, :], ALU.add))
                    c.add("bank")
                freed()
                tt(four(t_a, TAPS), taps(s5_i["Co"], TAPS), power(Ls, TAPS), ALU.mult).then_inc(sem("ktp_done"), 1)
                dve.wait_ge(sem("ktp_done"), c("blk", 1))
                step(tt(four(t_b, TAPS), taps(s5_i["Cx"], TAPS), power(Lr, TAPS), ALU.mult))
                step(tt(tab["Hs"], t_a[:], t_b[:], ALU.subtract))

            def chunk_angles():
                Er, Ei, q_r, q_i = tab["Er"], tab["Ei"], p_["er"], p_["ei"]
                step(V.memset(Er[:, :, 0:1], 1.0), V.memset(Ei[:, :, 0:1], 0.0))
                n = 1
                while n < NCH:
                    a, b_, d, e = (z[:, :, k:k + n] for z, k in ((t_a, 0), (t_b, 0), (t_a, n), (t_b, n)))
                    turned = [tt(a, Er[:, :, 0:n], over(q_r, n), ALU.mult), tt(b_, Ei[:, :, 0:n], over(q_i, n), ALU.mult),
                              tt(d, Er[:, :, 0:n], over(q_i, n), ALU.mult), tt(e, Ei[:, :, 0:n], over(q_r, n), ALU.mult)]
                    if 2 * n < NCH:
                        step(*turned, m_("t1", "er", "er"), m_("t2", "ei", "ei"), m_("t3", "er", "ei"))
                        step(tt(Er[:, :, n:2 * n], a, b_, ALU.subtract), tt(Ei[:, :, n:2 * n], d, e, ALU.add),
                             m_("er", "t1", "t2", ALU.subtract), ts_(q_i, p_["t3"], 2.0, None, ALU.mult))
                    else:
                        step(*turned)
                        step(tt(Er[:, :, n:2 * n], a, b_, ALU.subtract))
                        tt(Ei[:, :, n:2 * n], d, e, ALU.add).then_inc(sem("tab_done"), 1)
                        dve.wait_ge(sem("tab_done"), c("blk", 1))
                    n *= 2

            S5_STAGES = {0: angles, 1: powers, 2: factors, 4: h_cos, 5: k_and_hs, 6: chunk_angles}

            def s5_stage(s):
                if s in S5_STAGES:
                    S5_STAGES[s]()

            dve.wait_ge(sem("cond_done"), 2)
            ada(16, 0)
            dve.wait_ge(sem("consts_in"), 96)
            dve.wait_ge(sem("ones_set"), 2)
            ada_put()
            split()
            c.add("bank")
            norm(0, 0)
            for kind, p in A_WALK:
                if kind == "p":
                    banks = {}
                    natural(lambda t, b: banks.setdefault(t, b), 3)
                    dve.wait_ge(sem("a_sq_done"), TT * (p + 1))
                    V.tensor_reduce(stat[:], a_sq[:].rearrange("p t (h d) -> p (t h) d", d=HD), AX.X, ALU.add).then_inc(sem("a_red"), 1)
                    dve.wait_ge(sem("a_std"), p + 1)
                    step(V.reciprocal(stat[:], rstd[:]))
                    for t in range(TT):
                        free(tt(a_qn[:, p % 2, t, :].rearrange("p (h d) -> p h d", d=HD), banks[t][:].rearrange("p (h d) -> p h d", d=HD),
                                stat[:, 8 * t:8 * t + 8].unsqueeze(2).to_broadcast([P, 8, HD]), ALU.mult))
                    freed()
                    V.engine_nop().then_inc(sem("qn_done"), 1)
                elif kind == "v":
                    natural(lambda t, b: free(cp(a_v[:, t, p * 512:(p + 1) * 512], b[:])), 4)
                else:
                    for i in range(4):
                        dve.wait_ge(sem("xp_full"), 4 * p + i + 1)
                        o = (a_qT if p < 2 else a_kT)[:, 4 * (p % 2) + i, :]
                        free(ts_(o, ps_of(c)[:], aqk_g[:, p // 2:p // 2 + 1], HD ** -0.5 if p < 2 else 1.0, ALU.mult, ALU.mult))
                        c.add("bank")

            ada_put()

            def mask_a(u):
                h, it = u
                if it == 0:
                    dve.wait_ge(sem(f"bias_in{h % 3}"), 16 * (h // 3 + 1))
                return a_bias[:, h % 3, P * (TT - 1 - it):T]

            def combine_a(u, unit):
                h, it = unit
                dve.wait_ge(sem("o_full"), u + 1)
                ts_(a_o[:, it, h * HD:(h + 1) * HD], ps[5 + u % 2][:, 0:HD], row_inv[:, u % 8:u % 8 + 1], None, ALU.mult).then_inc(sem("o_done"), 1)
                if it == 1:
                    ada(1, 0)
                if it == TT - 1 and h % 8 == 7:
                    ada_put()

            attention(UNITS_A, lambda u: P * (u[1] + 1), mask_a, combine_a, "", SIDE_A)
            c.add("slab", 2)
            c.add("full", 2 * (TT - 1))
            for i in range(KT):
                dve.wait_ge(sem("xo_hi"), i + 1)
                tt(h_lo[:, i, :], ps_of(c)[:], h_hi[:, i, :].bitcast(F32), ALU.subtract).then_inc(sem("xo_lo"), 1)
                dve.wait_ge(sem("xo_lo"), i + 1)
                free(V.engine_nop())
                c.add("bank")
            residual(16, norm_next=True)
            norm(1, 24)
            ffn(40, ADA_TILES // QUARTERS, 0)

            norm(2, 48)
            dve.wait_ge(sem("bws_in"), 32)
            V.memset(b_ws[HD:P, :, 0:HD], 0.0).then_inc(sem("bws_masked"), 1)
            for p in range(6):
                def sq(t, b):
                    dve.wait_ge(sem("bv_done"), TT * p + t + 1)
                    v = b_v[:, t, p * 512:(p + 1) * 512]
                    free(V.tensor_tensor_reduce(out=b[:], in0=v, in1=v, scale=1.0, scalar=0.0, op0=ALU.mult, op1=ALU.add,
                                                accum_out=vss[:, t, p:p + 1]))
                natural(sq)
            freed()
            V.tensor_reduce(stat[:, 0:TT], vss[:], AX.X, ALU.add).then_inc(sem("v_red"), 1)
            dve.wait_ge(sem("v_std"), 1)
            step(V.reciprocal(rstd[:, 0:TT], stat[:, 0:TT]))
            for t in range(TT):
                ts_(b_v[:, t, :], b_v[:, t, :], rstd[:, t:t + 1], None, ALU.mult).then_inc(sem("bv_scaled"), 1)
            for ch in range(CHUNKS):
                for s in range(4):
                    split()
                    for m in range(2):
                        gm = KT * ch + 2 * s + m
                        full(m)
                        dve.wait_ge(sem("mix_full"), gm + 1)
                        b = ps_of(c)
                        c.add("bank")
                        if gm:
                            dve.wait_ge(sem("g_lo_done"), gm)
                        stt(b_vm[:].rearrange("p (n i) -> p n i", i=P), b[:].rearrange("p (n i) -> p n i", i=P), bv_g[:, gm:gm + 1],
                            b_bs[:, gm // 3, :].unsqueeze(1).to_broadcast([P, TT, P]), ALU.mult, ALU.add).then_inc(sem("bvm_done"), 1)
                        dve.wait_ge(sem("bvm_done"), gm + 1)
                        dve.wait_ge(sem("bu_done"), gm + 1)
                        free(tt(b_vm[:], b_vm[:], b_u[:], ALU.mult), 2)
                        dve.wait_ge(sem("g_hi_done"), gm + 1)
                        tt(g_lo[:, 2 * s + m, :], b_vm[:], g_hi[:, 2 * s + m, :].bitcast(F32), ALU.subtract).then_inc(sem("g_lo_done"), 1)
                    c.add("slab")
                residual(64, norm_next=ch == CHUNKS - 1)
            norm(3, 72)
            ffn(88, ADA2_TILES // QUARTERS, 1, s5_stage)

            norm(4, 96)
            N_SMALL = 12
            banks = {}
            natural(lambda t, b: banks.setdefault(t, b))
            dve.wait_ge(sem("h_sq_done"), TT)
            V.tensor_reduce(stat[:], h_sq[:].rearrange("p t (h d) -> p (t h) d", d=HD), AX.X, ALU.add).then_inc(sem("h_red"), 1)
            dve.wait_ge(sem("h_std"), 1)
            step(V.reciprocal(stat[:], rstd[:]))
            for t in range(TT):
                free(tt(h_qn[:, t, :].rearrange("p (h d) -> p h d", d=HD), banks[t][:].rearrange("p (h d) -> p h d", d=HD),
                        stat[:, 8 * t:8 * t + 8].unsqueeze(2).to_broadcast([P, 8, HD]), ALU.mult))
            freed()
            split()
            c.add("slab")
            dve.wait_ge(sem("h_in"), 16 * N_SMALL)
            step(*[tt(h_qn[:, t, :].rearrange("p (h d) -> p h d", d=HD), h_qn[:, t, :].rearrange("p (h d) -> p h d", d=HD),
                      qg_b[:].unsqueeze(1).to_broadcast([P, 8, HD]), ALU.mult) for t in range(TT)])

            def rope(src, dst, heads, signal):
                x = src[:].rearrange("p t (h d) -> p t h d", d=HD)
                o = dst[:].rearrange("p t (h d) -> p t h d", d=HD)
                x1, x2, o1, o2 = x[:, :, :, 0:32], x[:, :, :, 32:HD], o[:, :, :, 0:32], o[:, :, :, 32:HD]
                co = cos[:].unsqueeze(2).to_broadcast([P, TT, heads, 32])
                si = sin[:].unsqueeze(2).to_broadcast([P, TT, heads, 32])
                a, b = h_t1[:, :, 0:heads, :], h_t2[:, :, 0:heads, :]
                step(tt(a, x1, co, ALU.mult), tt(b, x2, si, ALU.mult))
                step(tt(o1, a, b, ALU.subtract))
                step(tt(a, x2, co, ALU.mult), tt(b, x1, si, ALU.mult))
                tt(o2, a, b, ALU.add).then_inc(sem(signal), 1)
                dve.wait_ge(sem(signal), 1)

            rope(h_qn, h_qr, 8, "hq_done")
            step(cp(wg_hi[:], wg[:]))
            tt(wg_lo[:], wg[:], wg_hi[:].bitcast(F32), ALU.subtract).then_inc(sem("wg_split"), 1)
            banks = {}
            natural_end(lambda t, b: banks.setdefault(t, b))
            dve.wait_ge(sem("h_sq_done"), 2 * TT)
            V.tensor_reduce(stat[:, 0:16], h_t1[:].rearrange("p t a b -> p (t a b)").rearrange("p (n d) -> p n d", d=HD), AX.X, ALU.add)\
             .then_inc(sem("h_red"), 1)
            dve.wait_ge(sem("h_std"), 2)
            step(V.reciprocal(stat[:, 0:16], rstd[:, 0:16]))
            for t in range(TT):
                step(tt(h_kn[:, t, :].rearrange("p (h d) -> p h d", d=HD), banks[t][:, 0:256].rearrange("p (h d) -> p h d", d=HD),
                        stat[:, 4 * t:4 * t + 4].unsqueeze(2).to_broadcast([P, 4, HD]), ALU.mult))
                free(cp(hv[:, t, :], banks[t][:, 256:512]))
            step(*[tt(h_kn[:, t, :].rearrange("p (h d) -> p h d", d=HD), h_kn[:, t, :].rearrange("p (h d) -> p h d", d=HD),
                      kg_b[:], ALU.mult) for t in range(TT)])
            rope(h_kn, h_kr, 4, "hk_done")
            dve.wait_ge(sem("gates_full"), 1)
            b = ps_of(c)
            c.add("bank")
            step(cp(h_gts[:], b[:, 0:TT * 24].rearrange("p (t n) -> p t n", n=24)))
            V.engine_nop().then_inc(sem("gates_copied"), 1)
            free(V.engine_nop())

            def half(tile, k):
                split()
                for m in range(2):
                    b = full(m)
                    free(cp(tile[:, 2 * k + m, :], b[:]))
                c.add("slab")

            def blocks(kind):
                ins = []
                src = crT[:, kind, :].rearrange("p (n l) -> p l n", l=16)
                for lp in range(2):
                    for g in range(H_GROUPS):
                        r = slice(HD * g, HD * g + HD)
                        for half_ in range(2):
                            ins.append(tt(bl[HD * lp:HD * lp + HD, 8 * half_:8 * half_ + 8, CMP_PAD * g:CMP_PAD * g + CMP_N],
                                          src[r, :, half_:half_ + CMP_N].rearrange("p (a b) n -> p a b n", b=2)[:, :, lp, :],
                                          posT[r, kind, 16 * half_:16 * half_ + 16].rearrange("p (a b) -> p a b", b=2)[:, :, lp].unsqueeze(2)
                                          .to_broadcast([HD, 8, CMP_N]), ALU.add))
                step(*ins)

            def split_blocks(kind):
                step(cp(bl_hi[:], bl[:]))
                tt(bl_lo[:], bl[:], bl_hi[:].bitcast(F32), ALU.subtract).then_inc(sem("bl_done"), 1)
                dve.wait_ge(sem("bl_done"), kind + 1)

            half(crT, 0)
            freed()
            step(V.memset(bl[:], 0.0))
            blocks(0)
            split_blocks(0)
            half(za, 0)
            for i in range(8):
                dve.wait_ge(sem("hx_full"), i + 1)
                free(ts_((hq if i < 4 else hqr)[:, i % 4, :], ps_of(c)[:], HD ** -0.5, None, ALU.mult))
                c.add("bank")
            for i in range(2):
                dve.wait_ge(sem("hx_full"), 9 + i)
                free(cp(hk[:, i, :], ps_of(c)[:]))
                c.add("bank")
            for kind in range(2):
                split()
                c.add("slab")
                c.add("full", 1)
                if kind == 0:
                    blocks(1)
                split()
                for m in range(2):
                    b = full(m)
                    free(cp(hdn[:, kind, m, :], b[:, 0:2 * CMP_PAD]))
                freed()
                V.engine_nop().then_inc(sem("hdn_copied"), 1)
                c.add("slab")
                if kind == 0:
                    split_blocks(1)
                    half(za, 1)
                else:
                    half(zs, 0)
            dve.wait_ge(sem("kc_full"), 1)
            b = ps_of(c)
            c.add("bank")
            step(cp(kcn[:], b[0:CMP_PAD, 0:2 * HD].rearrange("n (g d) -> n g d", d=HD)),
                 cp(vc[:], b[0:CMP_PAD, 2 * HD:4 * HD].rearrange("n (g d) -> n g d", d=HD)))
            free(tt(kcsq[:], kcn[:], kcn[:], ALU.mult))
            freed()
            V.tensor_reduce(kst[:, 0:2], kcsq[:], AX.X, ALU.add).then_inc(sem("kc_red"), 1)
            dve.wait_ge(sem("kc_std"), 1)
            step(V.reciprocal(kst[:, 2:4], kst[:, 0:2]))
            step(tt(kcn[:], kcn[:], kst[:, 2:4].unsqueeze(2).to_broadcast([CMP_PAD, 2, HD]), ALU.mult))
            tt(kcn[:], kcn[:], kcg_b[:].unsqueeze(1).to_broadcast([CMP_PAD, 2, HD]), ALU.mult).then_inc(sem("kcn_done"), 1)
            half(zs, 1)
            freed()
            V.engine_nop().then_inc(sem("z_copied"), 1)
            dve.wait_ge(sem("kct_full"), 1)
            free(cp(kcT[:], ps_of(c)[:, 0:CMP_PAD]))
            c.add("bank")
            dve.wait_ge(sem("gts_done"), 1)

            def mask_h(u):
                i, g, it, br = u
                return h_cmask[:, it, :] if br == 0 else h_mask[:, P * (TT - 1 - it):T]

            def combine_h(u, unit):
                i, g, it, br = unit
                hp = 2 * i + g
                w = wbr[:, u % 4:u % 4 + 1]
                step(stt(w, row_inv[:, u % 8:u % 8 + 1], h_flag[:, it:it + 1] if br == 0 else 1.0,
                         h_gts[:, it, N_BR * hp + br:N_BR * hp + br + 1], ALU.mult, ALU.mult))
                dve.wait_ge(sem("ho_full"), u + 1)
                o, p_ = h_o[:, it, hp * HD:(hp + 1) * HD], ps[5 + u % 2][:, 0:HD]
                if br == 0:
                    ins = ts_(o, p_, w, None, ALU.mult)
                else:
                    dve.wait_ge(sem("ho_done"), u)
                    ins = stt(o, p_, w, o, ALU.mult, ALU.add)
                ins.then_inc(sem("ho_done"), 1)

            attention(UNITS_H, lambda u: CMP_PAD if u[3] == 0 else P * (u[2] + 1), mask_h, combine_h, "h", SIDE_H)
            c.add("slab", 2)
            c.add("full", 2)
            dve.wait_ge(sem("z_done"), 2)
            dve.wait_ge(sem("ho_done"), NUH)
            for i in range(5):
                if i < 4:
                    dve.wait_ge(sem("hxo_full"), i + 1)
                    if i >= 2:
                        dve.wait_ge(sem("hx_done"), i - 1)
                    tt(h_gate[:, i % 2, :], ps_of(c)[:], za[:, i, :], ALU.mult).then_inc(sem("hxo_gated"), 1)
                    c.add("bank")
                if i:
                    dve.wait_ge(sem("hxo_hi"), i)
                    free(V.engine_nop())
                    tt(o_lo[:, i - 1, :], h_gate[:, (i - 1) % 2, :], o_hi[:, i - 1, :].bitcast(F32), ALU.subtract).then_inc(sem("hx_done"), 1)

            def y_free(blk):
                dve.wait_ge(sem("yn_gelu"), 2 * blk + 2)
                free(V.engine_nop(), 2)
                c.add("bank", 2)

            dve.wait_ge(sem("hx_done"), 4)
            step(V.memset(v_a[:, :, 0:1], 0.0), V.memset(v_b[:, :, 0:1], 0.0))
            for blk in range(NBLK):
                t = tables(s5_t[blk % 2])
                dve.wait_ge(sem(f"tab_in{blk % 2}"), 32 * (blk // 2 + 1))
                if blk:
                    y_free(blk - 1)
                va, vb = v_c[:], wst[:]
                dve.wait_ge(sem("x_full"), 2 * blk + 1)
                step(tt(va, ps_of(c)[:].rearrange("p (g n) -> p g n", n=NCH), t["Er"], ALU.mult))
                c.add("bank")
                dve.wait_ge(sem("x_full"), 2 * blk + 2)
                step(tt(vb, ps_of(c)[:].rearrange("p (g n) -> p g n", n=NCH), t["Ei"], ALU.mult))
                c.add("bank")
                free(tt(va, va, vb, ALU.add), 2)
                freed()
                step(*[V.tensor_tensor_scan(wst[:, g, :], t["r8"][:, g:g + 1].to_broadcast([P, NCH]), v_c[:, g, :],
                                            0.0, ALU.mult, ALU.add) for g in range(GB)])
                if blk:
                    dve.wait_ge(sem("y_mm"), 2 * blk)
                step(tt(v_a[:, :, 1:], wst[:, :, 0:NCH - 1], t["Er"][:, :, 0:NCH - 1], ALU.mult))
                tt(v_b[:, :, 1:], wst[:, :, 0:NCH - 1], t["Ei"][:, :, 0:NCH - 1], ALU.mult).then_inc(sem("st_done"), 1)
            y_free(NBLK - 1)
            for ct in range(4):
                dve.wait_ge(sem("yt_full"), ct + 1)
                cp(yT[:, ct, :].rearrange("p (n i) -> p i n", i=L), ps_of(c)[:].rearrange("p (i n) -> p i n", n=NCH)).then_inc(sem("yt_done"), 1)
                dve.wait_ge(sem("yt_done"), ct + 1)
                free(V.engine_nop())
                c.add("bank")
                dve.wait_ge(sem("y_hi_done"), ct + 1)
                tt(y_lo[:, ct, :], yT[:, ct, :], y_hi[:, ct, :].bitcast(F32), ALU.subtract).then_inc(sem("y_lo_done"), 1)
            split()
            for m in range(4):
                full(m, 4)
                dve.wait_ge(sem("sg_done"), m + 1)
                if m >= 2:
                    dve.wait_ge(sem("mix_lo"), m - 1)
                free(tt(mx_t[:, m % 2, :], sg_t[:, m % 2, :], yT[:, m, :], ALU.mult))
                freed()
                tt(mx_t[:, m % 2, :], mx_t[:, m % 2, :], zs[:, m, :], ALU.mult).then_inc(sem("mx_done"), 1)
                dve.wait_ge(sem("mix_hi"), m + 1)
                tt(h_lo[:, 4 + m, :], mx_t[:, m % 2, :], h_hi[:, 4 + m, :].bitcast(F32), ALU.subtract).then_inc(sem("mix_lo"), 1)
            c.add("slab")
            for s in range(4):
                split()
                for m in range(2):
                    o = 2 * s + m
                    b = full(m)
                    stt(xT[:, o, :], b[:], mod[:, 112 + o:113 + o], xT[:, o, :], ALU.mult, ALU.add).then_inc(sem("x_final"), 1)
                    dve.wait_ge(sem("x_final"), o + 1)
                    free(V.engine_nop())
                c.add("slab")


def kernel(**inputs):
    import numpy as np
    import concourse.bacc as _bacc
    from concourse.bass_utils import run_bass_kernel_spmd as _run

    a = {k: np.asarray(v) for k, v in inputs.items()}
    f = lambda x: np.ascontiguousarray(x, dtype=np.float32)

    def natural(w):
        K, N = w.shape
        return w.reshape(K // 512, 4, 128, N // 512, 512).transpose(3, 0, 2, 1, 4).reshape(-1, 128, SLAB)

    def transposed(w):
        K, N = w.shape
        return w.reshape(8, 128, N // 256, 256).transpose(2, 1, 0, 3).reshape(-1, 128, SLAB)

    def down(w, parts):
        return [transposed(x) for x in np.split(w, parts, axis=0)]

    def ffn(l):
        up = np.split(transposed(a["ffn_w1"][l]), QUARTERS)
        return [x for pair in zip(up, down(a["ffn_w2"][l], QUARTERS)) for x in pair]

    b_in = a["b_w_in"][0]
    u_slabs = np.split(transposed(b_in[:, :SG_HALF]), CHUNKS)
    b_slabs = [x for pair in zip(u_slabs, down(a["b_w_out"][0], CHUNKS)) for x in pair]
    order = [g * 4 + i for i in range(4) for g in range(2)]
    w = a["w_in_2"][0]
    cols = np.cumsum([0, 512] + [128] * 6 + [512, 24, 512, 512])
    q, kcr, vcr, ksl, vsl, kwn, vwn, z_a, g_br, u, z_s = (w[:, cols[i]:cols[i + 1]] for i in range(11))
    heads = lambda m, n: m.reshape(m.shape[0], 8, n)[:, order].reshape(m.shape[0], 8 * n)
    w_out = a["w_out_2"][0]
    w_out = np.concatenate([w_out[:512].reshape(8, 64, D)[order].reshape(512, D), w_out[512:]])
    glu = a["glu_w_2"][0].reshape(4, 128, 512).transpose(1, 0, 2).reshape(1, 128, SLAB)
    a_in = a["a_w_in"][0]
    za = transposed(heads(z_a, 64))
    slabs = np.concatenate([natural(a_in[:, :2560]), transposed(a_in[:, 2560:]), transposed(a["a_w_out"][0])] + ffn(0)
                           + [natural(b_in[:, SG_HALF:])] + b_slabs + ffn(1)
                           + [natural(heads(q, 64)), natural(np.concatenate([ksl, kwn, vsl, vwn], 1)),
                              transposed(np.concatenate([kcr, vcr], 1)), za[:1]] + down(a["cmp_w1_k_2"][0], 2) + [za[1:]]
                           + down(a["cmp_w1_v_2"][0], 2) + [transposed(z_s), transposed(u), glu, transposed(w_out)])
    assert slabs.shape == (N_SLABS, 128, SLAB), slabs.shape

    col = lambda v: v.reshape(-1, 128).T
    ada = lambda m: m.T.reshape(-1, 128, D)
    A = {"slabs": slabs, "ada": np.concatenate([ada(a["ada_w"][0]), ada(a["ada_w"][1]), ada(a["w_ada_2"][0])]),
         "xT": a["x"][0].T.reshape(KT, 128, T).transpose(1, 0, 2), "ident": np.eye(128),
         "norm_g": np.stack([col(a["norm_mix"][0]), col(a["norm_ffn"][0]), col(a["norm_mix"][1]), col(a["norm_ffn"][1]),
                             col(a["norm_g_2"][0])], 1),
         "mod_b": np.concatenate([col(a["ada_b"][0]), col(a["ada_b"][1]), col(a["b_ada_2"][0])], 1),
         "aqk_g": np.stack([np.tile(a["a_q_gain"][0], 2), np.tile(a["a_k_gain"][0], 2)], 1),
         "bv_g": col(a["b_v_gain"][0]), "c": np.concatenate([a["c"], a["c_2"]])}
    p, y = np.arange(128)[:, None], np.arange(T)[None, :]
    bias = a["a_rel_bias"][0][:, np.clip(p - y + 384, -63, 256) + 63]
    bias[:, (p < 64) & (y >= 448)] = -BIG
    A["a_bias"] = bias
    A["b_ws"] = a["b_w_s"][0].transpose(2, 0, 1)
    A["b_bs"] = a["b_b_s"]
    t = np.arange(T)
    tiles = lambda m: m.reshape(TT, 128, -1).transpose(1, 0, 2)
    A["h_cmask"] = tiles(np.where(np.arange(CMP_PAD)[None, :] * 16 + 31 <= t[:, None], 0.0, -BIG))
    A["h_cmask"][:, :, CMP_N] = -BIG
    A["h_flag"] = tiles((t >= 31)[:, None])[:, :, 0]
    A["h_mask"] = np.where(y - 384 <= p, 0.0, -BIG)
    inv = 1.0 / (10000.0 ** (np.arange(0, HD, 2, dtype=np.float32) / HD))
    ang = (t[:, None].astype(np.float32) * inv[None, :].astype(np.float32)).astype(np.float32)
    A["cos"], A["sin"] = tiles(np.cos(ang)), tiles(np.sin(ang))
    rows = lambda v, n=128: np.broadcast_to(v, (n,) + v.shape)
    A["qg_b"] = rows(a["q_norm_g_2"][0])
    ks, kw = a["k_slc_norm_g_2"][0], a["k_win_norm_g_2"][0]
    A["kg_b"] = rows(np.stack([ks, ks, kw, kw]))
    A["kcg_b"] = rows(a["k_cmp_norm_g_2"][0], CMP_PAD)
    A["wg"] = heads(g_br, 3).reshape(KT, 128, 24).transpose(1, 0, 2)
    A["posT"] = np.tile(np.stack([a["cmp_pos_k_2"][0].T, a["cmp_pos_v_2"][0].T], 1), (2, 1, 1))
    A["w2c"] = np.stack([a[f"cmp_w2_{x}_2"][0].reshape(2, 128, 64).transpose(1, 0, 2) for x in "kv"], 1)
    A["glu_b"] = col(a["glu_b_2"][0])
    half = np.repeat([-1.0, 1.0], 64)
    per_block = lambda m: m.reshape(128, NBLK, -1).transpose(1, 0, 2)
    b_re, b_im = (a[f"ssm_b_{x}_2"][0].transpose(1, 0, 2) for x in ("re", "im"))
    c_re, c_im = (a[f"ssm_c_{x}_2"][0].transpose(2, 0, 1) for x in ("re", "im"))
    A["s5_in"] = np.concatenate(
        [per_block(np.tile(a["ssm_a_re_2"][0].T, (2, 1))), per_block(np.tile(a["ssm_a_im_2"][0].T, (2, 1))),
         per_block(rows(a["ssm_log_dt_2"][0]).copy())]
        + [per_block(np.concatenate(m)) for m in ([b_re, b_im], [b_im, b_re], [c_re, c_im], [c_im, c_re])]
        + [np.broadcast_to(np.stack([half, -half], 1), (NBLK, 128, 2))], 2)
    dsk = np.zeros((CH, G_ALL, CH), np.float32)
    dsk[np.arange(CH), :, np.arange(CH)] = a["ssm_d_2"][0].reshape(G_ALL, CH).T
    A["dsk"] = dsk.reshape(CH, NBLK, GB, CH).transpose(1, 0, 2, 3)

    nc = _bacc.Bacc("TRN2", target_bir_lowering=False, num_devices=1)
    arrays, I = {}, {}
    for name, v in A.items():
        v = f(v)
        arrays[f"in_{name}"] = v
        I[name] = nc.dram_tensor(f"in_{name}", v.shape, F32, kind="ExternalInput").ap()
    out = nc.dram_tensor("out_x", (128, KT, T), F32, kind="ExternalOutput").ap()
    tab_d = nc.dram_tensor("s5_tables", (NBLK, 128, TAB_W), F32, kind="Internal").ap()
    tz_d = nc.dram_tensor("s5_toeplitz", (NBLK, 128, GB, L * CH), F32, kind="Internal").ap()
    program(nc, I, out, tab_d, tz_d)
    r = _run(nc, [arrays], core_ids=[0])
    y = np.asarray(r.results[0]["out_x"])
    return np.ascontiguousarray(y.transpose(1, 0, 2).reshape(D, T).T).reshape(1, T, D)
```
